# Optimizing a Trainium2 kernel written in Bass

```python
import math
import jax, jax.numpy as jnp
from jax import lax
import numpy as np

D_MODEL = 2048
BATCH = 1
SEQ = 512
DEPTH = 1
DEC_BATCH = 8
DEC_SEQ = 1
PAST_LEN = 4096
PAGE_SIZE = 128

ATT_HD = 64
ATT_HEADS_PER_GROUP = 8
DIL_PAIRS = ((128, 1), (512, 4), (2048, 16))
N_DIL = len(DIL_PAIRS)
ATT_WIDTH = N_DIL * ATT_HEADS_PER_GROUP * ATT_HD
QBLK = 128
CHUNK = 128
GM_HEADS = 4
GM_HD = 128
GM_WIDTH = GM_HEADS * GM_HD
MIX_WIDTH = ATT_WIDTH + GM_WIDTH
IN_WIDTH = 3 * ATT_WIDTH + 2 * GM_WIDTH
N_KEYS = 128
N_EXPERTS = N_KEYS * N_KEYS
PEER_HEADS = 8
PEER_DKEY = 256
PEER_TOPK = 16
PEER_TOK_BLOCK = 128
EPS = 1e-6

kernel_name = "hybrid_dilattn_gmlp_peer_decoder_step"

def rms_norm(x, g):
    xf = x.astype(jnp.float32)
    y = xf * lax.rsqrt(jnp.mean(xf * xf, axis=-1, keepdims=True) + EPS)
    return (y * g.astype(jnp.float32)).astype(x.dtype)

def layer_norm(x, g, b):
    xf = x.astype(jnp.float32)
    mu = jnp.mean(xf, axis=-1, keepdims=True)
    var = jnp.mean(jnp.square(xf - mu), axis=-1, keepdims=True)
    return (xf - mu) * lax.rsqrt(var + EPS) * g.astype(jnp.float32) + b.astype(jnp.float32)

def ada_mod(c, w_ada, b_ada):
    m = (jax.nn.silu(c) @ w_ada + b_ada)[:, None, :]
    return jnp.split(m, 6, axis=-1)

def dilated_attn_prompt(q, k, v, window, dil):
    B, S, H, hd = q.shape
    J = window // dil
    L = S // dil
    def fold(t):
        return t.reshape(B, L, dil, H, hd).transpose(0, 2, 1, 3, 4).reshape(B * dil, L, H, hd)
    nblk = -(-L // QBLK)
    Lp = nblk * QBLK
    pad = Lp - L
    qf = jnp.pad(fold(q), ((0, 0), (0, pad), (0, 0), (0, 0))).astype(jnp.float32)
    kf = jnp.pad(fold(k), ((0, 0), (QBLK, pad), (0, 0), (0, 0))).astype(jnp.float32)
    vf = jnp.pad(fold(v), ((0, 0), (QBLK, pad), (0, 0), (0, 0))).astype(jnp.float32)
    Z = B * dil
    qb = qf.reshape(Z, nblk, QBLK, H, hd)
    def band(t):
        prev = t[:, :Lp].reshape(Z, nblk, QBLK, H, hd)
        cur = t[:, QBLK:].reshape(Z, nblk, QBLK, H, hd)
        return jnp.concatenate([prev, cur], axis=2)
    kb, vb = band(kf), band(vf)
    s = jnp.einsum('znqhd,znkhd->znhqk', qb, kb) * (hd ** -0.5)
    qi = jnp.arange(QBLK)[:, None]
    kk = jnp.arange(2 * QBLK)[None, :]
    dist = qi + QBLK - kk
    kpos = jnp.arange(nblk)[:, None, None] * QBLK - QBLK + kk[None]
    mask = (dist >= 0)[None] & (dist <= J)[None] & (kpos >= 0)
    s = jnp.where(mask[None, :, None], s, -jnp.inf)
    m = jnp.max(s, axis=-1, keepdims=True)
    p = jnp.exp(s - m)
    den = jnp.sum(p, axis=-1, keepdims=True)
    o = jnp.einsum('znhqk,znkhd->znqhd', p / den, vb)
    lse = (m + jnp.log(den))[..., 0].transpose(0, 1, 3, 2)
    o = o.reshape(Z, Lp, H, hd)[:, :L].reshape(B, dil, L, H, hd).transpose(0, 2, 1, 3, 4).reshape(B, S, H, hd)
    lse = lse.reshape(Z, Lp, H)[:, :L].reshape(B, dil, L, H).transpose(0, 2, 1, 3).reshape(B, S, H)
    return o, lse

def dilated_attn_sample(q, k, v, buf, window, dil):
    T = q.shape[1]
    hd = q.shape[-1]
    nbuf = buf.shape[1]
    J = window // dil
    kall = jnp.concatenate([buf[:, :, 0].astype(jnp.float32), k.astype(jnp.float32)], axis=1)
    vall = jnp.concatenate([buf[:, :, 1].astype(jnp.float32), v.astype(jnp.float32)], axis=1)
    idx = nbuf + jnp.arange(T)[:, None] - dil * jnp.arange(J + 1)[None, :]
    valid = idx >= 0
    idxc = jnp.maximum(idx, 0)
    kg = kall[:, idxc]
    vg = vall[:, idxc]
    s = jnp.einsum('bthd,btjhd->bthj', q.astype(jnp.float32), kg) * (hd ** -0.5)
    s = jnp.where(valid[None, :, None, :], s, -jnp.inf)
    m = jnp.max(s, axis=-1, keepdims=True)
    p = jnp.exp(s - m)
    den = jnp.sum(p, axis=-1, keepdims=True)
    o = jnp.einsum('bthj,btjhd->bthd', p / den, vg)
    lse = (m + jnp.log(den))[..., 0]
    return o, lse

def gmlp_spatial(v, w_s, b_s, prompt):
    tril = jnp.tril(jnp.ones((CHUNK, CHUNK), dtype=jnp.float32))
    w = w_s.astype(jnp.float32) * tril
    B, S, Hg, C = v.shape
    if prompt:
        vc = v.reshape(B, S // CHUNK, CHUNK, Hg, C)
        z = jnp.einsum('hqp,bnphc->bnqhc', w, vc) + b_s.astype(jnp.float32).T[:, :, None]
        return z.reshape(B, S, Hg, C)
    z = jnp.einsum('hqp,bphc->bqhc', w[:, :S, :S], v) + b_s.astype(jnp.float32)[:, :S].T[:, :, None]
    return z

def token_mixers(h, w_in, gm_ln_g, gm_ln_b, w_s, b_s, bufs):
    B, S, _ = h.shape
    proj = h @ w_in
    q, k, v, gu, gv = jnp.split(proj, [ATT_WIDTH, 2 * ATT_WIDTH, 3 * ATT_WIDTH, 3 * ATT_WIDTH + GM_WIDTH], axis=-1)
    shp = (B, S, N_DIL, ATT_HEADS_PER_GROUP, ATT_HD)
    q, k, v = q.reshape(shp), k.reshape(shp), v.reshape(shp)
    outs, lses, kv_rows = [], [], []
    for g, (win, dil) in enumerate(DIL_PAIRS):
        qg, kg, vg = q[:, :, g], k[:, :, g], v[:, :, g]
        if bufs is None:
            o, lse = dilated_attn_prompt(qg, kg, vg, win, dil)
            keep = min(win, S)
            kv_rows.append(jnp.stack([kg[:, S - keep:], vg[:, S - keep:]], axis=2))
        else:
            o, lse = dilated_attn_sample(qg, kg, vg, bufs[g], win, dil)
            kv_rows.append(jnp.stack([kg, vg], axis=2))
        outs.append(o)
        lses.append(lse)
    alpha = jax.nn.softmax(jnp.stack(lses, axis=0), axis=0)
    att = jnp.stack([alpha[g][..., None] * outs[g] for g in range(N_DIL)], axis=2)
    att = att.reshape(B, S, ATT_WIDTH).astype(h.dtype)
    gu = jax.nn.gelu(gu).reshape(B, S, GM_HEADS, GM_HD).astype(jnp.float32)
    gvn = layer_norm(jax.nn.gelu(gv).reshape(B, S, GM_HEADS, GM_HD), gm_ln_g, gm_ln_b)
    z = gmlp_spatial(gvn, w_s, b_s, bufs is None)
    gm = (gu * z).reshape(B, S, GM_WIDTH).astype(h.dtype)
    return jnp.concatenate([att, gm], axis=-1), kv_rows, gvn.astype(h.dtype)

def peer(h, w_q, sub_keys, expert_u, expert_v):
    B, S, D = h.shape
    n = B * S
    xt = h.reshape(n, D)
    qr = (xt @ w_q).reshape(n, PEER_HEADS, 2, PEER_DKEY // 2).astype(jnp.float32)
    sc = jnp.einsum('nhpc,pkc->nhpk', qr, sub_keys.astype(jnp.float32))
    s1, i1 = lax.top_k(sc[:, :, 0], PEER_TOPK)
    s2, i2 = lax.top_k(sc[:, :, 1], PEER_TOPK)
    cand = (s1[..., :, None] + s2[..., None, :]).reshape(n, PEER_HEADS, PEER_TOPK * PEER_TOPK)
    cidx = (i1[..., :, None] * N_KEYS + i2[..., None, :]).reshape(n, PEER_HEADS, PEER_TOPK * PEER_TOPK)
    top_s, pos = lax.top_k(cand, PEER_TOPK)
    eidx = jnp.take_along_axis(cidx, pos, axis=-1)
    gate = jax.nn.softmax(top_s, axis=-1)
    blk = min(PEER_TOK_BLOCK, n)
    nb = -(-n // blk)
    pad = nb * blk - n
    xp = jnp.pad(xt, ((0, pad), (0, 0))).reshape(nb, blk, D)
    ep = jnp.pad(eidx, ((0, pad), (0, 0), (0, 0))).reshape(nb, blk, PEER_HEADS, PEER_TOPK)
    gp = jnp.pad(gate, ((0, pad), (0, 0), (0, 0))).reshape(nb, blk, PEER_HEADS, PEER_TOPK)
    def one_block(args):
        xb, eb, gb = args
        ub = expert_u[eb].astype(jnp.float32)
        a = jax.nn.gelu(jnp.einsum('td,thkd->thk', xb.astype(jnp.float32), ub))
        vb = expert_v[eb].astype(jnp.float32)
        return jnp.einsum('thk,thkd->td', gb * a, vb)
    out = lax.map(one_block, (xp, ep, gp))
    return out.reshape(nb * blk, D)[:n].reshape(B, S, D).astype(h.dtype)

def decoder_layer(x, c, wl, bufs):
    (w_ada, b_ada, norm_g, w_in, gm_ln_g, gm_ln_b, w_s, b_s, w_out, w_q, sub_keys, expert_u, expert_v) = wl
    sh1, sc1, gt1, sh2, sc2, gt2 = ada_mod(c, w_ada, b_ada)
    h = rms_norm(x, norm_g[0]) * (1 + sc1) + sh1
    mix, kv_rows, gv = token_mixers(h, w_in, gm_ln_g, gm_ln_b, w_s, b_s, bufs)
    x = x + gt1 * rms_norm(mix @ w_out, norm_g[1])
    h = rms_norm(x, norm_g[2]) * (1 + sc2) + sh2
    x = x + gt2 * rms_norm(peer(h, w_q, sub_keys, expert_u, expert_v), norm_g[3])
    return x, kv_rows, gv

def setup_inputs(seed: int = 0) -> dict:
    key = jax.random.key(seed)
    ks = jax.random.split(key, 22)
    D = D_MODEL
    def nrm(k, shape, s):
        return jax.random.normal(k, shape, jnp.float32) * s
    nbuf = [min(w, PAST_LEN) for w, _ in DIL_PAIRS]
    return {
        "x_prompt": nrm(ks[0], (BATCH, SEQ, D), 1.0),
        "x_sample": nrm(ks[1], (DEC_BATCH, DEC_SEQ, D), 1.0),
        "c_prompt": nrm(ks[2], (BATCH, D), 1.0),
        "c_sample": nrm(ks[3], (DEC_BATCH, D), 1.0),
        "cache_kv_dil1": nrm(ks[4], (DEPTH, DEC_BATCH, nbuf[0], 2, ATT_HEADS_PER_GROUP, ATT_HD), 1.0),
        "cache_kv_dil4": nrm(ks[5], (DEPTH, DEC_BATCH, nbuf[1], 2, ATT_HEADS_PER_GROUP, ATT_HD), 1.0),
        "cache_kv_dil16": nrm(ks[6], (DEPTH, DEC_BATCH, nbuf[2], 2, ATT_HEADS_PER_GROUP, ATT_HD), 1.0),
        "w_ada": nrm(ks[7], (DEPTH, D, 6 * D), 0.5 * D ** -0.5),
        "b_ada": nrm(ks[8], (DEPTH, 6 * D), 0.02),
        "norm_g": 1.0 + nrm(ks[9], (DEPTH, 4, D), 0.05),
        "w_in": nrm(ks[10], (DEPTH, D, IN_WIDTH), D ** -0.5),
        "gm_ln_g": 1.0 + nrm(ks[11], (DEPTH, GM_HEADS, GM_HD), 0.05),
        "gm_ln_b": nrm(ks[12], (DEPTH, GM_HEADS, GM_HD), 0.02),
        "w_s": nrm(ks[13], (DEPTH, GM_HEADS, CHUNK, CHUNK), CHUNK ** -0.5),
        "b_s": 1.0 + nrm(ks[14], (DEPTH, GM_HEADS, CHUNK), 0.1),
        "w_out": nrm(ks[15], (DEPTH, MIX_WIDTH, D), MIX_WIDTH ** -0.5),
        "w_q": nrm(ks[16], (DEPTH, D, PEER_HEADS * PEER_DKEY), D ** -0.5),
        "sub_keys": nrm(ks[17], (DEPTH, 2, N_KEYS, PEER_DKEY // 2), (PEER_DKEY // 2) ** -0.5),
        "expert_u": nrm(ks[18], (DEPTH, N_EXPERTS, D), D ** -0.5),
        "expert_v": nrm(ks[19], (DEPTH, N_EXPERTS, D), 1.0),
    }

def reference(x_prompt, x_sample, c_prompt, c_sample, cache_kv_dil1, cache_kv_dil4, cache_kv_dil16,
              w_ada, b_ada, norm_g, w_in, gm_ln_g, gm_ln_b, w_s, b_s, w_out, w_q, sub_keys,
              expert_u, expert_v):
    yp, ys = x_prompt, x_sample
    kvp = [[] for _ in DIL_PAIRS]
    kvs = [[] for _ in DIL_PAIRS]
    gvs = []
    for l in range(DEPTH):
        wl = (w_ada[l], b_ada[l], norm_g[l], w_in[l], gm_ln_g[l], gm_ln_b[l], w_s[l], b_s[l],
              w_out[l], w_q[l], sub_keys[l], expert_u[l], expert_v[l])
        yp, rows_p, _ = decoder_layer(yp, c_prompt, wl, None)
        ys, rows_s, gv = decoder_layer(ys, c_sample, wl, (cache_kv_dil1[l], cache_kv_dil4[l], cache_kv_dil16[l]))
        for g in range(N_DIL):
            kvp[g].append(rows_p[g])
            kvs[g].append(rows_s[g])
        gvs.append(gv)
    new_kv_dil1_prompt = jnp.stack(kvp[0], axis=0)
    new_kv_dil4_prompt = jnp.stack(kvp[1], axis=0)
    new_kv_dil16_prompt = jnp.stack(kvp[2], axis=0)
    new_kv_dil1_sample = jnp.stack(kvs[0], axis=0)
    new_kv_dil4_sample = jnp.stack(kvs[1], axis=0)
    new_kv_dil16_sample = jnp.stack(kvs[2], axis=0)
    state_gmlp_v_sample = jnp.stack(gvs, axis=0)
    return (yp, ys, new_kv_dil1_prompt, new_kv_dil4_prompt, new_kv_dil16_prompt,
            new_kv_dil1_sample, new_kv_dil4_sample, new_kv_dil16_sample, state_gmlp_v_sample)


_drawn_inputs = setup_inputs


def setup_inputs(seed=0):
    import zlib

    import numpy as np

    out = dict(_drawn_inputs(seed))
    spreads = {}
    factors = {'gm_ln_b': 2.871}
    for name, (base, spread) in spreads.items():
        noise = np.random.default_rng([zlib.crc32(name.encode()), seed]).standard_normal(out[name].shape)
        drawn = base * np.exp(spread * noise) if base else spread * noise
        out[name] = __import__('jax').numpy.asarray(drawn.astype(out[name].dtype))
    for name, factor in factors.items():
        out[name] = (out[name] * factor).astype(out[name].dtype)
    return out
```

```python
from contextlib import ExitStack

import numpy as np

import concourse.bass as bass
from concourse import mybir

ALU = mybir.AluOpType
ACT = mybir.ActivationFunctionType
F32 = mybir.dt.float32
U32 = mybir.dt.uint32
AX_X = mybir.AxisListType.X
ds = bass.ds

P = 128
D = 2048
KD = D // P
SEQ = 512
NT = SEQ // P
NS = 8
TOK = SEQ + NS
TILES = [(t * P, P) for t in range(NT)] + [(SEQ, NS)]
ROWS = NS + 1
HD, HEADS, GROUPS = 64, 8, 3
GW = HEADS * HD
ATT = GROUPS * GW
GM_HEADS, GM = 4, 512
WIN = 3 * ATT + 2 * GM
WINDOWS = ((128, 1), (512, 4), (2048, 16))
FOLD = 4
REACH = 128
PH, TOPK, NKEYS = 8, 16, 128
SLOTS = PH * TOPK
CK = 256
EPS = 1e-6
NEG = -1e30
SH1, SC1, GT1, SH2, SC2, GT2 = range(6)


class Memory:

    def __init__(self, nc, ctx, stage):
        self.nc, self.ctx, self.stage = nc, ctx, stage

    def sb(self, name, shape, dt=F32):
        return self.ctx.enter_context(self.nc.sbuf_tensor(f"{self.stage}_{name}", shape, dt))

    def ps(self, name, shape, dt=F32):
        return self.ctx.enter_context(self.nc.psum_tensor(f"{self.stage}_{name}", shape, dt))

    def sem(self, name):
        return self.ctx.enter_context(self.nc.semaphore(f"{self.stage}_{name}"))


class Chain:

    def __init__(self, eng, sem, base=0):
        self.eng, self.sem, self.base, self.n = eng, sem, base, 0

    def link(self, ins):
        ins.then_inc(self.sem, 1)
        self.n += 1
        self.eng.wait_ge(self.sem, self.base + self.n)


def repeat(eng, count, body):
    body(0)
    if count > 1:
        with eng.Fori(1, count) as i:
            body(i)


def after(eng, sem, value):
    if not isinstance(value, int) or value > 0:
        eng.wait_ge(sem, value)


def identity(nc, pool, ident, made):
    nc.gpsimd.memset(ident[:], 0.0).then_inc(made, 1)
    pool.wait_ge(made, 1)
    nc.gpsimd.affine_select(out=ident[:], in_=ident[:], compare_op=ALU.not_equal, fill=1.0, base=0,
                            pattern=[[-1, P]], channel_multiplier=1).then_inc(made, 1)


def modulation_stage(nc, ident, ident_made, c_prompt, c_sample, w_ada, b_ada, norm_g, mods_d):
    N = 512
    CHUNKS = 6 * D // N
    w_view = w_ada[0].rearrange("(k p) n -> p k n", p=P)
    b_row = b_ada[0:1, :]
    with ExitStack() as ctx:
        m = Memory(nc, ctx, "ada")
        cond = m.sb("cond", [ROWS, D])
        act_c = m.sb("act_c", [ROWS, D])
        condT = m.sb("condT", [P, KD, ROWS])
        w = m.sb("w", [P, 2, KD, N])
        bias = m.sb("bias", [ROWS, 2, N])
        gains = m.sb("gains", [ROWS, 4, D])
        mods = m.sb("mods", [ROWS, 6, D])
        mods_flat = mods[:].rearrange("r s n -> r (s n)")
        psT = m.ps("psT", [P, KD, ROWS])
        acc = [m.ps(f"acc{j}", [P, N]) for j in range(2)]
        c_in, g_in = m.sem("c_in"), m.sem("g_in")
        silu_done, turned, condT_ready = m.sem("silu_done"), m.sem("turned"), m.sem("condT_ready")
        w_in = [m.sem(f"w_in{j}") for j in range(2)]
        bias_in = [m.sem(f"bias_in{j}") for j in range(2)]
        chunk_done = [m.sem(f"chunk_done{j}") for j in range(2)]
        biased = [m.sem(f"biased{j}") for j in range(2)]
        folded, stored = m.sem("folded"), m.sem("stored")
        block = ctx.enter_context(nc.Block())

        @block.sync
        def _(sp):
            sp.dma_start(cond[0:NS, :], c_sample[:, :]).then_inc(c_in, 16)
            sp.dma_start(cond[NS:ROWS, :], c_prompt[:, :]).then_inc(c_in, 16)
            def chunk_pair(i):
                for j in range(2):
                    after(sp, chunk_done[j], i)
                    sp.dma_start(w[:, j], w_view[:, :, ds((2 * i + j) * N, N)]).then_inc(w_in[j], 16)
                    after(sp, biased[j], i)
                    sp.dma_start(bias[:, j], bcast(b_row[:, ds((2 * i + j) * N, N)], ROWS)).then_inc(bias_in[j], 16)

            repeat(sp, CHUNKS // 2, chunk_pair)
            sp.wait_ge(folded, 4)
            sp.dma_start(mods_d.rearrange("r s n -> r (s n)"), mods_flat).then_inc(stored, 16)
            sp.wait_ge(stored, 16)

        @block.gpsimd
        def _(pool):
            pool.dma_start(gains[:].rearrange("r s n -> r (s n)"),
                           bcast(norm_g.rearrange("a s n -> a (s n)"), ROWS)).then_inc(g_in, 16)
            identity(nc, pool, ident, ident_made)

        @block.scalar
        def _(act):
            act.wait_ge(c_in, 32)
            nc.scalar.activation(act_c[:], cond[:], ACT.Silu).then_inc(silu_done, 1)

        @block.tensor
        def _(pe):
            pe.wait_ge(ident_made, 2)
            pe.wait_ge(silu_done, 1)
            for k in range(KD):
                last = nc.tensor.transpose(psT[:, k, :], act_c[:, k * P:(k + 1) * P], ident[0:ROWS, 0:ROWS])
            last.then_inc(turned, 1)
            pe.wait_ge(condT_ready, 1)
            def chunk_pair(i):
                for j in range(2):
                    pe.wait_ge(w_in[j], 16 * i + 16)
                    after(pe, biased[j], i)
                    for k in range(KD):
                        last = nc.tensor.matmul(acc[j][0:ROWS, :], condT[:, k, :], w[:, j, k, :],
                                                start=(k == 0), stop=(k == KD - 1))
                    last.then_inc(chunk_done[j], 1)

            repeat(pe, CHUNKS // 2, chunk_pair)
        @block.vector
        def _(dve):
            dve.wait_ge(turned, 1)
            nc.vector.tensor_copy(condT[:], psT[:]).then_inc(condT_ready, 1)
            def chunk_pair(i):
                for j in range(2):
                    dve.wait_ge(chunk_done[j], i + 1)
                    dve.wait_ge(bias_in[j], 16 * i + 16)
                    nc.vector.tensor_tensor(mods_flat[:, ds((2 * i + j) * N, N)], acc[j][0:ROWS, :], bias[:, j],
                                            ALU.add).then_inc(biased[j], 1)

            repeat(dve, CHUNKS // 2, chunk_pair)
            dve.wait_ge(g_in, 16)
            for j in range(2):
                dve.wait_ge(biased[j], CHUNKS // 2)
            for scale, g in ((SC1, 0), (SC2, 2)):
                nc.vector.scalar_tensor_tensor(mods[:, scale], mods[:, scale], 1.0, gains[:, g], ALU.add,
                                               ALU.mult).then_inc(folded, 1)
            for gate, g in ((GT1, 1), (GT2, 3)):
                nc.vector.tensor_tensor(mods[:, gate], mods[:, gate], gains[:, g], ALU.mult).then_inc(folded, 1)


def bcast(row, n):
    return row.to_broadcast([n, row.shape[1]])


def load_mods(eng, mods_d, section, prompt_row, sample_rows, landed):
    eng.dma_start(prompt_row, bcast(mods_d[NS:ROWS, section, :], P)).then_inc(landed, 16)
    eng.dma_start(sample_rows, mods_d[0:NS, section, :]).then_inc(landed, 16)


def turn(nc, pe, src, n, psT, ident, psT_free, turned, done):
    for q in range(4):
        if done + q >= 3:
            pe.wait_ge(psT_free, done + q - 2)
        for b in range(4):
            k = 4 * q + b
            last = nc.tensor.transpose(psT[:, (done + q) % 3, b, 0:n], src[0:n, k * P:(k + 1) * P], ident[0:n, 0:n])
        last.then_inc(turned, 1)


def projection_stage(nc, ident, x_prompt, x_sample, mods_d, w_in, proj_d):
    CHUNKS = WIN // CK
    w_view = w_in[0].rearrange("(k p) n -> p k n", p=P)
    proj_prompt = proj_d[0:SEQ, :].rearrange("(t p) n -> p t n", p=P)
    with ExitStack() as ctx:
        m = Memory(nc, ctx, "proj")
        x = m.sb("x", [P, 2, D])
        sq = m.sb("sq", [P, D])
        scale_p, shift_p = m.sb("scale_p", [P, D]), m.sb("shift_p", [P, D])
        scale_s, shift_s = m.sb("scale_s", [NS, D]), m.sb("shift_s", [NS, D])
        stat = m.sb("stat", [P, 3, len(TILES)])
        eps = m.sb("eps", [P, 1])
        hT = m.sb("hT", [P, KD, TOK])
        w = m.sb("w", [P, 2, KD, CK])
        out = m.sb("out", [P, 2, len(TILES), CK])
        psT = m.ps("psT", [P, 3, 4, P])
        acc = [m.ps(f"acc{t}", [P, 512]) for t in range(len(TILES))]
        mod_in, eps_set = m.sem("mod_in"), m.sem("eps_set")
        x_in = [m.sem(f"x_in{j}") for j in range(2)]
        squared, rooted, inverse, scaled, shifted = (m.sem(s) for s in ("squared", "rooted", "inverse", "scaled", "shifted"))
        turned, psT_free = m.sem("turned"), m.sem("psT_free")
        w_ready = [m.sem(f"w_ready{j}") for j in range(2)]
        acc_full = [m.sem(f"acc_full{j}") for j in range(2)]
        out_full = [m.sem(f"out_full{j}") for j in range(2)]
        stored = [m.sem(f"stored{j}") for j in range(2)]
        NTL = len(TILES)
        block = ctx.enter_context(nc.Block())

        @block.sync
        def _(sp):
            for t, (at, n) in enumerate(TILES):
                if t >= 2:
                    sp.wait_ge(turned, 4 * (t - 1))
                src = x_prompt[0, at:at + n, :] if t < NT else x_sample.rearrange("b s d -> (b s) d")
                sp.dma_start(x[0:n, t % 2], src).then_inc(x_in[t % 2], 16)
                if t == 1:
                    load_mods(sp, mods_d, SC1, scale_p[:], scale_s[:], mod_in)
                    load_mods(sp, mods_d, SH1, shift_p[:], shift_s[:], mod_in)
            def chunk_pair(i):
                for j in range(2):
                    after(sp, acc_full[j], NTL * i)
                    sp.dma_start(w[:, j], w_view[:, :, ds((2 * i + j) * CK, CK)]).then_inc(w_ready[j], 16)

            repeat(sp, CHUNKS // 2, chunk_pair)
        @block.gpsimd
        def _(pool):
            nc.gpsimd.memset(eps[:], EPS).then_inc(eps_set, 1)
            def chunk_pair(i):
                for j in range(2):
                    cols = ds((2 * i + j) * CK, CK)
                    pool.wait_ge(out_full[j], NTL * i + NTL)
                    pool.dma_start(proj_prompt[:, :, cols], out[:, j, 0:NT]).then_inc(stored[j], 16)
                    pool.dma_start(proj_d[SEQ:TOK, cols], out[0:NS, j, NT]).then_inc(stored[j], 16)

            repeat(pool, CHUNKS // 2, chunk_pair)
            for j in range(2):
                pool.wait_ge(stored[j], 16 * CHUNKS)

        @block.scalar
        def _(act):
            act.wait_ge(eps_set, 1)
            for t, (at, n) in enumerate(TILES):
                act.wait_ge(x_in[t % 2], 16 * (t // 2 + 1))
                if t:
                    act.wait_ge(squared, t)
                nc.scalar.activation(sq[0:n, :], x[0:n, t % 2], ACT.Square,
                                     accum_out=stat[0:n, 0, t:t + 1]).then_inc(squared, 1)
                act.wait_ge(squared, t + 1)
                nc.scalar.activation(stat[0:n, 1, t:t + 1], stat[0:n, 0, t:t + 1], ACT.Sqrt, bias=eps[0:n, :],
                                     scale=1.0 / D).then_inc(rooted, 1)
                for q in range(4):
                    act.wait_ge(turned, 4 * t + q + 1)
                    nc.scalar.copy(hT[:, 4 * q:4 * q + 4, at:at + n], psT[:, (4 * t + q) % 3, :, 0:n])\
                        .then_inc(psT_free, 1)
            def chunk_pair(i):
                for j in range(2):
                    after(act, stored[j], 32 * i)
                    for t, (at, n) in enumerate(TILES):
                        act.wait_ge(acc_full[j], NTL * i + t + 1)
                        nc.scalar.copy(out[0:n, j, t], acc[t][0:n, 0:CK]).then_inc(out_full[j], 1)

            repeat(act, CHUNKS // 2, chunk_pair)
        @block.vector
        def _(dve):
            for t, (at, n) in enumerate(TILES):
                dve.wait_ge(rooted, t + 1)
                nc.vector.reciprocal(stat[0:n, 2, t:t + 1], stat[0:n, 1, t:t + 1]).then_inc(inverse, 1)
                dve.wait_ge(inverse, t + 1)
                if t == 0:
                    dve.wait_ge(mod_in, 64)
                xt = x[0:n, t % 2]
                gain, shift = (scale_p, shift_p) if t < NT else (scale_s, shift_s)
                nc.vector.scalar_tensor_tensor(xt, xt, stat[0:n, 2, t:t + 1], gain[0:n, :], ALU.mult,
                                               ALU.mult).then_inc(scaled, 1)
                dve.wait_ge(scaled, t + 1)
                nc.vector.tensor_tensor(xt, xt, shift[0:n, :], ALU.add).then_inc(shifted, 1)

        @block.tensor
        def _(pe):
            for t, (at, n) in enumerate(TILES):
                pe.wait_ge(shifted, t + 1)
                turn(nc, pe, x[:, t % 2], n, psT, ident, psT_free, turned, 4 * t)
            pe.wait_ge(psT_free, 4 * NTL)
            def chunk_pair(i):
                for j in range(2):
                    pe.wait_ge(w_ready[j], 16 * i + 16)
                    after(pe, out_full[1 - j], NTL * (i + j))
                    for t, (at, n) in enumerate(TILES):
                        for k in range(KD):
                            last = nc.tensor.matmul(acc[t][0:n, 0:CK], hT[:, k, at:at + n], w[:, j, k, :],
                                                    start=(k == 0), stop=(k == KD - 1))
                        last.then_inc(acc_full[j], 1)

            repeat(pe, CHUNKS // 2, chunk_pair)

def mixer_stage(nc, ident, proj_d, cache, gm_ln_g, gm_ln_b, w_s, b_s, mix_d, outs):
    fold = proj_d[0:SEQ, :].rearrange("(i r) c -> i r c", r=FOLD)
    mix_fold = mix_d[0:SEQ, :].rearrange("(i r) c -> i r c", r=FOLD)
    KEYS = 6 * P
    PAIRS = GW // P
    NQ, NK = GROUPS * PAIRS, (GROUPS - 1) * PAIRS
    TURNS = (NQ + NK) // 4
    SCALE = HD ** -0.5
    LINKS = 8
    V0 = 2 * ATT
    with ExitStack() as ctx:
        m = Memory(nc, ctx, "mix")
        k0n = m.sb("k0n", [P, FOLD, GW])
        v = m.sb("v", [P, FOLD, ATT])
        qkn = m.sb("qkn", [P, (NQ + NK) * P])
        kT0 = m.sb("kT0", [P, PAIRS, FOLD, P])
        qkT = m.sb("qkT", [P, NQ + NK, P])
        mask = m.sb("mask", [P, FOLD, 6, P])
        steps = m.sb("steps", [P, P], mybir.dt.int32)
        off = m.sb("off", [P, P])
        scores = m.sb("scores", [P, 2, KEYS])
        probs = m.sb("probs", [P, 2, KEYS])
        probsT = m.sb("probsT", [P, 2, 6, P])
        top, den, inv = m.sb("top", [P, HEADS]), m.sb("den", [P, HEADS]), m.sb("inv", [P, HEADS])
        att = m.sb("att", [P, GROUPS, HEADS, HD])
        gin = m.sb("gin", [P, 2, 2 * GM])
        gsq = m.sb("gsq", [P, GM])
        gst = m.sb("gst", [P, 3, GM_HEADS])
        gain, shift = m.sb("gain", [P, GM]), m.sb("shift", [P, GM])
        wn, wT = m.sb("wn", [P, GM_HEADS, P]), m.sb("wT", [P, GM_HEADS, P])
        bn, bT = m.sb("bn", [GM_HEADS, P]), m.sb("bT", [P, GM_HEADS])
        w00, b00 = m.sb("w00", [NS, GM_HEADS, 1]), m.sb("b00", [NS, GM_HEADS, 1])
        gout = m.sb("gout", [P, GM])
        eps = m.sb("eps", [P, 1])
        kv = m.sb("kv", [P, 2, GROUPS, 2, GW])
        qb = m.sb("qb", [P, 2, ATT])
        own = m.sb("own", [HEADS, 2, 3, GROUPS, HD])
        prod = m.sb("prod", [P, ATT])
        s24 = m.sb("s24", [P, GROUPS, HEADS])
        srow = m.sb("srow", [HEADS, GROUPS, P + 1])
        oprod = m.sb("oprod", [HEADS, GROUPS, HD])
        oself = m.sb("oself", [HEADS, GROUPS, 1])
        sst = m.sb("sst", [HEADS, 3])
        pT = m.sb("pT", [P, GROUPS, HEADS])
        spread = m.sb("spread", [HEADS, GROUPS, HEADS, HD])
        ones = m.sb("ones", [P, 1])
        arow = m.sb("arow", [1, ATT])

        psS = m.ps("psS", [P, 2, 1024])
        psP = m.ps("psP", [P, 1024])
        psO = m.ps("psO", [P, 512])
        psX = m.ps("psX", [P, 4, P])

        S = {n: m.sem(n) for n in (
            "k0_in", "v_in", "g_masked", "w_turned", "qk_in", "kept", "g_const", "masks", "mchain", "x_full", "x_free",
            "scored", "masked", "maxed", "exped", "p_turned", "p_copied", "mixed", "inverted", "normalised", "att_stored",
            "gelued", "gchain", "g_var", "g_root", "g_normed", "z_done", "g_out", "g_stored", "gv_stored",
            "s_in0", "s_in1", "schain", "s_scored", "s_turned", "s_max", "s_exp", "s_probs", "s_pT", "s_spread", "s_mixed",
            "s_row", "s_stored", "s_seen")}
        g_in = [m.sem(f"g_in{j}") for j in range(2)]
        s_in = [S["s_in0"], S["s_in1"]]
        block = ctx.enter_context(nc.Block())

        def last_of(t):
            return (t // 2 + 1) * 16

        @block.sync
        def _(sp):
            sp.dma_start(k0n[:], fold[:, :, ATT:ATT + GW]).then_inc(S["k0_in"], 16)
            for t in range(2):
                at, n = TILES[t]
                sp.dma_start(gin[0:n, t], proj_d[at:at + n, 3 * ATT:WIN]).then_inc(g_in[t], 16)
            sp.dma_start(wn[:], w_s[0].rearrange("h q p -> q h p")).then_inc(S["g_const"], 16)
            sp.dma_start(bn[:], b_s[0]).then_inc(S["g_const"], 16)
            sp.dma_start(gain[:], bcast(gm_ln_g.rearrange("a h c -> a (h c)"), P)).then_inc(S["g_const"], 16)
            sp.dma_start(shift[:], bcast(gm_ln_b.rearrange("a h c -> a (h c)"), P)).then_inc(S["g_const"], 16)
            with nc.allow_non_contiguous_dma(reason="four weights of one position"):
                for h in range(GM_HEADS):
                    sp.dma_start(w00[:, h, :], bcast(w_s[0, h, 0:1, 0:1], NS)).then_inc(S["g_const"], 16)
                    sp.dma_start(b00[:, h, :], bcast(b_s[0, h:h + 1, 0:1], NS)).then_inc(S["g_const"], 16)
            sp.dma_start(v[:], fold[:, :, V0:V0 + ATT]).then_inc(S["v_in"], 16)
            for t in range(2, len(TILES)):
                at, n = TILES[t]
                sp.wait_ge(S["g_out"], t - 1)
                sp.dma_start(gin[0:n, t % 2], proj_d[at:at + n, 3 * ATT:WIN]).then_inc(g_in[t % 2], 16)

            def load_qk(r):
                if not isinstance(r, int):
                    sp.wait_ge(S["x_full"], FOLD + 1 + TURNS * r)
                sp.dma_start(qkn[:, 0:ATT], fold[:, ds(r, 1), 0:ATT].rearrange("i a c -> i (a c)")).then_inc(S["qk_in"], 16)
                sp.dma_start(qkn[:, ATT:], fold[:, ds(r, 1), ATT + GW:2 * ATT].rearrange("i a c -> i (a c)"))\
                  .then_inc(S["qk_in"], 16)

            repeat(sp, FOLD, load_qk)
            n = 0
            for g, (win, dil) in enumerate(WINDOWS):
                keep = min(win, SEQ)
                for c in range(2):
                    src = proj_d[:, (1 + c) * ATT + g * GW:(1 + c) * ATT + (g + 1) * GW]
                    sp.dma_start(outs[2 + g][0, 0, :, c].rearrange("s h d -> s (h d)"), src[SEQ - keep:SEQ])\
                      .then_inc(S["kept"], 16)
                    sp.dma_start(outs[5 + g][0, :, 0, c].rearrange("s h d -> s (h d)"), src[SEQ:TOK])\
                      .then_inc(S["kept"], 16)
                    n += 2
            sp.wait_ge(S["kept"], 16 * n)
            sp.wait_ge(S["g_stored"], 16 * len(TILES))
            sp.wait_ge(S["gv_stored"], 16)

        @block.gpsimd
        def _(pool):
            pool.wait_ge(S["g_const"], 16 * (4 + 2 * GM_HEADS))
            nc.gpsimd.affine_select(out=wn[:], in_=wn[:], compare_op=ALU.is_ge, fill=0.0, base=0,
                                    pattern=[[0, GM_HEADS], [-1, P]], channel_multiplier=1).then_inc(S["g_masked"], 1)
            chain = Chain(pool, S["masks"])
            chain.link(nc.gpsimd.memset(mask[:], 0.0))
            chain.link(nc.gpsimd.memset(eps[:], EPS))
            chain.link(nc.gpsimd.memset(ones[:], 1.0))
            near = mask[:, :, 0:FOLD]
            chain.link(nc.gpsimd.affine_select(out=near, in_=near, compare_op=ALU.is_ge, fill=NEG, base=0,
                                               pattern=[[1, FOLD], [-1, FOLD], [-4, P]], channel_multiplier=4))
            chain.link(nc.gpsimd.affine_select(out=near, in_=near, compare_op=ALU.is_ge, fill=NEG, base=REACH,
                                               pattern=[[-1, FOLD], [1, FOLD], [4, P]], channel_multiplier=-4))
            far = mask[:, :, FOLD:6]
            chain.link(nc.gpsimd.affine_select(out=far, in_=far, compare_op=ALU.is_ge, fill=NEG, base=0,
                                               pattern=[[0, FOLD], [0, 2], [-1, P]], channel_multiplier=1))
            chain.link(nc.gpsimd.iota(steps[:], pattern=[[-1, P]], base=P, channel_multiplier=1))

            def store_att(r):
                pool.wait_ge(S["normalised"], HEADS * r + HEADS)
                pool.dma_start(mix_fold[:, ds(r, 1), 0:ATT].rearrange("i a c -> i (a c)"),
                               att[:].rearrange("p g h d -> p (g h d)")).then_inc(S["att_stored"], 16)

            repeat(pool, FOLD, store_att)

            def load_sample(i):
                for j in range(2):
                    b = 2 * i + j
                    after(pool, S["s_mixed"], b - 1)
                    for g, (win, dil) in enumerate(WINDOWS):
                        src = cache[g][0, ds(b, 1)].rearrange("a (j s) c h d -> (a j) s c (h d)", s=dil)[:, 0]
                        pool.dma_start(kv[:, j, g], src).then_inc(s_in[j], 16)
                    row = proj_d[ds(b + SEQ, 1), :]
                    pool.dma_start(qb[:, j], bcast(row[:, 0:ATT], P)).then_inc(s_in[j], 16)
                    for c in range(3):
                        pool.dma_start(own[:, j, c], row[:, c * ATT:(c + 1) * ATT].rearrange(
                            "a (g h d) -> (a h) g d", g=GROUPS, h=HEADS)).then_inc(s_in[j], 16)

            repeat(pool, NS // 2, load_sample)
            pool.wait_ge(S["att_stored"], 16 * FOLD)
            pool.wait_ge(S["s_stored"], 16 * NS)

        def mul_bcast(out, a, b, shape):
            return nc.vector.tensor_tensor(out, a, b.to_broadcast(shape), ALU.mult)

        @block.vector
        def _(dve):
            chain = Chain(dve, S["mchain"])
            dve.wait_ge(S["masks"], 7)
            chain.link(nc.vector.tensor_scalar(steps[:], steps[:], FOLD - 1, None, ALU.bitwise_and))
            chain.link(nc.vector.tensor_scalar(off[:], steps[:], 0.5, NEG, ALU.is_gt, ALU.mult))
            for r in range(FOLD):
                chain.link(nc.vector.tensor_tensor(mask[:, r, 5], mask[:, r, 5], off[:], ALU.min))

            g = Chain(dve, S["gchain"])
            dve.wait_ge(S["g_const"], 16 * (4 + 2 * GM_HEADS))
            for t, (at, n) in enumerate(TILES):
                dve.wait_ge(S["gelued"], t + 1)
                u = gin[0:n, t % 2, 0:GM].rearrange("p (h c) -> p h c", h=GM_HEADS)
                w = gin[0:n, t % 2, GM:]
                wh = w.rearrange("p (h c) -> p h c", h=GM_HEADS)
                sqh = gsq[0:n].rearrange("p (h c) -> p h c", h=GM_HEADS)
                bc = [n, GM_HEADS, GM // GM_HEADS]
                mean, var, rstd = (gst[0:n, a, :] for a in range(3))
                g.link(nc.vector.tensor_reduce(mean, wh, AX_X, ALU.add))
                g.link(nc.vector.tensor_scalar(mean, mean, GM_HEADS / GM, None, ALU.mult))
                g.link(nc.vector.tensor_tensor(wh, wh, mean.unsqueeze(2).to_broadcast(bc), ALU.subtract))
                g.link(nc.vector.tensor_tensor(gsq[0:n], w, w, ALU.mult))
                nc.vector.tensor_reduce(var, sqh, AX_X, ALU.add).then_inc(S["g_var"], 1)
                dve.wait_ge(S["g_root"], t + 1)
                g.link(nc.vector.reciprocal(rstd, var))
                g.link(nc.vector.tensor_tensor(wh, wh, rstd.unsqueeze(2).to_broadcast(bc), ALU.mult))
                g.link(nc.vector.tensor_tensor(w, w, gain[0:n], ALU.mult))
                nc.vector.tensor_tensor(w, w, shift[0:n], ALU.add).then_inc(S["g_normed"], 1)
                if t >= 1:
                    dve.wait_ge(S["g_stored"], 16 * t)
                go = gout[0:n].rearrange("p (h c) -> p h c", h=GM_HEADS)
                if t < NT:
                    dve.wait_ge(S["z_done"], t + 1)
                    for h in range(GM_HEADS):
                        last = nc.vector.scalar_tensor_tensor(go[:, h], psO[:, h * P:(h + 1) * P], bT[:, h:h + 1],
                                                              u[:, h], ALU.add, ALU.mult)
                else:
                    dve.wait_ge(S["g_normed"], t + 1)
                    g.link(nc.vector.tensor_tensor(go, wh, w00[:].to_broadcast(bc), ALU.mult))
                    g.link(nc.vector.tensor_tensor(go, go, b00[:].to_broadcast(bc), ALU.add))
                    last = nc.vector.tensor_tensor(go, go, u, ALU.mult)
                last.then_inc(S["g_out"], 1)

            def finish(r, h):
                n = HEADS * r + h
                dve.wait_ge(S["mixed"], n + 1)
                nc.vector.reciprocal(inv[:, h:h + 1], den[:, h:h + 1]).then_inc(S["inverted"], 1)
                dve.wait_ge(S["inverted"], n + 1)
                if h == 0:
                    after(dve, S["att_stored"], 16 * r)
                nc.vector.tensor_scalar(att[:, :, h], psO[:, 0:GROUPS * HD].rearrange("p (g d) -> p g d", g=GROUPS),
                                        inv[:, h:h + 1], None, ALU.mult).then_inc(S["normalised"], 1)

            def fold_tile(r):
                for h in range(HEADS):
                    n = HEADS * r + h
                    dve.wait_ge(S["scored"], n + 1)
                    after(dve, S["exped"], n - 1)
                    nc.vector.scalar_tensor_tensor(scores[:, h % 2], psS[:, h % 2, 0:KEYS], SCALE,
                                                   mask[:, ds(r, 1)].rearrange("p a b k -> p (a b k)"),
                                                   ALU.mult, ALU.add).then_inc(S["masked"], 1)
                    dve.wait_ge(S["masked"], n + 1)
                    nc.vector.tensor_reduce(top[:, h:h + 1], scores[:, h % 2], AX_X, ALU.max, negate=True)\
                        .then_inc(S["maxed"], 1)
                    if h:
                        finish(r, h - 1)
                finish(r, HEADS - 1)

            repeat(dve, FOLD, fold_tile)

            def sample_pair(i):
                for j in range(2):
                    b = 2 * i + j
                    c = Chain(dve, S["schain"], LINKS * b)
                    dve.wait_ge(s_in[j], 7 * 16 * i + 7 * 16)
                    c.link(nc.vector.tensor_tensor(prod[:].rearrange("p (g w) -> p g w", g=GROUPS), kv[:, j, :, 0],
                                                   qb[:, j].rearrange("p (g w) -> p g w", g=GROUPS), ALU.mult))
                    nc.vector.tensor_reduce(s24[:], prod[:].rearrange("p (g h d) -> p g h d", g=GROUPS, h=HEADS),
                                            AX_X, ALU.add).then_inc(S["s_scored"], 1)
                    c.link(nc.vector.tensor_tensor(oprod[:], own[:, j, 0], own[:, j, 1], ALU.mult))
                    c.link(nc.vector.tensor_reduce(oself[:, :, 0], oprod[:], AX_X, ALU.add))
                    c.link(nc.vector.tensor_scalar(srow[:, :, P:P + 1], oself[:], SCALE, None, ALU.mult))
                    dve.wait_ge(S["s_turned"], b + 1)
                    c.link(nc.vector.tensor_scalar(srow[:, :, 0:P], psX[0:HEADS, 0:GROUPS, :], SCALE, None, ALU.mult))
                    flat = srow[:].rearrange("h g k -> h (g k)")
                    nc.vector.tensor_reduce(sst[:, 0:1], flat, AX_X, ALU.max, negate=True).then_inc(S["s_max"], 1)
                    dve.wait_ge(S["s_exp"], b + 1)
                    c.link(nc.vector.reciprocal(sst[:, 2:3], sst[:, 1:2]))
                    nc.vector.tensor_scalar(flat, flat, sst[:, 2:3], None, ALU.mult).then_inc(S["s_probs"], 1)
                    dve.wait_ge(S["s_probs"], b + 1)
                    c.link(mul_bcast(oprod[:], own[:, j, 2], srow[:, :, P:P + 1], [HEADS, GROUPS, HD]))
                    for g in range(GROUPS):
                        last = nc.vector.tensor_tensor(
                            spread[:, g], oprod[:, g:g + 1].to_broadcast([HEADS, HEADS, HD]),
                            ident[0:HEADS, 0:HEADS].unsqueeze(2).to_broadcast([HEADS, HEADS, HD]), ALU.mult)
                    last.then_inc(S["s_spread"], 1)
                    dve.wait_ge(S["s_pT"], 2 * b + 1)
                    nc.vector.tensor_copy(pT[:], psO[:, 0:GROUPS * HEADS].rearrange("p (g h) -> p g h", g=GROUPS))\
                        .then_inc(S["s_pT"], 1)
                    dve.wait_ge(S["s_pT"], 2 * b + 2)
                    for g in range(GROUPS):
                        last = mul_bcast(prod[:, g * GW:(g + 1) * GW].rearrange("p (h d) -> p h d", h=HEADS),
                                         kv[:, j, g, 1].rearrange("p (h d) -> p h d", h=HEADS),
                                         pT[:, g].unsqueeze(2), [P, HEADS, HD])
                    c.link(last)
                    assert c.n == LINKS
                    dve.wait_ge(S["s_mixed"], b + 1)

            repeat(dve, NS // 2, sample_pair)

        @block.scalar
        def _(act):
            for t, (at, n) in enumerate(TILES):
                act.wait_ge(g_in[t % 2], last_of(t))
                nc.scalar.activation(gin[0:n, t % 2], gin[0:n, t % 2], ACT.Gelu_apprx_tanh).then_inc(S["gelued"], 1)
                if t == 0:
                    for n_x in range(FOLD):
                        act.wait_ge(S["x_full"], n_x + 1)
                        nc.scalar.copy(kT0[:, :, n_x], psX[:]).then_inc(S["x_free"], 1)
                    act.wait_ge(S["x_full"], FOLD + 1)
                    nc.scalar.copy(bT[:], psP[:, 0:GM_HEADS]).then_inc(S["w_turned"], 1)
                    nc.scalar.copy(wT[:], psX[:]).then_inc(S["w_turned"], 1)
                    act.wait_ge(S["w_turned"], 2)
                    act.sem_inc(S["x_free"], 1)
                act.wait_ge(S["g_var"], t + 1)
                if t == 0:
                    act.wait_ge(S["masks"], 2)
                nc.scalar.activation(gst[0:n, 1, :], gst[0:n, 1, :], ACT.Sqrt, bias=eps[0:n, :],
                                     scale=GM_HEADS / GM).then_inc(S["g_root"], 1)
                if t < NT:
                    act.wait_ge(S["g_out"], t + 1)
                    act.dma_start(mix_d[at:at + n, ATT:], gout[0:n]).then_inc(S["g_stored"], 16)
                else:
                    act.wait_ge(S["g_normed"], t + 1)
                    act.dma_start(outs[8].rearrange("a b s h c -> (a b s) (h c)"), gin[0:n, t % 2, GM:])\
                       .then_inc(S["gv_stored"], 16)
                    act.wait_ge(S["g_out"], t + 1)
                    act.dma_start(mix_d[at:at + n, ATT:], gout[0:n]).then_inc(S["g_stored"], 16)

            def fold_tile(r):
                for q in range(TURNS):
                    act.wait_ge(S["x_full"], FOLD + 1 + TURNS * r + q + 1)
                    nc.scalar.copy(qkT[:, 4 * q:4 * q + 4], psX[:]).then_inc(S["x_free"], 1)

                def exponentials(h):
                    n = HEADS * r + h
                    act.wait_ge(S["maxed"], n + 1)
                    after(act, S["p_turned"], n - 1)
                    nc.scalar.activation(probs[:, h % 2], scores[:, h % 2], ACT.Exp, bias=top[:, h:h + 1],
                                         accum_out=den[:, h:h + 1]).then_inc(S["exped"], 1)

                exponentials(0)
                for h in range(HEADS):
                    n = HEADS * r + h
                    if h + 1 < HEADS:
                        exponentials(h + 1)
                    act.wait_ge(S["p_turned"], n + 1)
                    after(act, S["mixed"], n - 1)
                    nc.scalar.copy(probsT[:, h % 2].rearrange("p b k -> p (b k)"), psP[:, 0:KEYS])\
                        .then_inc(S["p_copied"], 1)

            repeat(act, FOLD, fold_tile)

            def sample(b):
                act.wait_ge(S["s_max"], b + 1)
                flat = srow[:].rearrange("h g k -> h (g k)")
                nc.scalar.activation(flat, flat, ACT.Exp, bias=sst[:, 0:1], accum_out=sst[:, 1:2]).then_inc(S["s_exp"], 1)
                act.wait_ge(S["s_mixed"], b + 1)
                after(act, S["s_stored"], 16 * b)
                nc.scalar.copy(arow[:], psS[0:1].rearrange("p a k -> p (a k)")[:, 0:ATT]).then_inc(S["s_row"], 1)
                act.wait_ge(S["s_row"], b + 1)
                act.dma_start(mix_d[ds(b + SEQ, 1), 0:ATT], arow[:]).then_inc(S["s_stored"], 16)

            repeat(act, NS, sample)

        @block.tensor
        def _(pe):
            pe.wait_ge(S["k0_in"], 16)
            for r in range(FOLD):
                if r:
                    pe.wait_ge(S["x_free"], r)
                for p in range(PAIRS):
                    last = nc.tensor.transpose(psX[:, p], k0n[:, r, p * P:(p + 1) * P], ident[:])
                last.then_inc(S["x_full"], 1)
            pe.wait_ge(S["g_masked"], 1)
            pe.wait_ge(S["x_free"], FOLD)
            for h in range(GM_HEADS):
                nc.tensor.transpose(psX[:, h], wn[:, h], ident[:])
            nc.tensor.transpose(psP[:, 0:GM_HEADS], bn[:], ident[0:GM_HEADS, 0:GM_HEADS]).then_inc(S["x_full"], 1)
            pe.wait_ge(S["w_turned"], 2)
            for t in range(NT):
                pe.wait_ge(S["g_normed"], t + 1)
                if t:
                    pe.wait_ge(S["g_out"], t)
                for h in range(GM_HEADS):
                    last = nc.tensor.matmul(psO[:, h * P:(h + 1) * P], wT[:, h], gin[:, t % 2, GM + h * P:GM + (h + 1) * P],
                                            start=True, stop=True)
                last.then_inc(S["z_done"], 1)
            pe.wait_ge(S["v_in"], 16)

            def fold_tile(r):
                pe.wait_ge(S["qk_in"], 32 * r + 32)
                for q in range(TURNS):
                    pe.wait_ge(S["x_free"], FOLD + 1 + TURNS * r + q)
                    for b in range(4):
                        c = (4 * q + b) * P
                        last = nc.tensor.transpose(psX[:, b], qkn[:, c:c + P], ident[:])
                    last.then_inc(S["x_full"], 1)
                pe.wait_ge(S["x_free"], FOLD + 1 + TURNS * r + TURNS)

                def score(h):
                    n = HEADS * r + h
                    rows, p = slice(h % 2 * HD, h % 2 * HD + HD), h // 2
                    after(pe, S["masked"], n - 1)
                    nc.tensor.matmul(psS[:, h % 2, 0:FOLD * P], qkT[rows, p], kT0[rows, p].rearrange("p r k -> p (r k)"),
                                     start=True, stop=True)
                    for g in range(1, GROUPS):
                        last = nc.tensor.matmul(psS[:, h % 2, (FOLD + g - 1) * P:(FOLD + g) * P], qkT[rows, g * PAIRS + p],
                                                qkT[rows, NQ + (g - 1) * PAIRS + p], start=True, stop=True)
                    last.then_inc(S["scored"], 1)

                def turn_probs(h):
                    n = HEADS * r + h
                    pe.wait_ge(S["exped"], n + 1)
                    after(pe, S["p_copied"], n)
                    for b in range(6):
                        last = nc.tensor.transpose(psP[:, b * P:(b + 1) * P], probs[:, h % 2, b * P:(b + 1) * P], ident[:])
                    last.then_inc(S["p_turned"], 1)

                def mix(h):
                    n = HEADS * r + h
                    pe.wait_ge(S["p_copied"], n + 1)
                    if isinstance(n, int) and n == 0:
                        pe.wait_ge(S["g_out"], NT)
                    after(pe, S["normalised"], n)
                    for b in range(FOLD):
                        nc.tensor.matmul(psO[:, 0:HD], probsT[:, h % 2, b], v[:, b, h * HD:(h + 1) * HD],
                                         start=(b == 0), stop=(b == FOLD - 1))
                    for g in range(1, GROUPS):
                        last = nc.tensor.matmul(psO[:, g * HD:(g + 1) * HD], probsT[:, h % 2, FOLD + g - 1],
                                                v[:, ds(r, 1), g * GW + h * HD:g * GW + (h + 1) * HD]
                                                .rearrange("p a d -> p (a d)"), start=True, stop=True)
                    last.then_inc(S["mixed"], 1)

                score(0)
                for h in range(HEADS):
                    if h + 1 < HEADS:
                        score(h + 1)
                    turn_probs(h)
                    if h:
                        mix(h - 1)
                mix(HEADS - 1)

            repeat(pe, FOLD, fold_tile)
            pe.wait_ge(S["normalised"], FOLD * HEADS)

            def sample(b):
                pe.wait_ge(S["s_scored"], b + 1)
                for g in range(GROUPS):
                    last = nc.tensor.transpose(psX[0:HEADS, g], s24[:, g], ident[:])
                last.then_inc(S["s_turned"], 1)
                pe.wait_ge(S["s_probs"], b + 1)
                pe.sem_inc(S["s_seen"], 1)
                for g in range(GROUPS):
                    last = nc.tensor.transpose(psO[:, g * HEADS:(g + 1) * HEADS], srow[:, g, 0:P],
                                               ident[0:HEADS, 0:HEADS])
                last.then_inc(S["s_pT"], 1)
                pe.wait_ge(S["schain"], LINKS * b + LINKS)
                pe.wait_ge(S["s_spread"], b + 1)
                after(pe, S["s_row"], b)
                sums = psS[0:1].rearrange("p a k -> p (a k)")
                for g in range(GROUPS):
                    cols = slice(g * GW, (g + 1) * GW)
                    nc.tensor.matmul(sums[:, cols], ones[:], prod[:, cols], start=True, stop=False)
                    last = nc.tensor.matmul(sums[:, cols], ones[0:HEADS], spread[:, g].rearrange("p h d -> p (h d)"),
                                            start=False, stop=True)
                last.then_inc(S["s_mixed"], 1)

            repeat(pe, NS, sample)


def output_stage(nc, ident, x_prompt, x_sample, mods_d, w_out, mix_d, hT, x1_d, h2_d):
    CHUNKS = D // CK
    NTL = len(TILES)
    w_view = w_out[0].rearrange("(k p) n -> p k n", p=P)
    with ExitStack() as ctx:
        m = Memory(nc, ctx, "out")
        xin = m.sb("xin", [P, 2, D])
        sq = m.sb("sq", [P, D])
        y = m.sb("y", [P, NTL, D])
        w = m.sb("w", [P, 2, KD, CK])
        vec_p = {s: m.sb(f"vec_p{s}", [P, D]) for s in (GT1, SC2, SH2)}
        vec_s = {s: m.sb(f"vec_s{s}", [NS, D]) for s in (GT1, SC2, SH2)}
        stat = m.sb("stat", [P, 6, NTL])
        eps = m.sb("eps", [P, 1])
        psT = m.ps("psT", [P, 3, 4, P])
        acc = [m.ps(f"acc{t}", [P, 512]) for t in range(NTL)]
        mix_in = [m.sem(f"mix_in{j}") for j in range(2)]
        x_in = [m.sem(f"x_in{j}") for j in range(2)]
        w_ready = [m.sem(f"w_ready{j}") for j in range(2)]
        acc_full = [m.sem(f"acc_full{j}") for j in range(2)]
        copied = [m.sem(f"copied{j}") for j in range(2)]
        mod_in, eps_set, turned, psT_free, squared, rooted, chain_v, x1_done, h2_done, stored = (m.sem(s) for s in (
            "mod_in", "eps_set", "turned", "psT_free", "squared", "rooted", "chain", "x1_done", "h2_done", "stored"))
        LINKS = 4
        block = ctx.enter_context(nc.Block())

        @block.sync
        def _(sp):
            for t, (at, n) in enumerate(TILES):
                if t >= 2:
                    sp.wait_ge(turned, 4 * (t - 1))
                sp.dma_start(xin[0:n, t % 2], mix_d[at:at + n, :]).then_inc(mix_in[t % 2], 16)

            def chunk_pair(i):
                for j in range(2):
                    after(sp, acc_full[j], NTL * i)
                    sp.dma_start(w[:, j], w_view[:, :, ds((2 * i + j) * CK, CK)]).then_inc(w_ready[j], 16)

            repeat(sp, CHUNKS // 2, chunk_pair)
            for s in (GT1, SC2, SH2):
                load_mods(sp, mods_d, s, vec_p[s][:], vec_s[s][:], mod_in)
            for t, (at, n) in enumerate(TILES):
                if t < 2:
                    sp.wait_ge(turned, 4 * NTL)
                else:
                    sp.wait_ge(stored, 32 * (t - 1))
                src = x_prompt[0, at:at + n, :] if t < NT else x_sample.rearrange("b s d -> (b s) d")
                sp.dma_start(xin[0:n, t % 2], src).then_inc(x_in[t % 2], 16)

        @block.gpsimd
        def _(pool):
            nc.gpsimd.memset(eps[:], EPS).then_inc(eps_set, 1)
            for t, (at, n) in enumerate(TILES):
                pool.wait_ge(h2_done, t + 1)
                if t:
                    pool.wait_ge(stored, 32 * t)
                pool.dma_start(x1_d[at:at + n, :], xin[0:n, t % 2]).then_inc(stored, 16)
                pool.dma_start(h2_d[at:at + n, :], y[0:n, t]).then_inc(stored, 16)
            pool.wait_ge(stored, 32 * NTL)

        @block.scalar
        def _(act):
            for t, (at, n) in enumerate(TILES):
                for q in range(4):
                    act.wait_ge(turned, 4 * t + q + 1)
                    nc.scalar.copy(hT[:, 4 * q:4 * q + 4, at:at + n], psT[:, (4 * t + q) % 3, :, 0:n])\
                        .then_inc(psT_free, 1)

            def chunk_pair(i):
                for j in range(2):
                    for t, (at, n) in enumerate(TILES):
                        act.wait_ge(acc_full[j], NTL * i + t + 1)
                        nc.scalar.copy(y[0:n, t, ds((2 * i + j) * CK, CK)], acc[t][0:n, 0:CK]).then_inc(copied[j], 1)

            repeat(act, CHUNKS // 2, chunk_pair)
            act.wait_ge(eps_set, 1)
            for j in range(2):
                act.wait_ge(copied[j], NTL * CHUNKS // 2)
            for t, (at, n) in enumerate(TILES):
                for part, src in ((0, y[0:n, t]), (1, xin[0:n, t % 2])):
                    if part:
                        act.wait_ge(x1_done, t + 1)
                    if t or part:
                        act.wait_ge(squared, 2 * t + part)
                    s = 3 * part
                    nc.scalar.activation(sq[0:n, :], src, ACT.Square, accum_out=stat[0:n, s, t:t + 1]).then_inc(squared, 1)
                    act.wait_ge(squared, 2 * t + part + 1)
                    nc.scalar.activation(stat[0:n, s + 1, t:t + 1], stat[0:n, s, t:t + 1], ACT.Sqrt, bias=eps[0:n, :],
                                         scale=1.0 / D).then_inc(rooted, 1)
                for q in range(4):
                    act.wait_ge(turned, 4 * (NTL + t) + q + 1)
                    nc.scalar.copy(hT[:, 4 * q:4 * q + 4, at:at + n], psT[:, (4 * (NTL + t) + q) % 3, :, 0:n])\
                        .then_inc(psT_free, 1)

        @block.vector
        def _(dve):
            chain = Chain(dve, chain_v)
            dve.wait_ge(mod_in, 6 * 16)
            for t, (at, n) in enumerate(TILES):
                vec = vec_p if t < NT else vec_s
                yt, xt = y[0:n, t], xin[0:n, t % 2]
                dve.wait_ge(rooted, 2 * t + 1)
                chain.link(nc.vector.reciprocal(stat[0:n, 2, t:t + 1], stat[0:n, 1, t:t + 1]))
                chain.link(nc.vector.scalar_tensor_tensor(yt, yt, stat[0:n, 2, t:t + 1], vec[GT1][0:n], ALU.mult, ALU.mult))
                dve.wait_ge(x_in[t % 2], 16 * (t // 2 + 1))
                nc.vector.tensor_tensor(xt, xt, yt, ALU.add).then_inc(x1_done, 1)
                dve.wait_ge(rooted, 2 * t + 2)
                chain.link(nc.vector.reciprocal(stat[0:n, 5, t:t + 1], stat[0:n, 4, t:t + 1]))
                chain.link(nc.vector.scalar_tensor_tensor(yt, xt, stat[0:n, 5, t:t + 1], vec[SC2][0:n], ALU.mult, ALU.mult))
                nc.vector.tensor_tensor(yt, yt, vec[SH2][0:n], ALU.add).then_inc(h2_done, 1)

        @block.tensor
        def _(pe):
            for t, (at, n) in enumerate(TILES):
                pe.wait_ge(mix_in[t % 2], 16 * (t // 2 + 1))
                turn(nc, pe, xin[:, t % 2], n, psT, ident, psT_free, turned, 4 * t)
            pe.wait_ge(psT_free, 4 * NTL)

            def chunk_pair(i):
                for j in range(2):
                    pe.wait_ge(w_ready[j], 16 * i + 16)
                    after(pe, copied[1 - j], NTL * (i + j))
                    for t, (at, n) in enumerate(TILES):
                        for k in range(KD):
                            last = nc.tensor.matmul(acc[t][0:n, 0:CK], hT[:, k, at:at + n], w[:, j, k, :],
                                                    start=(k == 0), stop=(k == KD - 1))
                        last.then_inc(acc_full[j], 1)

            repeat(pe, CHUNKS // 2, chunk_pair)
            for t, (at, n) in enumerate(TILES):
                pe.wait_ge(h2_done, t + 1)
                turn(nc, pe, y[:, t], n, psT, ident, psT_free, turned, 4 * (NTL + t))


def routing_stage(nc, ident, w_q, sub_keys, hT, experts, gates, experts_s, gates_s):
    CHUNKS = D // CK
    NTL = len(TILES)
    SEG = 2 * PH
    MIN = -3.0e38
    w_view = w_q[0].rearrange("(k p) n -> p k n", p=P)
    with ExitStack() as ctx:
        m = Memory(nc, ctx, "route")
        w = m.sb("w", [P, 2, KD, CK])
        qrT = m.sb("qrT", [P, SEG, TOK])
        keys_n, keysT = m.sb("keys_n", [P, 2, P]), m.sb("keysT", [P, 2, P])
        sc = m.sb("sc", [P, 2, SEG, NKEYS])
        rest = m.sb("rest", [P, SEG, NKEYS])
        best = m.sb("best", [P, SEG, TOPK])
        besti = m.sb("besti", [P, SEG, TOPK], U32)
        bestf = m.sb("bestf", [P, SEG, TOPK])
        sums = m.sb("sums", [P, PH, TOPK * TOPK])
        sums2 = m.sb("sums2", [P, PH, TOPK * TOPK])
        picked = m.sb("picked", [P, PH, TOPK])
        pos = m.sb("pos", [P, SLOTS], U32)
        half = m.sb("half", [P, 2, SLOTS], U32)
        halff = m.sb("halff", [P, 2, SLOTS])
        iota_i = m.sb("iota_i", [P, TOPK], mybir.dt.int32)
        iota_f = m.sb("iota_f", [P, TOPK])
        onehot = m.sb("onehot", [P, SLOTS, TOPK])
        found = m.sb("found", [P, 2, SLOTS])
        row = m.sb("row", [P, SLOTS])
        gsum = m.sb("gsum", [P, 2, PH])
        acc = [m.ps(f"acc{j}", [P, 512]) for j in range(2)]
        acc_s = [m.ps(f"acc_s{j}", [P, 512]) for j in range(2)]
        psC = m.ps("psC", [P, SEG, NKEYS])
        keys_in, keys_turned, keys_set, iota_set = (m.sem(s) for s in ("keys_in", "keys_turned", "keys_set", "iota_set"))
        w_ready = [m.sem(f"w_ready{j}") for j in range(2)]
        acc_full = [m.sem(f"acc_full{j}") for j in range(2)]
        copied = [m.sem(f"copied{j}") for j in range(2)]
        scored, sc_copied, sc_used, chain_v, shifted, exped, s_turned, s_kept = (m.sem(s) for s in (
            "scored", "sc_copied", "sc_used", "chain", "shifted", "exped", "s_turned", "s_kept"))
        block = ctx.enter_context(nc.Block())

        @block.sync
        def _(sp):
            sp.dma_start(keys_n[:], sub_keys[0].rearrange("a k c -> k a c")).then_inc(keys_in, 16)

            def chunk_pair(i):
                for j in range(2):
                    if not isinstance(i, int):
                        sp.wait_ge(acc_full[0], 2 * i + j - 1)
                        sp.wait_ge(acc_full[1], 2 * i + j - 1)
                    sp.dma_start(w[:, j], w_view[:, :, ds((2 * i + j) * CK, CK)]).then_inc(w_ready[j], 16)

            repeat(sp, CHUNKS // 2, chunk_pair)

        @block.gpsimd
        def _(pool):
            nc.gpsimd.iota(iota_i[:], pattern=[[1, TOPK]], base=0, channel_multiplier=0).then_inc(iota_set, 1)

        @block.scalar
        def _(act):
            act.wait_ge(keys_turned, 1)
            nc.scalar.copy(keysT[:], psC[:, 0:2]).then_inc(keys_set, 1)

            def chunk_pair(i):
                for j in range(2):
                    for b in range(2):
                        block_at = 2 * (2 * i + j) + b
                        act.wait_ge(acc_full[b], 2 * i + j + 1)
                        nc.scalar.copy(qrT[:, ds(block_at, 1), 0:SEQ].rearrange("p a t -> p (a t)"), acc[b][:])\
                            .then_inc(copied[b], 1)
                        nc.scalar.copy(qrT[:, ds(block_at, 1), SEQ:TOK].rearrange("p a t -> p (a t)"),
                                       acc_s[b][:, 0:NS]).then_inc(copied[b], 1)

            repeat(act, CHUNKS // 2, chunk_pair)
            for t, (at, n) in enumerate(TILES):
                act.wait_ge(scored, t + 1)
                if t >= 2:
                    act.wait_ge(sc_used, t - 1)
                nc.scalar.copy(sc[0:n, t % 2], psC[0:n]).then_inc(sc_copied, 1)
                act.wait_ge(shifted, t + 1)
                g = gates[0:n, t]
                nc.scalar.activation(g, g, ACT.Exp).then_inc(exped, 1)

        @block.vector
        def _(dve):
            c = Chain(dve, chain_v)
            dve.wait_ge(iota_set, 1)
            c.link(nc.vector.tensor_copy(iota_f[:], iota_i[:]))

            def top16(n, values, left, top, index, segments):
                for lo in (0, 8):
                    src = left if lo else values
                    for s in range(segments):
                        last = nc.vector.max(top[0:n, s, lo:lo + 8], src[0:n, s])
                    c.link(last)
                    for s in range(segments):
                        last = nc.vector.max_index(index[0:n, s, lo:lo + 8], top[0:n, s, lo:lo + 8], src[0:n, s])
                        if not lo:
                            last = nc.vector.match_replace(left[0:n, s], top[0:n, s, 0:8], values[0:n, s], MIN)
                    c.link(last)

            for t, (at, n) in enumerate(TILES):
                dve.wait_ge(sc_copied, t + 1)
                top16(n, sc[:, t % 2], rest, best, besti, SEG)
                dve.sem_inc(sc_used, 1)
                c.link(nc.vector.tensor_copy(bestf[0:n], besti[0:n]))
                pair = best[0:n].rearrange("p (h a) k -> p h a k", a=2)
                shape = [n, PH, TOPK, TOPK]
                c.link(nc.vector.tensor_tensor(sums[0:n].rearrange("p h (a b) -> p h a b", a=TOPK),
                                               pair[:, :, 0].unsqueeze(3).to_broadcast(shape),
                                               pair[:, :, 1].unsqueeze(2).to_broadcast(shape), ALU.add))
                top16(n, sums, sums2, picked, pos[:].rearrange("p (h k) -> p h k", h=PH), PH)
                nc.vector.tensor_scalar(half[0:n, 0], pos[0:n], 4, None, ALU.logical_shift_right)
                c.link(nc.vector.tensor_scalar(half[0:n, 1], pos[0:n], TOPK - 1, None, ALU.bitwise_and))
                c.link(nc.vector.tensor_copy(halff[0:n], half[0:n]))
                listed = bestf[0:n].rearrange("p (h a) k -> p h a k", a=2)
                for a in range(2):
                    c.link(nc.vector.tensor_tensor(onehot[0:n], halff[0:n, a].unsqueeze(2).to_broadcast([n, SLOTS, TOPK]),
                                                   iota_f[0:n].unsqueeze(1).to_broadcast([n, SLOTS, TOPK]), ALU.is_equal))
                    hot = onehot[0:n].rearrange("p (h s) k -> p h s k", h=PH)
                    c.link(nc.vector.tensor_tensor(hot, hot, listed[:, :, a].unsqueeze(2).to_broadcast(shape), ALU.mult))
                    c.link(nc.vector.tensor_reduce(found[0:n, a], onehot[0:n], AX_X, ALU.add))
                c.link(nc.vector.scalar_tensor_tensor(row[0:n], found[0:n, 0], float(NKEYS), found[0:n, 1], ALU.mult, ALU.add))
                c.link(nc.vector.tensor_copy(experts[0:n, t], row[0:n]))
                g = gates[0:n, t].rearrange("p (h k) -> p h k", h=PH)
                nc.vector.tensor_tensor(g, picked[0:n], picked[0:n, :, 0:1].to_broadcast([n, PH, TOPK]), ALU.subtract)\
                    .then_inc(shifted, 1)
                dve.wait_ge(exped, t + 1)
                c.link(nc.vector.tensor_reduce(gsum[0:n, 0], g, AX_X, ALU.add))
                c.link(nc.vector.reciprocal(gsum[0:n, 1], gsum[0:n, 0]))
                c.link(nc.vector.tensor_tensor(g, g, gsum[0:n, 1].unsqueeze(2).to_broadcast([n, PH, TOPK]), ALU.mult))
            dve.sem_inc(sc_used, 1)
            dve.wait_ge(s_turned, 1)
            nc.vector.tensor_copy(experts_s[:], acc[0][:, 0:NS])
            nc.vector.tensor_copy(gates_s[:], acc[0][:, NS:2 * NS]).then_inc(s_kept, 1)

        @block.tensor
        def _(pe):
            pe.wait_ge(keys_in, 16)
            for a in range(2):
                last = nc.tensor.transpose(psC[:, a], keys_n[:, a], ident[:])
            last.then_inc(keys_turned, 1)

            def chunk_pair(i):
                for j in range(2):
                    pe.wait_ge(w_ready[j], 16 * i + 16)
                    for b in range(2):
                        after(pe, copied[b], 2 * (2 * i + j))
                        for k in range(KD):
                            nc.tensor.matmul(acc[b][:], w[:, j, k, b * P:(b + 1) * P], hT[:, k, 0:SEQ],
                                             start=(k == 0), stop=(k == KD - 1))
                            last = nc.tensor.matmul(acc_s[b][:, 0:NS], w[:, j, k, b * P:(b + 1) * P], hT[:, k, SEQ:TOK],
                                                    start=(k == 0), stop=(k == KD - 1))
                        last.then_inc(acc_full[b], 1)

            repeat(pe, CHUNKS // 2, chunk_pair)
            pe.wait_ge(keys_set, 1)
            for b in range(2):
                pe.wait_ge(copied[b], 2 * CHUNKS)
            for t, (at, n) in enumerate(TILES):
                if t:
                    pe.wait_ge(sc_copied, t)
                for s in range(SEG):
                    last = nc.tensor.matmul(psC[0:n, s], qrT[:, s, at:at + n], keysT[:, s % 2], start=True, stop=True)
                last.then_inc(scored, 1)
            pe.wait_ge(sc_used, NTL + 1)
            nc.tensor.transpose(acc[0][:, 0:NS], row[0:NS], ident[0:NS, 0:NS])
            nc.tensor.transpose(acc[0][:, NS:2 * NS], gates[0:NS, NT], ident[0:NS, 0:NS]).then_inc(s_turned, 1)


def expert_stage(nc, ident, mods_d, x1_d, h2_d, expert_u, expert_v, experts, gates, experts_s, gates_s, outs):
    R = 4
    U, V = expert_u[0], expert_v[0]
    N = 512
    ROUNDS = SLOTS // R
    BEFORE = NS // R
    with ExitStack() as ctx:
        m = Memory(nc, ctx, "exp")
        u = m.sb("u", [P, R, D])
        v = m.sb("v", [P, R, D])
        row_ids = m.sb("row_ids", [P, R, 1], U32)
        h2 = m.sb("h2", [P, 2, D])
        x1 = m.sb("x1", [P, D])
        gain_p, gain_s = m.sb("gain_p", [P, D]), m.sb("gain_s", [NS, D])
        y = m.sb("y", [P, D])
        dots = m.sb("dots", [P, R])
        act_d = m.sb("act_d", [P, R])
        wgt = m.sb("wgt", [P, R])
        diag = m.sb("diag", [P, R, P])
        col = m.sb("col", [P, NS, NS])
        zero = m.sb("zero", [P, N])
        stat = m.sb("stat", [P, 3])
        eps = m.sb("eps", [P, 1])
        acc = m.ps("acc", [P, D])
        const, h2_in, h2_in1, x1_in, gain_in, ids_set, zeroed = (m.sem(s) for s in (
            "const", "h2_in", "h2_in1", "x1_in", "gain_in", "ids_set", "zeroed"))
        u_in = [m.sem(f"u_in{j}") for j in range(R)]
        v_in = [m.sem(f"v_in{j}") for j in range(R)]
        dotted = [m.sem(f"dotted{j}") for j in range(R)]
        v_used = [m.sem(f"v_used{j}") for j in range(R)]
        weighted = [m.sem(f"weighted{j}") for j in range(R)]
        carrier, carrier_v = m.sem("carrier"), m.sem("carrier_v")
        chain_a, chain_v, tile_dotted, acc_full, squared, rooted, y_done, stored = (m.sem(s) for s in (
            "chain_a", "chain_v", "tile_dotted", "acc_full", "squared", "rooted", "y_done", "stored"))
        block = ctx.enter_context(nc.Block())
        y_out = outs[0][0].rearrange("(t p) d -> p t d", p=P)
        x1_tiles = x1_d[0:SEQ, :].rearrange("(t p) d -> p t d", p=P)
        h2_tiles = h2_d[0:SEQ, :].rearrange("(t p) d -> p t d", p=P)
        flat = lambda ap: ap.rearrange("p a d -> p (a d)")

        @block.sync
        def _(sp):
            sp.dma_start(x1[0:NS], x1_d[SEQ:TOK, :]).then_inc(x1_in, 16)
            sp.dma_start(gain_s[:], mods_d[0:NS, GT2, :]).then_inc(gain_in, 16)
            sp.dma_start(gain_p[:], bcast(mods_d[NS:ROWS, GT2, :], P)).then_inc(gain_in, 16)
            for b in range(NS):
                if b >= 2:
                    sp.wait_ge(dotted[(b - 2) % R], (b - 2) // R + 2)
                sp.dma_start(h2[:, b % 2], bcast(h2_d[SEQ + b:SEQ + b + 1, :], P)).then_inc((h2_in, h2_in1)[b % 2], 16)
            sp.wait_ge(tile_dotted, 1)
            sp.wait_ge(y_done, 1)
            sp.dma_start(outs[1].rearrange("b s d -> (b s) d"), y[0:NS]).then_inc(stored, 16)

            def tile(t):
                sp.wait_ge(tile_dotted, t + 1)
                sp.dma_start(h2[:, 0], flat(h2_tiles[:, ds(t, 1)])).then_inc(h2_in, 16)
                sp.wait_ge(y_done, t + 1)
                sp.dma_start(x1[:], flat(x1_tiles[:, ds(t, 1)])).then_inc(x1_in, 16)
                sp.wait_ge(y_done, t + 2)
                sp.dma_start(flat(y_out[:, ds(t, 1)]), y[:]).then_inc(stored, 16)

            with sp.Fori(0, NT) as t:
                tile(t)
            sp.wait_ge(stored, 16 * (NT + 1))

        @block.gpsimd
        def _(pool):
            nc.gpsimd.memset(eps[:], EPS).then_inc(const, 1)
            nc.gpsimd.memset(zero[:], 0.0).then_inc(const, 1)
            nc.gpsimd.memset(col[:], 0.0).then_inc(const, 1)

            def gather(j, ids):
                at = bass.IndirectOffsetOnAxis(ap=ids, axis=0)
                pool.indirect_dma_start(u[:, j], None, U, at).then_inc(u_in[j], 16)
                pool.indirect_dma_start(v[:, j], None, V, at).then_inc(v_in[j], 16)

            for b in range(NS):
                if b >= R:
                    pool.wait_ge(dotted[b % R], b // R + 1)
                    pool.wait_ge(v_used[b % R], b // R + 1)
                gather(b % R, experts_s[:, b:b + 1])
            with pool.Fori(0, NT) as t:
                with pool.Fori(0, ROUNDS) as i:
                    for j in range(R):
                        n = ROUNDS * t + i
                        pool.wait_ge(dotted[j], n + BEFORE + 1)
                        pool.wait_ge(v_used[j], n + BEFORE + 1)
                        nc.gpsimd.tensor_copy(row_ids[:, j], experts[:, ds(t, 1), ds(R * i + j, 1)]
                                              .rearrange("p a s -> p (a s)")).then_inc(ids_set, 1)
                        pool.wait_ge(ids_set, R * n + j + 1)
                        pool.sem_inc(carrier, 1)
                        gather(j, row_ids[:, j])

        @block.vector
        def _(dve):
            for j in range(R):
                dve.sem_inc(dotted[j], 1)

            def dot(j, h2_rows, times):
                dve.wait_ge(u_in[j], 16 * times)
                nc.vector.tensor_tensor_reduce(u[:, j], u[:, j], h2_rows, 1.0, 0.0, ALU.mult, ALU.add,
                                               dots[:, j:j + 1]).then_inc(dotted[j], 1)

            for b in range(NS):
                dve.wait_ge((h2_in, h2_in1)[b % 2], 16 * (b // 2 + 1))
                dot(b % R, h2[:, b % 2], b // R + 1)
            for j in range(R):
                dve.wait_ge(dotted[j], BEFORE + 1)
            dve.sem_inc(tile_dotted, 1)

            def finish_tile(n, gain, t):
                c = Chain(dve, chain_v, 2 * t)
                dve.wait_ge(rooted, t + 1)
                c.link(nc.vector.reciprocal(stat[0:n, 2:3], stat[0:n, 1:2]))
                dve.wait_ge(x1_in, 16 * t + 16)
                c.link(nc.vector.scalar_tensor_tensor(y[0:n], y[0:n], stat[0:n, 2:3], gain[0:n], ALU.mult, ALU.mult))
                nc.vector.tensor_tensor(y[0:n], y[0:n], x1[0:n], ALU.add).then_inc(y_done, 1)

            dve.wait_ge(gain_in, 32)
            finish_tile(NS, gain_s, 0)
            with dve.Fori(0, NT) as t:
                dve.wait_ge(h2_in, 16 * t + 16 * (NS // 2 + 1))
                dve.sem_inc(carrier_v, 1)
                with dve.Fori(0, ROUNDS) as i:
                    for j in range(R):
                        dot(j, h2[:, 0], ROUNDS * t + i + BEFORE + 1)
                for j in range(R):
                    dve.wait_ge(dotted[j], ROUNDS * t + ROUNDS + BEFORE + 1)
                dve.sem_inc(tile_dotted, 1)
                finish_tile(P, gain_p, t + 1)

        @block.scalar
        def _(act):
            def weigh(j, times, gate, out, count):
                act.wait_ge(dotted[j], times + 1)
                nc.scalar.activation(act_d[:, j:j + 1], dots[:, j:j + 1], ACT.Gelu_apprx_tanh).then_inc(chain_a, 1)
                act.wait_ge(chain_a, count + 1)
                if out is None:
                    nc.scalar.activation(wgt[:, j:j + 1], act_d[:, j:j + 1], ACT.Copy, scale=gate).then_inc(chain_a, 1)
                    act.wait_ge(chain_a, count + 2)
                    nc.scalar.activation(diag[:, j], ident[:], ACT.Copy, scale=wgt[:, j:j + 1]).then_inc(weighted[j], 1)
                else:
                    nc.scalar.activation(out, act_d[:, j:j + 1], ACT.Copy, scale=gate).then_inc(weighted[j], 1)

            def norm(n, t):
                act.wait_ge(acc_full, t + 1)
                if not isinstance(t, int):
                    act.wait_ge(stored, 16 * t)
                nc.scalar.copy(y[0:n], acc[0:n]).then_inc(squared, 1)
                nc.scalar.activation(acc[0:n], acc[0:n], ACT.Square, accum_out=stat[0:n, 0:1]).then_inc(squared, 1)
                act.wait_ge(squared, 2 * t + 2)
                nc.scalar.activation(stat[0:n, 1:2], stat[0:n, 0:1], ACT.Sqrt, bias=eps[0:n], scale=1.0 / D)\
                    .then_inc(rooted, 1)

            act.wait_ge(const, 3)
            for b in range(NS):
                weigh(b % R, b // R + 1, gates_s[:, b:b + 1], col[:, b, b:b + 1], b)
            norm(NS, 0)
            with act.Fori(0, NT) as t:
                with act.Fori(0, ROUNDS) as i:
                    for j in range(R):
                        n = ROUNDS * t + i
                        gate = gates[:, ds(t, 1), ds(R * i + j, 1)].rearrange("p a s -> p (a s)")
                        weigh(j, n + BEFORE + 1, gate, None, 2 * R * n + 2 * j + NS)
                norm(P, t + 1)

        @block.tensor
        def _(pe):
            for j in range(R):
                pe.sem_inc(v_used[j], 1)
            pe.wait_ge(const, 3)
            for b in range(NS):
                pe.wait_ge(weighted[b % R], b // R + 1)
                pe.wait_ge(v_in[b % R], 16 * (b // R + 1))
                for c in range(D // N):
                    last = nc.tensor.matmul(acc[0:NS, c * N:(c + 1) * N], col[:, b], v[:, b % R, c * N:(c + 1) * N],
                                            start=(b == 0), stop=(b == NS - 1))
                last.then_inc(v_used[b % R], 1)
            for j in range(R):
                pe.wait_ge(v_used[j], BEFORE + 1)
            pe.sem_inc(acc_full, 1)
            with pe.Fori(0, NT) as t:
                pe.wait_ge(rooted, t + 1)
                for c in range(D // N):
                    nc.tensor.matmul(acc[:, c * N:(c + 1) * N], zero[:, 0:P], zero[:], start=True, stop=False)
                with pe.Fori(0, ROUNDS) as i:
                    for j in range(R):
                        n = ROUNDS * t + i
                        pe.wait_ge(weighted[j], n + BEFORE + 1)
                        pe.wait_ge(v_in[j], 16 * n + 16 * (BEFORE + 1))
                        for c in range(D // N):
                            last = nc.tensor.matmul(acc[:, c * N:(c + 1) * N], diag[:, j], v[:, j, c * N:(c + 1) * N],
                                                    start=False, stop=False)
                        last.then_inc(v_used[j], 1)
                for c in range(D // N):
                    last = nc.tensor.matmul(acc[:, c * N:(c + 1) * N], zero[:, 0:P], zero[:], start=False, stop=True)
                last.then_inc(acc_full, 1)


def program(nc, x_prompt, x_sample, c_prompt, c_sample, cache1, cache4, cache16, w_ada, b_ada, norm_g, w_in,
            gm_ln_g, gm_ln_b, w_s, b_s, w_out, w_q, sub_keys, expert_u, expert_v, outs):
    scratch = lambda name, shape: nc.dram_tensor(name, shape, F32, kind="Internal").ap()
    mods_d = scratch("mods_d", (ROWS, 6, D))
    proj_d = scratch("proj_d", (TOK, WIN))
    mix_d = scratch("mix_d", (TOK, D))
    x1_d = scratch("x1_d", (TOK, D))
    h2_d = scratch("h2_d", (TOK, D))
    with ExitStack() as ctx:
        ident = ctx.enter_context(nc.sbuf_tensor("ident", [P, P], F32))
        ident_made = ctx.enter_context(nc.semaphore("ident_made"))
        modulation_stage(nc, ident, ident_made, c_prompt, c_sample, w_ada, b_ada, norm_g, mods_d)
        projection_stage(nc, ident, x_prompt, x_sample, mods_d, w_in, proj_d)
        mixer_stage(nc, ident, proj_d, (cache1, cache4, cache16), gm_ln_g, gm_ln_b, w_s, b_s, mix_d, outs)
        NTL = len(TILES)
        buffer = lambda name, shape, dt=F32: ctx.enter_context(nc.sbuf_tensor(name, shape, dt))
        experts, gates = buffer("experts", [P, NTL, SLOTS], U32), buffer("gates", [P, NTL, SLOTS])
        experts_s, gates_s = buffer("experts_s", [P, NS], U32), buffer("gates_s", [P, NS])
        with nc.sbuf_tensor("hT", [P, KD, TOK], F32) as hT:
            output_stage(nc, ident, x_prompt, x_sample, mods_d, w_out, mix_d, hT, x1_d, h2_d)
            routing_stage(nc, ident, w_q, sub_keys, hT, experts, gates, experts_s, gates_s)
        expert_stage(nc, ident, mods_d, x1_d, h2_d, expert_u, expert_v, experts, gates, experts_s, gates_s, outs)


_INS = ['x_prompt', 'x_sample', 'c_prompt', 'c_sample', 'cache_kv_dil1', 'cache_kv_dil4', 'cache_kv_dil16', 'w_ada',
        'b_ada', 'norm_g', 'w_in', 'gm_ln_g', 'gm_ln_b', 'w_s', 'b_s', 'w_out', 'w_q', 'sub_keys', 'expert_u', 'expert_v']
_OUTS = [(1, SEQ, D), (NS, 1, D)] + [(1, 1, min(w, SEQ), 2, HEADS, HD) for w, _ in WINDOWS] \
    + [(1, NS, 1, 2, HEADS, HD)] * 3 + [(1, NS, 1, GM_HEADS, GM // GM_HEADS)]


def kernel(**inputs):
    import concourse.bacc as _bacc
    from concourse.bass_utils import run_bass_kernel_spmd as _run

    nc = _bacc.Bacc("TRN2", target_bir_lowering=False, num_devices=1)
    arrays, args = {}, []
    for name in _INS:
        a = np.ascontiguousarray(inputs[name])
        arrays[f"in_{name}_dram"] = a
        args.append(nc.dram_tensor(f"in_{name}_dram", a.shape, mybir.dt.from_np(a.dtype), kind="ExternalInput").ap())
    outs = [nc.dram_tensor(f"out_{i}_dram", shape, F32, kind="ExternalOutput").ap() for i, shape in enumerate(_OUTS)]
    program(nc, *args, outs)
    r = _run(nc, [arrays], core_ids=[0])
    return tuple(r.results[0][f"out_{i}_dram"] for i in range(len(_OUTS)))
```

```python
from contextlib import ExitStack

import numpy as np

import concourse.bass as bass
from concourse import mybir

ALU = mybir.AluOpType
ACT = mybir.ActivationFunctionType
F32 = mybir.dt.float32
U32 = mybir.dt.uint32
AX_X = mybir.AxisListType.X
ds = bass.ds

P = 128
D = 2048
KD = D // P
SEQ = 512
NT = SEQ // P
NS = 8
TOK = SEQ + NS
FIRST = ((0, P, 0), (SEQ, NS, P))
SECOND = tuple((t * P, P, (t - 1) * P) for t in range(1, NT))
ROWS = NS + 1
HD, HEADS, GROUPS = 64, 8, 3
GW = HEADS * HD
ATT = GROUPS * GW
GM_HEADS, GM = 4, 512
WIN = 3 * ATT + 2 * GM
WINDOWS = ((128, 1), (512, 4), (2048, 16))
REACH = 128
PH, TOPK, NKEYS = 8, 16, 128
SLOTS = PH * TOPK
CK = 256
R = 4
ROUNDS = SLOTS // R
EPS = 1e-6
NEG = -1e30
SH1, SC1, GT1, SH2, SC2, GT2 = range(6)


class Stage:

    def __init__(self, nc, name):
        self.nc, self.name, self.ctx, self.sems = nc, name, ExitStack(), []

    def __enter__(self):
        return self

    def __exit__(self, *failure):
        if failure[0] is None:
            self.ctx.close()
            self.nc.clear_and_free_semaphores(self.sems)
            self.nc.all_engine_barrier()

    def sb(self, name, shape, dt=F32):
        return self.ctx.enter_context(self.nc.sbuf_tensor(f"{self.name}_{name}", shape, dt))

    def ps(self, name, shape, dt=F32):
        return self.ctx.enter_context(self.nc.psum_tensor(f"{self.name}_{name}", shape, dt))

    def sem(self, name):
        self.sems.append(self.nc.alloc_semaphore(f"{self.name}_{name}"))
        return self.sems[-1]

    def pair(self, name):
        return [self.sem(f"{name}{j}") for j in range(2)]

    def block(self):
        return self.ctx.enter_context(self.nc.Block())


class Chain:

    def __init__(self, eng, sem, base=0):
        self.eng, self.sem, self.base, self.n = eng, sem, base, 0

    def link(self, ins):
        ins.then_inc(self.sem, 1)
        self.n += 1
        self.eng.wait_ge(self.sem, self.base + self.n)


def repeat(eng, count, body):
    body(0)
    if count > 1:
        with eng.Fori(1, count) as i:
            body(i)


def after(eng, sem, value):
    if not isinstance(value, int) or value > 0:
        eng.wait_ge(sem, value)


def flat(ap):
    return ap.rearrange("p a d -> p (a d)")


def of_tile(buffer, t, cols):
    return flat(buffer[:, ds(t, 1), cols])


def identity(nc, pool, ident, made):
    nc.gpsimd.memset(ident[:], 0.0).then_inc(made, 1)
    pool.wait_ge(made, 1)
    nc.gpsimd.affine_select(out=ident[:], in_=ident[:], compare_op=ALU.not_equal, fill=1.0, base=0,
                            pattern=[[-1, P]], channel_multiplier=1).then_inc(made, 1)


def modulation_stage(nc, ident, ident_made, c_prompt, c_sample, w_ada, b_ada, norm_g, mods_d):
    N = 512
    CHUNKS = 6 * D // N
    w_view = w_ada[0].rearrange("(k p) n -> p k n", p=P)
    b_row = b_ada[0:1, :]
    with Stage(nc, "ada") as m:
        cond = m.sb("cond", [ROWS, D])
        act_c = m.sb("act_c", [ROWS, D])
        condT = m.sb("condT", [P, KD, ROWS])
        w = m.sb("w", [P, 2, KD, N])
        bias = m.sb("bias", [ROWS, 2, N])
        gains = m.sb("gains", [ROWS, 4, D])
        mods = m.sb("mods", [ROWS, 6, D])
        mods_flat = mods[:].rearrange("r s n -> r (s n)")
        psT = m.ps("psT", [P, KD, ROWS])
        acc = [m.ps(f"acc{j}", [P, N]) for j in range(2)]
        c_in, g_in = m.sem("c_in"), m.sem("g_in")
        silu_done, turned, condT_ready = m.sem("silu_done"), m.sem("turned"), m.sem("condT_ready")
        w_in = [m.sem(f"w_in{j}") for j in range(2)]
        bias_in = [m.sem(f"bias_in{j}") for j in range(2)]
        chunk_done = [m.sem(f"chunk_done{j}") for j in range(2)]
        biased = [m.sem(f"biased{j}") for j in range(2)]
        folded, stored = m.sem("folded"), m.sem("stored")
        block = m.block()

        @block.sync
        def _(sp):
            sp.dma_start(cond[0:NS, :], c_sample[:, :]).then_inc(c_in, 16)
            sp.dma_start(cond[NS:ROWS, :], c_prompt[:, :]).then_inc(c_in, 16)
            def chunk_pair(i):
                for j in range(2):
                    after(sp, chunk_done[j], i)
                    sp.dma_start(w[:, j], w_view[:, :, ds((2 * i + j) * N, N)]).then_inc(w_in[j], 16)
                    after(sp, biased[j], i)
                    sp.dma_start(bias[:, j], bcast(b_row[:, ds((2 * i + j) * N, N)], ROWS)).then_inc(bias_in[j], 16)

            repeat(sp, CHUNKS // 2, chunk_pair)
            sp.wait_ge(folded, 4)
            sp.dma_start(mods_d.rearrange("r s n -> r (s n)"), mods_flat).then_inc(stored, 16)
            sp.wait_ge(stored, 16)

        @block.gpsimd
        def _(pool):
            pool.dma_start(gains[:].rearrange("r s n -> r (s n)"),
                           bcast(norm_g.rearrange("a s n -> a (s n)"), ROWS)).then_inc(g_in, 16)
            identity(nc, pool, ident, ident_made)

        @block.scalar
        def _(act):
            act.wait_ge(c_in, 32)
            nc.scalar.activation(act_c[:], cond[:], ACT.Silu).then_inc(silu_done, 1)

        @block.tensor
        def _(pe):
            pe.wait_ge(ident_made, 2)
            pe.wait_ge(silu_done, 1)
            for k in range(KD):
                last = nc.tensor.transpose(psT[:, k, :], act_c[:, k * P:(k + 1) * P], ident[0:ROWS, 0:ROWS])
            last.then_inc(turned, 1)
            pe.wait_ge(condT_ready, 1)
            def chunk_pair(i):
                for j in range(2):
                    pe.wait_ge(w_in[j], 16 * i + 16)
                    after(pe, biased[j], i)
                    for k in range(KD):
                        last = nc.tensor.matmul(acc[j][0:ROWS, :], condT[:, k, :], w[:, j, k, :],
                                                start=(k == 0), stop=(k == KD - 1))
                    last.then_inc(chunk_done[j], 1)

            repeat(pe, CHUNKS // 2, chunk_pair)
        @block.vector
        def _(dve):
            dve.wait_ge(turned, 1)
            nc.vector.tensor_copy(condT[:], psT[:]).then_inc(condT_ready, 1)
            def chunk_pair(i):
                for j in range(2):
                    dve.wait_ge(chunk_done[j], i + 1)
                    dve.wait_ge(bias_in[j], 16 * i + 16)
                    nc.vector.tensor_tensor(mods_flat[:, ds((2 * i + j) * N, N)], acc[j][0:ROWS, :], bias[:, j],
                                            ALU.add).then_inc(biased[j], 1)

            repeat(dve, CHUNKS // 2, chunk_pair)
            dve.wait_ge(g_in, 16)
            for j in range(2):
                dve.wait_ge(biased[j], CHUNKS // 2)
            for scale, g in ((SC1, 0), (SC2, 2)):
                nc.vector.scalar_tensor_tensor(mods[:, scale], mods[:, scale], 1.0, gains[:, g], ALU.add,
                                               ALU.mult).then_inc(folded, 1)
            for gate, g in ((GT1, 1), (GT2, 3)):
                nc.vector.tensor_tensor(mods[:, gate], mods[:, gate], gains[:, g], ALU.mult).then_inc(folded, 1)


def bcast(row, n):
    return row.to_broadcast([n, row.shape[1]])


def load_mods(eng, mods_d, section, vectors, landed):
    eng.dma_start(vectors[0][:], bcast(mods_d[NS:ROWS, section, :], P)).then_inc(landed, 16)
    for v in vectors[1:]:
        eng.dma_start(v[:], mods_d[0:NS, section, :]).then_inc(landed, 16)


def turn(nc, pe, src, n, psT, ident, psT_free, turned, done):
    for q in range(4):
        if done + q >= 3:
            pe.wait_ge(psT_free, done + q - 2)
        for b in range(4):
            k = 4 * q + b
            last = nc.tensor.transpose(psT[:, (done + q) % 3, b, 0:n], src[0:n, k * P:(k + 1) * P], ident[0:n, 0:n])
        last.then_inc(turned, 1)


def width(tiles):
    return sum(n for _, n, _ in tiles)


def rows_of(tiles, prompt, sample):
    return [prompt[at:at + n, :] if at < SEQ else sample for at, n, _ in tiles]


def projection_stage(nc, name, tiles, ident, x_prompt, x_sample, mods_d, w_in, proj_d, slots=None, base=0):
    CHUNKS = WIN // CK
    NTL = len(tiles)
    w_view = w_in[0].rearrange("(k p) n -> p k n", p=P)
    x_rows = rows_of(tiles, x_prompt[0], x_sample.rearrange("b s d -> (b s) d"))
    proj_rows = rows_of(tiles, proj_d, proj_d[SEQ:TOK, :])
    with Stage(nc, name) as m:
        x = m.sb("x", [P, 2, D])
        sq = m.sb("sq", [P, D])
        kinds = [P, NS] if tiles[-1][1] == NS else [P]
        scale = [m.sb(f"scale{n}", [n, D]) for n in kinds]
        shift = [m.sb(f"shift{n}", [n, D]) for n in kinds]
        stat = m.sb("stat", [P, 3, NTL])
        eps = m.sb("eps", [P, 1])
        hT = m.sb("hT", [P, KD, width(tiles)])
        w = m.sb("w", [P, 2, KD, CK])
        out = m.sb("out", [P, 2, NTL, CK])
        psT = m.ps("psT", [P, 3, 4, P])
        acc = [m.ps(f"acc{t}", [P, 512]) for t in range(NTL)]
        mod_in, eps_set, squared, rooted, inverse, scaled, shifted, turned, psT_free = (m.sem(s) for s in (
            "mod_in", "eps_set", "squared", "rooted", "inverse", "scaled", "shifted", "turned", "psT_free"))
        x_in, w_ready, acc_full, out_full, stored = (m.pair(s) for s in ("x_in", "w_ready", "acc_full", "out_full", "stored"))
        block = m.block()

        @block.sync
        def _(sp):
            for t, (at, n, _) in enumerate(tiles):
                if t >= 2:
                    sp.wait_ge(turned, 4 * (t - 1))
                sp.dma_start(x[0:n, t % 2], x_rows[t]).then_inc(x_in[t % 2], 16)
                if t == 0:
                    for section, vectors in ((SC1, scale), (SH1, shift)):
                        load_mods(sp, mods_d, section, vectors, mod_in)

            def load(j, c):
                sp.dma_start(w[:, j], w_view[:, :, ds(c * CK, CK)]).then_inc(w_ready[j], 16)

            def store(j, i):
                sp.wait_ge(out_full[j], NTL * i + NTL)
                for t, (at, n, _) in enumerate(tiles):
                    sp.dma_start(proj_rows[t][:, ds((2 * i + j) * CK, CK)], out[0:n, j, t]).then_inc(stored[j], 16)

            load(0, 0)
            load(1, 1)
            with sp.Fori(0, CHUNKS // 2 - 1) as i:
                for j in range(2):
                    sp.wait_ge(acc_full[j], NTL * i + NTL)
                    load(j, 2 * i + j + 2)
                    store(j, i)
            for j in range(2):
                store(j, CHUNKS // 2 - 1)
            for j in range(2):
                sp.wait_ge(stored[j], 16 * NTL * CHUNKS // 2)

        @block.gpsimd
        def _(pool):
            nc.gpsimd.memset(eps[:], EPS).then_inc(eps_set, 1)
            if slots:
                repeat(pool, CHUNKS // 2, lambda i: slots.gather_round(pool, 0, base + i))

        @block.scalar
        def _(act):
            act.wait_ge(eps_set, 1)
            for t, (at, n, c) in enumerate(tiles):
                act.wait_ge(x_in[t % 2], 16 * (t // 2 + 1))
                if t:
                    act.wait_ge(squared, t)
                nc.scalar.activation(sq[0:n, :], x[0:n, t % 2], ACT.Square,
                                     accum_out=stat[0:n, 0, t:t + 1]).then_inc(squared, 1)
                act.wait_ge(squared, t + 1)
                nc.scalar.activation(stat[0:n, 1, t:t + 1], stat[0:n, 0, t:t + 1], ACT.Sqrt, bias=eps[0:n, :],
                                     scale=1.0 / D).then_inc(rooted, 1)
                for q in range(4):
                    act.wait_ge(turned, 4 * t + q + 1)
                    nc.scalar.copy(hT[:, 4 * q:4 * q + 4, c:c + n], psT[:, (4 * t + q) % 3, :, 0:n])\
                        .then_inc(psT_free, 1)

            def chunk_pair(i):
                for j in range(2):
                    if slots:
                        slots.weigh(act, base + i, 2 * j)
                        slots.weigh(act, base + i, 2 * j + 1)
                    after(act, stored[j], 16 * NTL * i)
                    for t, (at, n, _) in enumerate(tiles):
                        act.wait_ge(acc_full[j], NTL * i + t + 1)
                        nc.scalar.copy(out[0:n, j, t], acc[t][0:n, 0:CK]).then_inc(out_full[j], 1)

            repeat(act, CHUNKS // 2, chunk_pair)

        @block.vector
        def _(dve):
            for t, (at, n, _) in enumerate(tiles):
                dve.wait_ge(rooted, t + 1)
                nc.vector.reciprocal(stat[0:n, 2, t:t + 1], stat[0:n, 1, t:t + 1]).then_inc(inverse, 1)
                dve.wait_ge(inverse, t + 1)
                if t == 0:
                    dve.wait_ge(mod_in, 32 * len(scale))
                xt = x[0:n, t % 2]
                s = len(scale) - 1 if n == NS else 0
                nc.vector.scalar_tensor_tensor(xt, xt, stat[0:n, 2, t:t + 1], scale[s][0:n, :], ALU.mult,
                                               ALU.mult).then_inc(scaled, 1)
                dve.wait_ge(scaled, t + 1)
                nc.vector.tensor_tensor(xt, xt, shift[s][0:n, :], ALU.add).then_inc(shifted, 1)
            if slots:
                repeat(dve, CHUNKS // 2, lambda i: slots.sum_round(dve, base + i))

        @block.tensor
        def _(pe):
            for t, (at, n, _) in enumerate(tiles):
                pe.wait_ge(shifted, t + 1)
                turn(nc, pe, x[:, t % 2], n, psT, ident, psT_free, turned, 4 * t)
            pe.wait_ge(psT_free, 4 * NTL)

            def chunk_pair(i):
                for j in range(2):
                    pe.wait_ge(w_ready[j], 16 * i + 16)
                    after(pe, out_full[1 - j], NTL * (i + j))
                    for t, (at, n, c) in enumerate(tiles):
                        for k in range(KD):
                            last = nc.tensor.matmul(acc[t][0:n, 0:CK], hT[:, k, c:c + n], w[:, j, k, :],
                                                    start=(k == 0), stop=(k == KD - 1))
                        last.then_inc(acc_full[j], 1)

            repeat(pe, CHUNKS // 2, chunk_pair)


class Slots:

    def __init__(self, ctx, nc, ident, expert_u, expert_v, experts, gates, h2_d):
        self.nc, self.ident, self.experts, self.gates, self.h2_d = nc, ident, experts, gates, h2_d
        buffer = lambda name, shape, dt=F32: ctx.enter_context(nc.sbuf_tensor(f"slots_{name}", shape, dt))
        semaphore = lambda name: nc.alloc_semaphore(f"slots_{name}")
        self.U, self.V = expert_u[0], expert_v[0]
        self.u, self.v = buffer("u", [P, R, D]), buffer("v", [P, R, D])
        self.h2, self.sum = buffer("h2", [P, D]), buffer("sum", [P, D])
        self.row_ids = buffer("row_ids", [P, R, 1], U32)
        self.dots, self.gelu, self.weight = (buffer(s, [P, R]) for s in ("dots", "gelu", "weight"))
        each = lambda s: [semaphore(f"{s}{j}") for j in range(R)]
        self.u_in, self.v_in, self.weighted = each("u_in"), each("v_in"), each("weighted")
        self.dotted, self.v_used = each("dotted"), each("v_used")
        self.ids_set, self.carrier, self.gelued, self.h2_in = (semaphore(s) for s in ("ids_set", "carrier", "gelued", "h2_in"))

    def start(self):
        nc = self.nc
        with Stage(nc, "start") as m:
            block = m.block()
            zeroed = m.sem("zeroed")

            @block.sync
            def _(sp):
                sp.dma_start(self.h2[:], self.h2_d[0:P, :]).then_inc(self.h2_in, 16)
                sp.wait_ge(self.h2_in, 16)

            @block.vector
            def _(dve):
                nc.vector.memset(self.sum[:], 0.0).then_inc(zeroed, 1)
                dve.wait_ge(zeroed, 1)
                for j in range(R):
                    dve.sem_inc(self.dotted[j], 1)
                    dve.sem_inc(self.v_used[j], 1)

    def gather(self, pool, j, ids):
        at = bass.IndirectOffsetOnAxis(ap=ids, axis=0)
        pool.indirect_dma_start(self.u[:, j], None, self.U, at).then_inc(self.u_in[j], 16)
        pool.indirect_dma_start(self.v[:, j], None, self.V, at).then_inc(self.v_in[j], 16)

    def gather_round(self, pool, t, i):
        n = ROUNDS * t + i
        for j in range(R):
            pool.wait_ge(self.dotted[j], n + 1)
            pool.wait_ge(self.v_used[j], n + 1)
            self.nc.gpsimd.tensor_copy(self.row_ids[:, j], self.experts[:, t, ds(R * i + j, 1)])\
                .then_inc(self.ids_set, 1)
            pool.wait_ge(self.ids_set, R * n + j + 1)
            pool.sem_inc(self.carrier, 1)
            self.gather(pool, j, self.row_ids[:, j])

    def dot(self, dve, n, j, h2):
        dve.wait_ge(self.u_in[j], 16 * n + 16)
        u = self.u[:, j]
        self.nc.vector.tensor_tensor_reduce(u, u, h2, 1.0, 0.0, ALU.mult, ALU.add, self.dots[:, j:j + 1])\
            .then_inc(self.dotted[j], 1)

    def activate(self, act, n, j):
        act.wait_ge(self.dotted[j], n + 2)
        self.nc.scalar.activation(self.gelu[:, j:j + 1], self.dots[:, j:j + 1], ACT.Gelu_apprx_tanh)\
            .then_inc(self.gelued, 1)
        act.wait_ge(self.gelued, R * n + j + 1)

    def weigh(self, act, n, j):
        self.activate(act, n, j)
        self.nc.scalar.activation(self.weight[:, j:j + 1], self.gelu[:, j:j + 1], ACT.Copy,
                                  scale=self.gates[:, 0, ds(R * n + j, 1)]).then_inc(self.weighted[j], 1)

    def add(self, dve, n, j):
        dve.wait_ge(self.weighted[j], n + 1)
        dve.wait_ge(self.v_in[j], 16 * n + 16)
        dve.wait_ge(self.v_used[j - 1], n + 2 if j else n + 1)
        self.nc.vector.scalar_tensor_tensor(self.sum[:], self.v[:, j], self.weight[:, j:j + 1], self.sum[:],
                                            ALU.mult, ALU.add).then_inc(self.v_used[j], 1)

    def sum_round(self, dve, n):
        self.dot(dve, n, 0, self.h2[:])
        for j in range(R):
            if j + 1 < R:
                self.dot(dve, n, j + 1, self.h2[:])
            self.add(dve, n, j)


def mixer_stage(nc, name, tiles, F, ident, proj_d, cache, gm_ln_g, gm_ln_b, w_s, b_s, mix_d, outs, slots=None, base=0):
    at_prompt = tiles[0][0]
    fold = proj_d[0:F * P, :].rearrange("(i r) c -> i r c", r=F)
    mix_fold = mix_d[0:F * P, :].rearrange("(i r) c -> i r c", r=F)
    samples = tiles[-1][1] == NS
    FROM = at_prompt // F
    BLOCKS, NEAR = F + 2, F * P
    KEYS = BLOCKS * P
    PAIRS = GW // P
    NQ, NK = GROUPS * PAIRS, (GROUPS - 1) * PAIRS
    TURNS = (NQ + NK) // 4
    SCALE = HD ** -0.5
    LINKS = 5
    K_LOADS, V_LOADS = 16 * (GROUPS + 3), 16 * (GROUPS + 1)
    V0 = 2 * ATT
    NTL = len(tiles)
    PROMPTS = NTL - samples
    round_of = lambda r, h: HEADS // R * r + (base + h // R)
    lag = lambda h: (2, 2, 5)[h] if h < 3 else 3
    with Stage(nc, name) as m:
        k0n = m.sb("k0n", [P, F, GW])
        v = m.sb("v", [P, F, ATT])
        qkn = m.sb("qkn", [P, (NQ + NK) * P])
        kT0 = m.sb("kT0", [P, PAIRS, F, P])
        qkT = m.sb("qkT", [P, NQ + NK, P])
        near, far = m.sb("near", [P, F, F, P]), m.sb("far", [P, F, 2, P])
        steps = m.sb("steps", [P, 3, P], mybir.dt.int32)
        off = m.sb("off", [P, 2, P])
        scores = m.sb("scores", [P, 3, KEYS])
        probsT = m.sb("probsT", [P, 2, BLOCKS, P])
        top, den, inv = m.sb("top", [P, HEADS]), m.sb("den", [P, HEADS]), m.sb("inv", [P, HEADS])
        att = m.sb("att", [P, GROUPS, HEADS, HD])
        gin = m.sb("gin", [P, 2, 2 * GM])
        gsq = m.sb("gsq", [P, GM])
        gst = m.sb("gst", [P, 3, GM_HEADS])
        gain, shift = m.sb("gain", [P, GM]), m.sb("shift", [P, GM])
        wn, wT = m.sb("wn", [P, GM_HEADS, P]), m.sb("wT", [P, GM_HEADS, P])
        bn, bT = m.sb("bn", [GM_HEADS, P]), m.sb("bT", [P, GM_HEADS])
        w00, b00 = m.sb("w00", [NS, GM_HEADS, 1]), m.sb("b00", [NS, GM_HEADS, 1])
        gout = m.sb("gout", [P, GM])
        eps = m.sb("eps", [P, 1])
        if samples:
            k_s, v_s = m.sb("k_s", [P, 2, GROUPS, GW]), m.sb("v_s", [P, 2, GROUPS, GW])
            qb = m.sb("qb", [P, 2, ATT])
            own = m.sb("own", [HEADS, 2, 3, GROUPS, HD])
            prod = m.sb("prod", [P, 2, ATT])
            s24 = m.sb("s24", [P, 2, GROUPS, HEADS])
            srow = m.sb("srow", [HEADS, 2, GROUPS, P + 1])
            oprod = m.sb("oprod", [HEADS, 2, GROUPS, HD])
            oself = m.sb("oself", [HEADS, 2, GROUPS, 1])
            sst = m.sb("sst", [HEADS, 2, 3])
            pT = m.sb("pT", [P, 2, GROUPS, HEADS])
            spread = m.sb("spread", [HEADS, 2, GROUPS, HEADS, HD])
            arow = m.sb("arow", [1, ATT])
        ones = m.sb("ones", [P, 1])

        psS = m.ps("psS", [P, 4, 512])
        psP = m.ps("psP", [P, 2, 512])
        psO = m.ps("psO", [P, 2, 512])
        psP_flat = psP[:].rearrange("p a k -> p (a k)")

        S = {n: m.sem(n) for n in (
            "k0_in", "v_in", "g_masked", "w_turned", "qk_in", "kept", "g_const", "masks", "mchain", "x_full", "x_free",
            "scored", "masked", "maxed", "exped", "p_turned", "p_copied", "mixed", "inverted", "normalised", "att_stored",
            "gelued", "gchain", "g_var", "g_root", "g_normed", "z_done", "g_out", "g_stored", "gv_stored",
            "schain", "s_scored", "s_turned", "s_max", "s_exp", "s_probs", "s_probs_v", "s_pT", "s_pT_copied", "s_spread", "s_mixed",
            "s_k_used", "s_v_used", "s_row", "s_stored", "s_seen")}
        g_in, sk_in, sv_in = m.pair("g_in"), m.pair("sk_in"), m.pair("sv_in")
        block = m.block()

        def last_of(t):
            return (t // 2 + 1) * 16

        @block.sync
        def _(sp):
            sp.dma_start(k0n[:], fold[:, :, ATT:ATT + GW]).then_inc(S["k0_in"], 16)
            for t in range(2):
                at, n, _ = tiles[t]
                sp.dma_start(gin[0:n, t], proj_d[at:at + n, 3 * ATT:WIN]).then_inc(g_in[t], 16)
            sp.dma_start(wn[:], w_s[0].rearrange("h q p -> q h p")).then_inc(S["g_const"], 16)
            sp.dma_start(bn[:], b_s[0]).then_inc(S["g_const"], 16)
            sp.dma_start(gain[:], bcast(gm_ln_g.rearrange("a h c -> a (h c)"), P)).then_inc(S["g_const"], 16)
            sp.dma_start(shift[:], bcast(gm_ln_b.rearrange("a h c -> a (h c)"), P)).then_inc(S["g_const"], 16)
            with nc.allow_non_contiguous_dma(reason="four weights of one position"):
                for h in range(GM_HEADS):
                    sp.dma_start(w00[:, h, :], bcast(w_s[0, h, 0:1, 0:1], NS)).then_inc(S["g_const"], 16)
                    sp.dma_start(b00[:, h, :], bcast(b_s[0, h:h + 1, 0:1], NS)).then_inc(S["g_const"], 16)
            sp.dma_start(v[:], fold[:, :, V0:V0 + ATT]).then_inc(S["v_in"], 16)
            for t, (at, n, _) in enumerate(tiles[2:], 2):
                sp.wait_ge(S["g_out"], t - 1)
                sp.dma_start(gin[0:n, t % 2], proj_d[at:at + n, 3 * ATT:WIN]).then_inc(g_in[t % 2], 16)

            def load_qk(r):
                if not isinstance(r, int):
                    sp.wait_ge(S["x_full"], F + 1 + TURNS * r)
                sp.dma_start(qkn[:, 0:ATT], flat(fold[:, ds(r, 1), 0:ATT])).then_inc(S["qk_in"], 16)
                sp.dma_start(qkn[:, ATT:], flat(fold[:, ds(r, 1), ATT + GW:2 * ATT])).then_inc(S["qk_in"], 16)

            repeat(sp, F, load_qk)

            def load_sample(i):
                for j in range(2):
                    b = 2 * i + j
                    row = proj_d[ds(b + SEQ, 1), :]
                    cached = [cache[g][0, ds(b, 1)].rearrange("a (j s) c h d -> (a j) s c (h d)", s=dil)[:, 0]
                              for g, (win, dil) in enumerate(WINDOWS)]
                    ours = lambda c: row[:, c * ATT:(c + 1) * ATT].rearrange("a (g h d) -> (a h) g d", g=GROUPS, h=HEADS)
                    after(sp, S["s_k_used"], b - 1)
                    for g in range(GROUPS):
                        sp.dma_start(k_s[:, j, g], cached[g][:, 0]).then_inc(sk_in[j], 16)
                    sp.dma_start(qb[:, j], bcast(row[:, 0:ATT], P)).then_inc(sk_in[j], 16)
                    for c in range(2):
                        sp.dma_start(own[:, j, c], ours(c)).then_inc(sk_in[j], 16)
                    after(sp, S["s_v_used"], b - 1)
                    for g in range(GROUPS):
                        sp.dma_start(v_s[:, j, g], cached[g][:, 1]).then_inc(sv_in[j], 16)
                    sp.dma_start(own[:, j, 2], ours(2)).then_inc(sv_in[j], 16)

            if samples:
                repeat(sp, NS // 2, load_sample)
            n = 0
            for g, (win, dil) in enumerate(WINDOWS):
                keep = min(win, SEQ)
                for c in range(2):
                    src = proj_d[:, (1 + c) * ATT + g * GW:(1 + c) * ATT + (g + 1) * GW]
                    if samples:
                        sp.dma_start(outs[5 + g][0, :, 0, c].rearrange("s h d -> s (h d)"), src[SEQ:TOK])\
                          .then_inc(S["kept"], 16)
                    else:
                        sp.dma_start(outs[2 + g][0, 0, :, c].rearrange("s h d -> s (h d)"), src[SEQ - keep:SEQ])\
                          .then_inc(S["kept"], 16)
                    n += 1
            sp.wait_ge(S["kept"], 16 * n)
            sp.wait_ge(S["g_stored"], 16 * NTL)
            if samples:
                sp.wait_ge(S["gv_stored"], 16)

        @block.gpsimd
        def _(pool):
            pool.wait_ge(S["g_const"], 16 * (4 + 2 * GM_HEADS))
            nc.gpsimd.affine_select(out=wn[:], in_=wn[:], compare_op=ALU.is_ge, fill=0.0, base=0,
                                    pattern=[[0, GM_HEADS], [-1, P]], channel_multiplier=1).then_inc(S["g_masked"], 1)
            chain = Chain(pool, S["masks"])
            chain.link(nc.gpsimd.memset(near[:], 0.0))
            chain.link(nc.gpsimd.memset(far[:], 0.0))
            chain.link(nc.gpsimd.memset(eps[:], EPS))
            chain.link(nc.gpsimd.memset(ones[:], 1.0))
            chain.link(nc.gpsimd.affine_select(out=near[:], in_=near[:], compare_op=ALU.is_ge, fill=NEG, base=0,
                                               pattern=[[1, F], [-1, F], [-F, P]], channel_multiplier=F))
            chain.link(nc.gpsimd.affine_select(out=near[:], in_=near[:], compare_op=ALU.is_ge, fill=NEG, base=REACH,
                                               pattern=[[-1, F], [1, F], [F, P]], channel_multiplier=-F))
            chain.link(nc.gpsimd.affine_select(out=far[:], in_=far[:], compare_op=ALU.is_ge, fill=NEG, base=0,
                                               pattern=[[0, F], [0, 2], [-1, P]], channel_multiplier=1))
            chain.link(nc.gpsimd.iota(steps[:, 2], pattern=[[-1, P]], base=P, channel_multiplier=1))

            def store_att(r):
                if slots:
                    for k in range(HEADS // R):
                        slots.gather_round(pool, 0, HEADS // R * r + (base + k))
                pool.wait_ge(S["normalised"], HEADS * r + HEADS)
                pool.dma_start(flat(mix_fold[FROM:, ds(r, 1), 0:ATT]),
                               att[FROM:].rearrange("p g h d -> p (g h d)")).then_inc(S["att_stored"], 16)

            repeat(pool, F, store_att)
            pool.wait_ge(S["att_stored"], 16 * F)
            if samples:
                pool.wait_ge(S["s_stored"], 16 * NS)

        def mul_bcast(out, a, b, shape):
            return nc.vector.tensor_tensor(out, a, b.to_broadcast(shape), ALU.mult)

        @block.vector
        def _(dve):
            chain = Chain(dve, S["mchain"])
            dve.wait_ge(S["masks"], 8)
            for g in range(GROUPS - 1):
                apart = WINDOWS[g + 1][1] // F
                chain.link(nc.vector.tensor_scalar(steps[:, g], steps[:, 2], apart - 1, None, ALU.bitwise_and))
                chain.link(nc.vector.tensor_scalar(off[:, g], steps[:, g], 0.5, NEG, ALU.is_gt, ALU.mult))
                for r in range(F):
                    chain.link(nc.vector.tensor_tensor(far[:, r, g], far[:, r, g], off[:, g], ALU.min))

            g = Chain(dve, S["gchain"])
            dve.wait_ge(S["g_const"], 16 * (4 + 2 * GM_HEADS))
            for t, (at, n, _) in enumerate(tiles):
                dve.wait_ge(S["gelued"], t + 1)
                u = gin[0:n, t % 2, 0:GM].rearrange("p (h c) -> p h c", h=GM_HEADS)
                w = gin[0:n, t % 2, GM:]
                wh = w.rearrange("p (h c) -> p h c", h=GM_HEADS)
                sqh = gsq[0:n].rearrange("p (h c) -> p h c", h=GM_HEADS)
                bc = [n, GM_HEADS, GM // GM_HEADS]
                mean, var, rstd = (gst[0:n, a, :] for a in range(3))
                g.link(nc.vector.tensor_reduce(mean, wh, AX_X, ALU.add))
                g.link(nc.vector.tensor_scalar(mean, mean, GM_HEADS / GM, None, ALU.mult))
                g.link(nc.vector.tensor_tensor(wh, wh, mean.unsqueeze(2).to_broadcast(bc), ALU.subtract))
                g.link(nc.vector.tensor_tensor(gsq[0:n], w, w, ALU.mult))
                nc.vector.tensor_reduce(var, sqh, AX_X, ALU.add).then_inc(S["g_var"], 1)
                dve.wait_ge(S["g_root"], t + 1)
                g.link(nc.vector.reciprocal(rstd, var))
                g.link(nc.vector.tensor_tensor(wh, wh, rstd.unsqueeze(2).to_broadcast(bc), ALU.mult))
                g.link(nc.vector.tensor_tensor(w, w, gain[0:n], ALU.mult))
                nc.vector.tensor_tensor(w, w, shift[0:n], ALU.add).then_inc(S["g_normed"], 1)
                if t >= 1:
                    dve.wait_ge(S["g_stored"], 16 * t)
                go = gout[0:n].rearrange("p (h c) -> p h c", h=GM_HEADS)
                if n == P:
                    dve.wait_ge(S["z_done"], t + 1)
                    for h in range(GM_HEADS):
                        last = nc.vector.scalar_tensor_tensor(go[:, h], psO[:, 0, h * P:(h + 1) * P], bT[:, h:h + 1],
                                                              u[:, h], ALU.add, ALU.mult)
                else:
                    dve.wait_ge(S["g_normed"], t + 1)
                    g.link(nc.vector.tensor_tensor(go, wh, w00[:].to_broadcast(bc), ALU.mult))
                    g.link(nc.vector.tensor_tensor(go, go, b00[:].to_broadcast(bc), ALU.add))
                    last = nc.vector.tensor_tensor(go, go, u, ALU.mult)
                last.then_inc(S["g_out"], 1)

            def finish(r, h):
                n = HEADS * r + h
                dve.wait_ge(S["mixed"], n + 1)
                nc.vector.reciprocal(inv[:, h:h + 1], den[:, h:h + 1]).then_inc(S["inverted"], 1)
                dve.wait_ge(S["inverted"], n + 1)
                if h == 0:
                    after(dve, S["att_stored"], 16 * r)
                nc.vector.tensor_scalar(att[:, :, h], psO[:, h % 2, 0:GROUPS * HD].rearrange("p (g d) -> p g d", g=GROUPS),
                                        inv[:, h:h + 1], None, ALU.mult).then_inc(S["normalised"], 1)

            def fold_tile(r):
                for h in range(HEADS):
                    n = HEADS * r + h
                    dve.wait_ge(S["scored"], n + 1)
                    after(dve, S["p_turned"], n - lag(h) + 1)
                    nc.vector.scalar_tensor_tensor(scores[:, h % 3, 0:NEAR], psS[:, h % 2, 0:NEAR], SCALE,
                                                   near[:, ds(r, 1)].rearrange("p a b k -> p (a b k)"), ALU.mult, ALU.add)
                    nc.vector.scalar_tensor_tensor(scores[:, h % 3, NEAR:KEYS], psS[:, 2 + h % 2, 0:KEYS - NEAR], SCALE,
                                                   far[:, ds(r, 1)].rearrange("p a b k -> p (a b k)"),
                                                   ALU.mult, ALU.add).then_inc(S["masked"], 1)
                    dve.wait_ge(S["masked"], n + 1)
                    nc.vector.tensor_reduce(top[:, h:h + 1], scores[:, h % 3], AX_X, ALU.max, negate=True)\
                        .then_inc(S["maxed"], 1)
                    if slots:
                        slots.dot(dve, round_of(r, h), h % R, slots.h2[:])
                        if h:
                            slots.add(dve, round_of(r, h - 1), (h - 1) % R)
                    if h >= 2:
                        finish(r, h - 2)
                if slots:
                    slots.add(dve, round_of(r, HEADS - 1), R - 1)
                finish(r, HEADS - 2)
                finish(r, HEADS - 1)

            repeat(dve, F, fold_tile)

            def sample_pair(i):
                c = Chain(dve, S["schain"], 2 * LINKS * i)
                grouped = lambda a: a.rearrange("p (g w) -> p g w", g=GROUPS)
                for j in range(2):
                    dve.wait_ge(sk_in[j], K_LOADS * i + K_LOADS)
                    after(dve, S["s_mixed"], 2 * i + j - 1)
                    c.link(nc.vector.tensor_tensor(grouped(prod[:, j]), k_s[:, j], grouped(qb[:, j]), ALU.mult))
                    nc.vector.tensor_reduce(s24[:, j], prod[:, j].rearrange("p (g h d) -> p g h d", g=GROUPS, h=HEADS),
                                            AX_X, ALU.add).then_inc(S["s_scored"], 1)
                    c.link(nc.vector.tensor_tensor(oprod[:, j], own[:, j, 0], own[:, j, 1], ALU.mult))
                    c.link(nc.vector.tensor_reduce(oself[:, j, :, 0], oprod[:, j], AX_X, ALU.add))
                    nc.vector.tensor_scalar(srow[:, j, :, P:P + 1], oself[:, j], SCALE, None, ALU.mult)\
                        .then_inc(S["s_k_used"], 1)
                for j in range(2):
                    b = 2 * i + j
                    dve.wait_ge(S["s_turned"], b + 1)
                    c.link(nc.vector.tensor_scalar(srow[:, j, :, 0:P],
                                                   psP[0:HEADS, j, 0:GROUPS * P].rearrange("h (g k) -> h g k", g=GROUPS),
                                                   SCALE, None, ALU.mult))
                    row = srow[:, j].rearrange("h g k -> h (g k)")
                    nc.vector.tensor_reduce(sst[:, j, 0:1], row, AX_X, ALU.max, negate=True).then_inc(S["s_max"], 1)
                for j in range(2):
                    b = 2 * i + j
                    row = srow[:, j].rearrange("h g k -> h (g k)")
                    dve.wait_ge(S["s_exp"], b + 1)
                    c.link(nc.vector.reciprocal(sst[:, j, 2:3], sst[:, j, 1:2]))
                    nc.vector.tensor_scalar(row, row, sst[:, j, 2:3], None, ALU.mult).then_inc(S["s_probs"], 1)
                for j in range(2):
                    b = 2 * i + j
                    dve.wait_ge(S["s_probs"], b + 1)
                    dve.wait_ge(sv_in[j], V_LOADS * i + V_LOADS)
                    mul_bcast(oprod[:, j], own[:, j, 2], srow[:, j, :, P:P + 1], [HEADS, GROUPS, HD])\
                        .then_inc(S["s_probs_v"], 1)
                    dve.wait_ge(S["s_probs_v"], b + 1)
                    for g in range(GROUPS):
                        last = nc.vector.tensor_tensor(
                            spread[:, j, g], oprod[:, j, g:g + 1].to_broadcast([HEADS, HEADS, HD]),
                            ident[0:HEADS, 0:HEADS].unsqueeze(2).to_broadcast([HEADS, HEADS, HD]), ALU.mult)
                    last.then_inc(S["s_spread"], 1)
                    dve.wait_ge(S["s_pT"], b + 1)
                    nc.vector.tensor_copy(pT[:, j], psO[:, j, 0:GROUPS * HEADS].rearrange("p (g h) -> p g h", g=GROUPS))\
                        .then_inc(S["s_pT_copied"], 1)
                    dve.wait_ge(S["s_pT_copied"], b + 1)
                    for g in range(GROUPS):
                        last = mul_bcast(prod[:, j, g * GW:(g + 1) * GW].rearrange("p (h d) -> p h d", h=HEADS),
                                         v_s[:, j, g].rearrange("p (h d) -> p h d", h=HEADS),
                                         pT[:, j, g].unsqueeze(2), [P, HEADS, HD])
                    last.then_inc(S["s_v_used"], 1)
                assert c.n == 2 * LINKS

            if samples:
                repeat(dve, NS // 2, sample_pair)

        @block.scalar
        def _(act):
            for t, (at, n, _) in enumerate(tiles):
                act.wait_ge(g_in[t % 2], last_of(t))
                nc.scalar.activation(gin[0:n, t % 2], gin[0:n, t % 2], ACT.Gelu_apprx_tanh).then_inc(S["gelued"], 1)
                if t == 0:
                    for n_x in range(F):
                        act.wait_ge(S["x_full"], n_x + 1)
                        nc.scalar.copy(kT0[:, :, n_x], psP[:, n_x % 2].rearrange("p (b k) -> p b k", b=PAIRS)).then_inc(S["x_free"], 1)
                    act.wait_ge(S["x_full"], F + 1)
                    nc.scalar.copy(bT[:], psO[:, 0, 0:GM_HEADS]).then_inc(S["w_turned"], 1)
                    nc.scalar.copy(wT[:], psP[:, F % 2].rearrange("p (b k) -> p b k", b=GM_HEADS)).then_inc(S["w_turned"], 1)
                    act.wait_ge(S["w_turned"], 2)
                    act.sem_inc(S["x_free"], 1)
                act.wait_ge(S["g_var"], t + 1)
                if t == 0:
                    act.wait_ge(S["masks"], 3)
                nc.scalar.activation(gst[0:n, 1, :], gst[0:n, 1, :], ACT.Sqrt, bias=eps[0:n, :],
                                     scale=GM_HEADS / GM).then_inc(S["g_root"], 1)
                if n == P:
                    act.wait_ge(S["g_out"], t + 1)
                    act.dma_start(mix_d[at:at + n, ATT:], gout[0:n]).then_inc(S["g_stored"], 16)
                else:
                    act.wait_ge(S["g_normed"], t + 1)
                    act.dma_start(outs[8].rearrange("a b s h c -> (a b s) (h c)"), gin[0:n, t % 2, GM:])\
                       .then_inc(S["gv_stored"], 16)
                    act.wait_ge(S["g_out"], t + 1)
                    act.dma_start(mix_d[at:at + n, ATT:], gout[0:n]).then_inc(S["g_stored"], 16)

            def fold_tile(r):
                for q in range(TURNS):
                    act.wait_ge(S["x_full"], F + 1 + TURNS * r + q + 1)
                    nc.scalar.copy(qkT[:, 4 * q:4 * q + 4], psP[:, q % 2].rearrange("p (b k) -> p b k", b=4))\
                        .then_inc(S["x_free"], 1)

                def exponentials(h):
                    n = HEADS * r + h
                    act.wait_ge(S["maxed"], n + 1)
                    nc.scalar.activation(scores[:, h % 3], scores[:, h % 3], ACT.Exp, bias=top[:, h:h + 1],
                                         accum_out=den[:, h:h + 1]).then_inc(S["exped"], 1)

                exponentials(0)
                for h in range(HEADS):
                    n = HEADS * r + h
                    if h + 1 < HEADS:
                        exponentials(h + 1)
                    if slots:
                        slots.weigh(act, round_of(r, h), h % R)
                    act.wait_ge(S["p_turned"], n + 1)
                    after(act, S["mixed"], n - 1)
                    nc.scalar.copy(probsT[:, h % 2].rearrange("p b k -> p (b k)"), psP_flat[:, 0:KEYS])\
                        .then_inc(S["p_copied"], 1)

            repeat(act, F, fold_tile)

            def sample_pair(i):
                for j in range(2):
                    act.wait_ge(S["s_max"], 2 * i + j + 1)
                    row = srow[:, j].rearrange("h g k -> h (g k)")
                    nc.scalar.activation(row, row, ACT.Exp, bias=sst[:, j, 0:1], accum_out=sst[:, j, 1:2])\
                        .then_inc(S["s_exp"], 1)
                for j in range(2):
                    b = 2 * i + j
                    act.wait_ge(S["s_mixed"], b + 1)
                    after(act, S["s_stored"], 16 * b)
                    nc.scalar.copy(arow[:], psS[0:1, 0:GROUPS].rearrange("p a k -> p (a k)")).then_inc(S["s_row"], 1)
                    act.wait_ge(S["s_row"], b + 1)
                    act.dma_start(mix_d[ds(b + SEQ, 1), 0:ATT], arow[:]).then_inc(S["s_stored"], 16)

            if samples:
                repeat(act, NS // 2, sample_pair)

        @block.tensor
        def _(pe):
            pe.wait_ge(S["k0_in"], 16)
            for r in range(F):
                if r >= 2:
                    pe.wait_ge(S["x_free"], r - 1)
                for p in range(PAIRS):
                    last = nc.tensor.transpose(psP[:, r % 2, p * P:(p + 1) * P], k0n[:, r, p * P:(p + 1) * P], ident[:])
                last.then_inc(S["x_full"], 1)
            pe.wait_ge(S["g_masked"], 1)
            pe.wait_ge(S["x_free"], F)
            for h in range(GM_HEADS):
                nc.tensor.transpose(psP[:, F % 2, h * P:(h + 1) * P], wn[:, h], ident[:])
            nc.tensor.transpose(psO[:, 0, 0:GM_HEADS], bn[:], ident[0:GM_HEADS, 0:GM_HEADS]).then_inc(S["x_full"], 1)
            pe.wait_ge(S["w_turned"], 2)
            for t in range(PROMPTS):
                pe.wait_ge(S["g_normed"], t + 1)
                if t:
                    pe.wait_ge(S["g_out"], t)
                for h in range(GM_HEADS):
                    last = nc.tensor.matmul(psO[:, 0, h * P:(h + 1) * P], wT[:, h],
                                            gin[:, t % 2, GM + h * P:GM + (h + 1) * P], start=True, stop=True)
                last.then_inc(S["z_done"], 1)
            pe.wait_ge(S["v_in"], 16)

            def fold_tile(r):
                pe.wait_ge(S["qk_in"], 32 * r + 32)
                after(pe, S["p_copied"], HEADS * r)
                pe.wait_ge(S["x_free"], F + 1 + TURNS * r)
                for q in range(TURNS):
                    if q >= 2:
                        pe.wait_ge(S["x_free"], F + 1 + TURNS * r + q - 1)
                    for b in range(4):
                        c = (4 * q + b) * P
                        last = nc.tensor.transpose(psP[:, q % 2, b * P:(b + 1) * P], qkn[:, c:c + P], ident[:])
                    last.then_inc(S["x_full"], 1)
                pe.wait_ge(S["x_free"], F + 1 + TURNS * r + TURNS)

                def score(h):
                    n = HEADS * r + h
                    rows, p = slice(h % 2 * HD, h % 2 * HD + HD), h // 2
                    after(pe, S["masked"], n - 1)
                    nc.tensor.matmul(psS[:, h % 2, 0:NEAR], qkT[rows, p], kT0[rows, p].rearrange("p r k -> p (r k)"),
                                     start=True, stop=True)
                    for g in range(1, GROUPS):
                        last = nc.tensor.matmul(psS[:, 2 + h % 2, (g - 1) * P:g * P], qkT[rows, g * PAIRS + p],
                                                qkT[rows, NQ + (g - 1) * PAIRS + p], start=True, stop=True)
                    last.then_inc(S["scored"], 1)

                def turn_probs(h):
                    n = HEADS * r + h
                    pe.wait_ge(S["exped"], n + 1)
                    after(pe, S["p_copied"], n)
                    for b in range(BLOCKS):
                        last = nc.tensor.transpose(psP_flat[:, b * P:(b + 1) * P], scores[:, h % 3, b * P:(b + 1) * P], ident[:])
                    last.then_inc(S["p_turned"], 1)

                def mix(h):
                    n = HEADS * r + h
                    pe.wait_ge(S["p_copied"], n + 1)
                    if isinstance(n, int) and n == 0:
                        pe.wait_ge(S["g_out"], PROMPTS)
                    after(pe, S["normalised"], n - 1)
                    for b in range(F):
                        nc.tensor.matmul(psO[:, h % 2, 0:HD], probsT[:, h % 2, b], v[:, b, h * HD:(h + 1) * HD],
                                         start=(b == 0), stop=(b == F - 1))
                    for g in range(1, GROUPS):
                        last = nc.tensor.matmul(psO[:, h % 2, g * HD:(g + 1) * HD], probsT[:, h % 2, F + g - 1],
                                                flat(v[:, ds(r, 1), g * GW + h * HD:g * GW + (h + 1) * HD]),
                                                start=True, stop=True)
                    last.then_inc(S["mixed"], 1)

                score(0)
                score(1)
                for h in range(HEADS):
                    if h + 2 < HEADS:
                        score(h + 2)
                    turn_probs(h)
                    if h:
                        mix(h - 1)
                mix(HEADS - 1)

            repeat(pe, F, fold_tile)
            if not samples:
                return
            pe.wait_ge(S["normalised"], F * HEADS)

            def sample_pair(i):
                for j in range(2):
                    pe.wait_ge(S["s_scored"], 2 * i + j + 1)
                    pe.sem_inc(S["s_seen"], 1)
                    for g in range(GROUPS):
                        last = nc.tensor.transpose(psP[0:HEADS, j, g * P:(g + 1) * P], s24[:, j, g], ident[:])
                    last.then_inc(S["s_turned"], 1)
                for j in range(2):
                    pe.wait_ge(S["s_probs"], 2 * i + j + 1)
                    pe.sem_inc(S["s_seen"], 1)
                    for g in range(GROUPS):
                        last = nc.tensor.transpose(psO[:, j, g * HEADS:(g + 1) * HEADS], srow[:, j, g, 0:P],
                                                   ident[0:HEADS, 0:HEADS])
                    last.then_inc(S["s_pT"], 1)
                for j in range(2):
                    b = 2 * i + j
                    pe.wait_ge(S["s_v_used"], b + 1)
                    pe.wait_ge(S["s_spread"], b + 1)
                    after(pe, S["s_row"], b)
                    sums = psS[0:1, 0:GROUPS].rearrange("p a k -> p (a k)")
                    for g in range(GROUPS):
                        cols = slice(g * GW, (g + 1) * GW)
                        nc.tensor.matmul(sums[:, cols], ones[:], prod[:, j, cols], start=True, stop=False)
                        last = nc.tensor.matmul(sums[:, cols], ones[0:HEADS], spread[:, j, g].rearrange("p h d -> p (h d)"),
                                                start=False, stop=True)
                    last.then_inc(S["s_mixed"], 1)

            repeat(pe, NS // 2, sample_pair)


def output_stage(nc, name, tiles, ident, x_prompt, x_sample, mods_d, w_out, mix_d, hT, x1_d, h2_d, slots=None, base=0):
    CHUNKS = D // CK
    NTL = len(tiles)
    HALF = KD // 2
    w_view = w_out[0].rearrange("(k p) n -> p k n", p=P)
    x_rows = rows_of(tiles, x_prompt[0], x_sample.rearrange("b s d -> (b s) d"))
    with Stage(nc, name) as m:
        xin = m.sb("xin", [P, 2, D])
        y = m.sb("y", [P, NTL, D])
        w = m.sb("w", [P, 2, KD, CK])
        quarter = lambda j, a: w[:, j, a * HALF:(a + 1) * HALF].rearrange("p k n -> p (k n)")
        sq = quarter(1, 1)
        vec = {GT1: [quarter(0, 0)], SC2: [quarter(0, 1)], SH2: [quarter(1, 0)]}
        if tiles[-1][1] == NS:
            for s in vec:
                vec[s].append(m.sb(f"vec_s{s}", [NS, D])[:])
        stat = m.sb("stat", [P, 6, NTL])
        eps = m.sb("eps", [P, 1])
        psT = m.ps("psT", [P, 3, 4, P])
        acc = [m.ps(f"acc{t}", [P, 512]) for t in range(NTL)]
        mix_in, x_in, w_ready, acc_full, copied = (m.pair(s) for s in ("mix_in", "x_in", "w_ready", "acc_full", "copied"))
        mod_in, eps_set, turned, psT_free, squared, rooted, chain_v, x1_done, h2_done, stored = (m.sem(s) for s in (
            "mod_in", "eps_set", "turned", "psT_free", "squared", "rooted", "chain", "x1_done", "h2_done", "stored"))
        block = m.block()

        @block.sync
        def _(sp):
            for t, (at, n, _) in enumerate(tiles):
                if t >= 2:
                    sp.wait_ge(turned, 4 * (t - 1))
                sp.dma_start(xin[0:n, t % 2], mix_d[at:at + n, :]).then_inc(mix_in[t % 2], 16)

            def chunk_pair(i):
                for j in range(2):
                    after(sp, acc_full[j], NTL * i)
                    sp.dma_start(w[:, j], w_view[:, :, ds((2 * i + j) * CK, CK)]).then_inc(w_ready[j], 16)

            repeat(sp, CHUNKS // 2, chunk_pair)
            for t in range(2):
                n = tiles[t][1]
                if t == 0:
                    sp.wait_ge(turned, 4 * NTL)
                sp.dma_start(xin[0:n, t], x_rows[t]).then_inc(x_in[t], 16)
            for j in range(2):
                sp.wait_ge(acc_full[j], NTL * CHUNKS // 2)
            for s in (GT1, SC2, SH2):
                load_mods(sp, mods_d, s, vec[s], mod_in)
            for t, (at, n, _) in enumerate(tiles[2:], 2):
                sp.wait_ge(stored, 32 * (t - 1))
                sp.dma_start(xin[0:n, t % 2], x_rows[t]).then_inc(x_in[t % 2], 16)

        @block.gpsimd
        def _(pool):
            nc.gpsimd.memset(eps[:], EPS).then_inc(eps_set, 1)
            if slots:
                repeat(pool, CHUNKS // 2, lambda i: slots.gather_round(pool, 0, base + i))
            for t, (at, n, _) in enumerate(tiles):
                pool.wait_ge(h2_done, t + 1)
                if t:
                    pool.wait_ge(stored, 32 * t)
                pool.dma_start(x1_d[at:at + n, :], xin[0:n, t % 2]).then_inc(stored, 16)
                pool.dma_start(h2_d[at:at + n, :], y[0:n, t]).then_inc(stored, 16)
            pool.wait_ge(stored, 32 * NTL)

        @block.scalar
        def _(act):
            for t, (at, n, c) in enumerate(tiles):
                for q in range(4):
                    act.wait_ge(turned, 4 * t + q + 1)
                    nc.scalar.copy(hT[:, 4 * q:4 * q + 4, c:c + n], psT[:, (4 * t + q) % 3, :, 0:n])\
                        .then_inc(psT_free, 1)

            def chunk_pair(i):
                for j in range(2):
                    for t, (at, n, _) in enumerate(tiles):
                        if slots and t < R // 2:
                            slots.weigh(act, base + i, R // 2 * j + t)
                        act.wait_ge(acc_full[j], NTL * i + t + 1)
                        nc.scalar.copy(y[0:n, t, ds((2 * i + j) * CK, CK)], acc[t][0:n, 0:CK]).then_inc(copied[j], 1)

            repeat(act, CHUNKS // 2, chunk_pair)
            act.wait_ge(eps_set, 1)
            for j in range(2):
                act.wait_ge(copied[j], NTL * CHUNKS // 2)
                act.wait_ge(acc_full[j], NTL * CHUNKS // 2)
            for t, (at, n, c) in enumerate(tiles):
                for part, src in ((0, y[0:n, t]), (1, xin[0:n, t % 2])):
                    if part:
                        act.wait_ge(x1_done, t + 1)
                    if t or part:
                        act.wait_ge(squared, 2 * t + part)
                    s = 3 * part
                    nc.scalar.activation(sq[0:n, :], src, ACT.Square, accum_out=stat[0:n, s, t:t + 1]).then_inc(squared, 1)
                    act.wait_ge(squared, 2 * t + part + 1)
                    nc.scalar.activation(stat[0:n, s + 1, t:t + 1], stat[0:n, s, t:t + 1], ACT.Sqrt, bias=eps[0:n, :],
                                         scale=1.0 / D).then_inc(rooted, 1)
                for q in range(4):
                    act.wait_ge(turned, 4 * (NTL + t) + q + 1)
                    nc.scalar.copy(hT[:, 4 * q:4 * q + 4, c:c + n], psT[:, (4 * (NTL + t) + q) % 3, :, 0:n])\
                        .then_inc(psT_free, 1)

        @block.vector
        def _(dve):
            if slots:
                repeat(dve, CHUNKS // 2, lambda i: slots.sum_round(dve, base + i))
            chain = Chain(dve, chain_v)
            dve.wait_ge(mod_in, 16 * sum(len(v) for v in vec.values()))
            for t, (at, n, _) in enumerate(tiles):
                gate, scale, shift = (vec[s][-1 if n == NS else 0][0:n] for s in (GT1, SC2, SH2))
                yt, xt = y[0:n, t], xin[0:n, t % 2]
                dve.wait_ge(rooted, 2 * t + 1)
                chain.link(nc.vector.reciprocal(stat[0:n, 2, t:t + 1], stat[0:n, 1, t:t + 1]))
                chain.link(nc.vector.scalar_tensor_tensor(yt, yt, stat[0:n, 2, t:t + 1], gate, ALU.mult, ALU.mult))
                dve.wait_ge(x_in[t % 2], 16 * (t // 2 + 1))
                nc.vector.tensor_tensor(xt, xt, yt, ALU.add).then_inc(x1_done, 1)
                dve.wait_ge(rooted, 2 * t + 2)
                chain.link(nc.vector.reciprocal(stat[0:n, 5, t:t + 1], stat[0:n, 4, t:t + 1]))
                chain.link(nc.vector.scalar_tensor_tensor(yt, xt, stat[0:n, 5, t:t + 1], scale, ALU.mult, ALU.mult))
                nc.vector.tensor_tensor(yt, yt, shift, ALU.add).then_inc(h2_done, 1)

        @block.tensor
        def _(pe):
            for t, (at, n, _) in enumerate(tiles):
                pe.wait_ge(mix_in[t % 2], 16 * (t // 2 + 1))
                turn(nc, pe, xin[:, t % 2], n, psT, ident, psT_free, turned, 4 * t)
            pe.wait_ge(psT_free, 4 * NTL)

            def chunk_pair(i):
                for j in range(2):
                    pe.wait_ge(w_ready[j], 16 * i + 16)
                    for t, (at, n, c) in enumerate(tiles):
                        after(pe, copied[1 - j], 0 if isinstance(i, int) and not j else NTL * (i + j - 1) + t + 1)
                        for k in range(KD):
                            last = nc.tensor.matmul(acc[t][0:n, 0:CK], hT[:, k, c:c + n], w[:, j, k, :],
                                                    start=(k == 0), stop=(k == KD - 1))
                        last.then_inc(acc_full[j], 1)

            repeat(pe, CHUNKS // 2, chunk_pair)
            for t, (at, n, _) in enumerate(tiles):
                pe.wait_ge(h2_done, t + 1)
                turn(nc, pe, y[:, t], n, psT, ident, psT_free, turned, 4 * (NTL + t))


class Picker:
    LINKS, MIN = 18, -3.0e38

    def __init__(self, m, nc, scores, experts, gates):
        self.nc, self.scores, self.experts, self.gates = nc, scores, experts, gates
        self.keys, self.left = m.sb("keys", [P, 2, NKEYS]), m.sb("left", [P, 2, NKEYS])
        self.best, self.place = m.sb("best", [P, 2, TOPK]), m.sb("place", [P, 2, TOPK], U32)
        self.placef = m.sb("placef", [P, 2, TOPK])
        self.sums, self.sums_left = m.sb("sums", [P, 1, TOPK * TOPK]), m.sb("sums_left", [P, 1, TOPK * TOPK])
        self.picked, self.pos = m.sb("picked", [P, 1, TOPK]), m.sb("pos", [P, 1, TOPK], U32)
        self.half, self.halff = m.sb("half", [P, 2, TOPK], U32), m.sb("halff", [P, 2, TOPK])
        self.onehot, self.found = m.sb("onehot", [P, 2 * TOPK, TOPK]), m.sb("found", [P, 2, TOPK])
        self.row, self.rows = m.sb("row", [P, TOPK]), m.sb("rows", [P, SLOTS])
        self.expo, self.total = m.sb("expo", [P, TOPK]), m.sb("total", [P, 2])
        self.iota_i, self.iota_f = m.sb("iota_i", [P, TOPK], mybir.dt.int32), m.sb("iota_f", [P, TOPK])
        self.iota_set, self.chain, self.shifted, self.exped, self.done, self.carrier = (m.sem(s) for s in (
            "iota_set", "pick_chain", "pick_shifted", "pick_exped", "pick_done", "pick_carrier"))

    def number(self, pool):
        self.nc.gpsimd.iota(self.iota_i[:], pattern=[[1, TOPK]], base=0, channel_multiplier=0).then_inc(self.iota_set, 1)

    def prepare(self, dve):
        dve.wait_ge(self.iota_set, 1)
        self.nc.vector.tensor_copy(self.iota_f[:], self.iota_i[:]).then_inc(self.iota_set, 1)
        dve.wait_ge(self.iota_set, 2)

    def top16(self, dve, c, values, left, top, index):
        segments = range(values.shape[1])
        for lo in (0, 8):
            src = left if lo else values
            dve.sem_inc(self.carrier, 1)
            for s in segments:
                last = self.nc.vector.max(top[:, s, lo:lo + 8], src[:, s])
            c.link(last)
            dve.sem_inc(self.carrier, 1)
            for s in segments:
                last = self.nc.vector.max_index(index[:, s, lo:lo + 8], top[:, s, lo:lo + 8], src[:, s])
                if not lo:
                    last = self.nc.vector.match_replace(left[:, s], top[:, s, 0:8], values[:, s], self.MIN)
            c.link(last)

    def pick(self, dve, h, t, n):
        v, c = self.nc.vector, Chain(dve, self.chain, self.LINKS * n)
        c.link(v.tensor_copy(self.keys[:], self.scores[:, ds(2 * h, 2)]))
        self.top16(dve, c, self.keys, self.left, self.best, self.place)
        v.tensor_copy(self.placef[:], self.place[:])
        shape = [P, TOPK, TOPK]
        c.link(v.tensor_tensor(self.sums[:, 0].rearrange("p (a b) -> p a b", a=TOPK),
                               self.best[:, 0].unsqueeze(2).to_broadcast(shape),
                               self.best[:, 1].unsqueeze(1).to_broadcast(shape), ALU.add))
        self.top16(dve, c, self.sums, self.sums_left, self.picked, self.pos)
        v.tensor_tensor(self.expo[:], self.picked[:, 0], self.picked[:, 0, 0:1].to_broadcast([P, TOPK]), ALU.subtract)\
            .then_inc(self.shifted, 1)
        v.tensor_scalar(self.half[:, 0], self.pos[:, 0], 4, None, ALU.logical_shift_right)
        c.link(v.tensor_scalar(self.half[:, 1], self.pos[:, 0], TOPK - 1, None, ALU.bitwise_and))
        c.link(v.tensor_copy(self.halff[:], self.half[:]))
        c.link(v.tensor_tensor(self.onehot[:], self.halff[:].rearrange("p a k -> p (a k)").unsqueeze(2)
                               .to_broadcast([P, 2 * TOPK, TOPK]),
                               self.iota_f[:].unsqueeze(1).to_broadcast([P, 2 * TOPK, TOPK]), ALU.is_equal))
        for a in range(2):
            hot = self.onehot[:, a * TOPK:(a + 1) * TOPK]
            last = v.tensor_tensor(hot, hot, self.placef[:, a].unsqueeze(1).to_broadcast(shape), ALU.mult)
        c.link(last)
        c.link(v.tensor_reduce(self.found[:].rearrange("p a k -> p (a k)"), self.onehot[:], AX_X, ALU.add))
        c.link(v.scalar_tensor_tensor(self.row[:], self.found[:, 0], float(NKEYS), self.found[:, 1], ALU.mult, ALU.add))
        v.tensor_copy(self.rows[:, ds(TOPK * h, TOPK)], self.row[:])
        c.link(v.tensor_copy(of_tile(self.experts, t, ds(TOPK * h, TOPK)), self.row[:]))
        assert c.n == self.LINKS - 1

    def exponentials(self, act, n):
        act.wait_ge(self.shifted, n + 1)
        self.nc.scalar.activation(self.expo[:], self.expo[:], ACT.Exp, accum_out=self.total[:, 0:1]).then_inc(self.exped, 1)

    def gate(self, dve, h, t, n):
        c = Chain(dve, self.chain, self.LINKS * n + self.LINKS - 1)
        dve.wait_ge(self.exped, n + 1)
        c.link(self.nc.vector.reciprocal(self.total[:, 1:2], self.total[:, 0:1]))
        self.nc.vector.tensor_scalar(of_tile(self.gates, t, ds(TOPK * h, TOPK)), self.expo[:], self.total[:, 1:2], None,
                                     ALU.mult).then_inc(self.done, 1)
        dve.wait_ge(self.done, n + 1)


def routing_stage(nc, name, tiles, ident, w_q, sub_keys, hT, scores_d, experts, gates, slots=None, base=0):
    CHUNKS = D // CK
    NTL, W = len(tiles), width(tiles)
    SEG = 2 * PH
    w_view = w_q[0].rearrange("(k p) n -> p k n", p=P)
    with Stage(nc, name) as m:
        w = m.sb("w", [P, 2, KD, CK])
        qrT = m.sb("qrT", [P, SEG, W])
        keys_n, keysT = m.sb("keys_n", [P, 2, P]), m.sb("keysT", [P, 2, P])
        sc = m.sb("sc", [P, 2, SEG, NKEYS])
        acc = [m.ps(f"acc{j}", [P, 512]) for j in range(2)]
        psC = m.ps("psC", [P, SEG, NKEYS])
        picker = None if slots else Picker(m, nc, sc[:, 0], experts, gates)
        keys_in, keys_turned, keys_set, scored, sc_copied = (m.sem(s) for s in (
            "keys_in", "keys_turned", "keys_set", "scored", "sc_copied"))
        w_ready, acc_full, copied, stored = (m.pair(s) for s in ("w_ready", "acc_full", "copied", "stored"))
        block = m.block()

        @block.sync
        def _(sp):
            sp.dma_start(keys_n[:], sub_keys[0].rearrange("a k c -> k a c")).then_inc(keys_in, 16)

            def chunk_pair(i):
                for j in range(2):
                    if not isinstance(i, int):
                        sp.wait_ge(acc_full[0], 2 * i + j - 1)
                        sp.wait_ge(acc_full[1], 2 * i + j - 1)
                    sp.dma_start(w[:, j], w_view[:, :, ds((2 * i + j) * CK, CK)]).then_inc(w_ready[j], 16)

            repeat(sp, CHUNKS // 2, chunk_pair)
            for t, (at, n, _) in enumerate(tiles):
                sp.wait_ge(sc_copied, t + 1)
                sp.dma_start(scores_d[at:at + n, :], sc[0:n, t % 2].rearrange("p s k -> p (s k)")).then_inc(stored[t % 2], 16)
            for j in range(2):
                sp.wait_ge(stored[j], 16 * ((NTL + 1 - j) // 2))

        @block.gpsimd
        def _(pool):
            if slots:
                repeat(pool, CHUNKS // 2, lambda i: slots.gather_round(pool, 0, base + i))
            else:
                picker.number(pool)

        @block.scalar
        def _(act):
            act.wait_ge(keys_turned, 1)
            nc.scalar.copy(keysT[:], psC[:, 0:2]).then_inc(keys_set, 1)

            def chunk_pair(i):
                for j in range(2):
                    for b in range(2):
                        if slots:
                            slots.weigh(act, base + i, R // 2 * j + b)
                        act.wait_ge(acc_full[b], 2 * i + j + 1)
                        nc.scalar.copy(flat(qrT[:, ds(2 * (2 * i + j) + b, 1)]), acc[b][:, 0:W]).then_inc(copied[b], 1)

            repeat(act, CHUNKS // 2, chunk_pair)
            for t, (at, n, _) in enumerate(tiles):
                act.wait_ge(scored, t + 1)
                if t >= 2:
                    act.wait_ge(stored[t % 2], 16 * (t // 2))
                nc.scalar.copy(sc[0:n, t % 2], psC[0:n]).then_inc(sc_copied, 1)
            if not slots:
                with act.Fori(0, PH) as h:
                    picker.exponentials(act, h)

        @block.vector
        def _(dve):
            if slots:
                repeat(dve, CHUNKS // 2, lambda i: slots.sum_round(dve, base + i))
                return
            picker.prepare(dve)
            dve.wait_ge(sc_copied, 1)
            with dve.Fori(0, PH) as h:
                picker.pick(dve, h, 0, h)
                picker.gate(dve, h, 0, h)

        @block.tensor
        def _(pe):
            pe.wait_ge(keys_in, 16)
            for a in range(2):
                last = nc.tensor.transpose(psC[:, a], keys_n[:, a], ident[:])
            last.then_inc(keys_turned, 1)

            def chunk_pair(i):
                for j in range(2):
                    pe.wait_ge(w_ready[j], 16 * i + 16)
                    for b in range(2):
                        after(pe, copied[b], 2 * i + j)
                        for k in range(KD):
                            last = nc.tensor.matmul(acc[b][:, 0:W], w[:, j, k, b * P:(b + 1) * P], hT[:, k, :],
                                                    start=(k == 0), stop=(k == KD - 1))
                        last.then_inc(acc_full[b], 1)

            repeat(pe, CHUNKS // 2, chunk_pair)
            pe.wait_ge(keys_set, 1)
            for b in range(2):
                pe.wait_ge(copied[b], CHUNKS)
            for t, (at, n, c) in enumerate(tiles):
                if t:
                    pe.wait_ge(sc_copied, t)
                for s in range(SEG):
                    last = nc.tensor.matmul(psC[0:n, s], qrT[:, s, c:c + n], keysT[:, s % 2], start=True, stop=True)
                last.then_inc(scored, 1)


def expert_stage(nc, ident, mods_d, x1_d, h2_d, scores_d, slots, base, experts, gates, outs):
    N = 512
    SEG = 2 * PH
    LAST = NT * ROUNDS
    with Stage(nc, "exp") as m:
        x1, y = m.sb("x1", [P, D]), m.sb("y", [P, D])
        gain_p, gain_s = m.sb("gain_p", [P, D]), m.sb("gain_s", [NS, D])
        h2_s = m.sb("h2_s", [P, 2, D])
        scores = m.sb("scores", [P, SEG, NKEYS])
        diag = m.sb("diag", [P, R, P])
        col = m.sb("col", [P, NS, NS])
        experts_s, gates_s = m.sb("experts_s", [P, NS], U32), m.sb("gates_s", [P, NS])
        zero = m.sb("zero", [P, N])
        stat = m.sb("stat", [P, 3])
        eps = m.sb("eps", [P, 1])
        acc = m.ps("acc", [P, D])
        psE = m.ps("psE", [P, 2, NS])
        picker = Picker(m, nc, scores, experts, gates)
        const, scores_in, x1_in, gain_in, weight_set, carrier, carrier_v, carrier_a = (m.sem(s) for s in (
            "const", "scores_in", "x1_in", "gain_in", "weight_set", "carrier", "carrier_v", "carrier_a"))
        h2_s_in = m.pair("h2_s_in")
        chain_v, tile_dotted, acc_full, squared, rooted, y_done, stored, s_turned, s_kept = (m.sem(s) for s in (
            "chain_v", "tile_dotted", "acc_full", "squared", "rooted", "y_done", "stored", "s_turned", "s_kept"))
        block = m.block()
        y_out = outs[0][0].rearrange("(t p) d -> p t d", p=P)
        x1_tiles = x1_d[0:SEQ, :].rearrange("(t p) d -> p t d", p=P)
        h2_tiles = h2_d[0:SEQ, :].rearrange("(t p) d -> p t d", p=P)
        scores_tiles = scores_d[0:SEQ, :].rearrange("(t p) d -> p t d", p=P)
        scores_flat = scores[:].rearrange("p s k -> p (s k)")

        def over_tiles(eng, tile):
            tile(0)
            with eng.Fori(1, NT - 1) as t:
                tile(t)
            tile(NT - 1)

        def over_rounds(eng, t, picking, plain):
            lo, heads = (base, 2) if isinstance(t, int) and t == 0 else (0, 1)
            with eng.Fori(0, PH // heads) as g:
                picking([heads * g + k for k in range(heads)], g + lo)
            with eng.Fori(lo + PH // heads, ROUNDS) as i:
                plain(i)

        @block.sync
        def _(sp):
            sp.dma_start(gain_s[:], mods_d[0:NS, GT2, :]).then_inc(gain_in, 16)
            sp.dma_start(gain_p[:], bcast(mods_d[NS:ROWS, GT2, :], P)).then_inc(gain_in, 16)

            def tile(t):
                first, last = isinstance(t, int) and t == 0, isinstance(t, int) and t == NT - 1
                if not first:
                    sp.wait_ge(tile_dotted, t)
                    sp.dma_start(slots.h2[:], flat(h2_tiles[:, ds(t, 1)])).then_inc(slots.h2_in, 16)
                    sp.wait_ge(picker.done, PH * t)
                sp.dma_start(scores_flat[0:NS if last else P], scores_d[SEQ:TOK, :] if last else
                             flat(scores_tiles[:, ds(t + 1, 1)])).then_inc(scores_in, 16)
                if not first:
                    sp.wait_ge(y_done, t)
                    sp.dma_start(flat(y_out[:, ds(t - 1, 1)]), y[:]).then_inc(stored, 16)
                sp.dma_start(x1[:], flat(x1_tiles[:, ds(t, 1)])).then_inc(x1_in, 16)

            over_tiles(sp, tile)
            for b in range(NS):
                if b >= 2:
                    sp.wait_ge(slots.dotted[(b - 2) % R], LAST + (b - 2) // R + 2)
                sp.dma_start(h2_s[:, b % 2], bcast(h2_d[SEQ + b:SEQ + b + 1, :], P)).then_inc(h2_s_in[b % 2], 16)
                if b == 1:
                    sp.wait_ge(y_done, NT)
                    sp.dma_start(y_out[:, NT - 1], y[:]).then_inc(stored, 16)
                    sp.dma_start(x1[0:NS], x1_d[SEQ:TOK, :]).then_inc(x1_in, 16)
            sp.wait_ge(y_done, NT + 1)
            sp.dma_start(outs[1].rearrange("b s d -> (b s) d"), y[0:NS]).then_inc(stored, 16)
            sp.wait_ge(stored, 16 * (NT + 1))

        @block.gpsimd
        def _(pool):
            nc.gpsimd.memset(eps[:], EPS).then_inc(const, 1)
            nc.gpsimd.memset(zero[:], 0.0).then_inc(const, 1)
            nc.gpsimd.memset(col[:], 0.0).then_inc(const, 1)
            picker.number(pool)

            def tile(t):
                lo = base if isinstance(t, int) and t == 0 else 0
                if not lo:
                    pool.wait_ge(picker.done, PH * t)
                    pool.sem_inc(carrier, 1)
                with pool.Fori(lo, ROUNDS) as i:
                    slots.gather_round(pool, t, i)

            over_tiles(pool, tile)
            pool.wait_ge(s_kept, 1)
            for b in range(NS):
                n, j = LAST + b // R, b % R
                pool.wait_ge(slots.dotted[j], n + 1)
                pool.wait_ge(slots.v_used[j], n + 1)
                slots.gather(pool, j, experts_s[:, b:b + 1])

        @block.vector
        def _(dve):
            picker.prepare(dve)

            def finish_tile(n, gain, t):
                c = Chain(dve, chain_v, 2 * t)
                dve.wait_ge(rooted, t + 1)
                c.link(nc.vector.reciprocal(stat[0:n, 2:3], stat[0:n, 1:2]))
                dve.wait_ge(x1_in, 16 * t + 16)
                c.link(nc.vector.scalar_tensor_tensor(y[0:n], y[0:n], stat[0:n, 2:3], gain[0:n], ALU.mult, ALU.mult))
                nc.vector.tensor_tensor(y[0:n], y[0:n], x1[0:n], ALU.add).then_inc(y_done, 1)

            def tile(t):
                dve.wait_ge(slots.h2_in, 16 * t + 16)
                dve.wait_ge(scores_in, 16 * t + 16)
                dve.sem_inc(carrier_v, 1)

                def picking(picks, i):
                    for h in picks[:-1]:
                        picker.pick(dve, h, t + 1, PH * t + h)
                        picker.gate(dve, h, t + 1, PH * t + h)
                    picker.pick(dve, picks[-1], t + 1, PH * t + picks[-1])
                    plain(i)
                    picker.gate(dve, picks[-1], t + 1, PH * t + picks[-1])

                def plain(i):
                    for j in range(R):
                        slots.dot(dve, ROUNDS * t + i, j, slots.h2[:])

                over_rounds(dve, t, picking, plain)
                for j in range(R):
                    dve.wait_ge(slots.dotted[j], ROUNDS * t + ROUNDS + 1)
                dve.sem_inc(tile_dotted, 1)
                if isinstance(t, int) and t == NT - 1:
                    dve.wait_ge(s_turned, 1)
                    nc.vector.tensor_copy(experts_s[:], psE[:, 0])
                    nc.vector.tensor_copy(gates_s[:], psE[:, 1]).then_inc(s_kept, 1)
                if isinstance(t, int) and t == 0:
                    dve.wait_ge(gain_in, 32)
                finish_tile(P, gain_p, t)

            over_tiles(dve, tile)
            for b in range(NS):
                dve.wait_ge(h2_s_in[b % 2], 16 * (b // 2 + 1))
                slots.dot(dve, LAST + b // R, b % R, h2_s[:, b % 2])
            finish_tile(NS, gain_s, NT)

        @block.scalar
        def _(act):
            def weigh(t, i, j):
                n = ROUNDS * t + i
                slots.activate(act, n, j)
                nc.scalar.activation(slots.weight[:, j:j + 1], slots.gelu[:, j:j + 1], ACT.Copy,
                                     scale=gates[:, t, ds(R * i + j, 1)]).then_inc(weight_set, 1)
                act.wait_ge(weight_set, R * (n - base) + j + 1)
                nc.scalar.activation(diag[:, j], ident[:], ACT.Copy, scale=slots.weight[:, j:j + 1])\
                    .then_inc(slots.weighted[j], 1)

            def norm(n, t):
                act.wait_ge(acc_full, t + 1)
                if not isinstance(t, int) or t:
                    act.wait_ge(stored, 16 * t)
                nc.scalar.copy(y[0:n], acc[0:n]).then_inc(squared, 1)
                nc.scalar.activation(acc[0:n], acc[0:n], ACT.Square, accum_out=stat[0:n, 0:1]).then_inc(squared, 1)
                act.wait_ge(squared, 2 * t + 2)
                nc.scalar.activation(stat[0:n, 1:2], stat[0:n, 0:1], ACT.Sqrt, bias=eps[0:n], scale=1.0 / D)\
                    .then_inc(rooted, 1)

            def tile(t):
                if not isinstance(t, int) or t:
                    act.wait_ge(picker.done, PH * t)
                    act.sem_inc(carrier_a, 1)

                def picking(picks, i):
                    for h in picks:
                        picker.exponentials(act, PH * t + h)
                    plain(i)

                def plain(i):
                    for j in range(R):
                        weigh(t, i, j)

                over_rounds(act, t, picking, plain)
                norm(P, t)

            act.wait_ge(const, 3)
            over_tiles(act, tile)
            act.wait_ge(s_kept, 1)
            for b in range(NS):
                n, j = LAST + b // R, b % R
                slots.activate(act, n, j)
                nc.scalar.activation(col[:, b, b:b + 1], slots.gelu[:, j:j + 1], ACT.Copy, scale=gates_s[:, b:b + 1])\
                    .then_inc(slots.weighted[j], 1)
            norm(NS, NT)

        @block.tensor
        def _(pe):
            pe.wait_ge(const, 3)

            def spread(lhsT, rows, **flags):
                for c in range(D // N):
                    last = nc.tensor.matmul(acc[:, c * N:(c + 1) * N], lhsT, rows[:, c * N:(c + 1) * N], **flags)
                return last

            def add(n):
                for j in range(R):
                    pe.wait_ge(slots.weighted[j], n + 1)
                    pe.wait_ge(slots.v_in[j], 16 * n + 16)
                    spread(diag[:, j], slots.v[:, j], start=False, stop=False).then_inc(slots.v_used[j], 1)

            def tile(t):
                if isinstance(t, int) and t == 0:
                    spread(ident[:], slots.sum, start=True, stop=False)
                else:
                    pe.wait_ge(rooted, t)
                    for c in range(D // N):
                        nc.tensor.matmul(acc[:, c * N:(c + 1) * N], zero[:, 0:P], zero[:], start=True, stop=False)
                over_rounds(pe, t, lambda picks, i: add(ROUNDS * t + i), lambda i: add(ROUNDS * t + i))
                for c in range(D // N):
                    last = nc.tensor.matmul(acc[:, c * N:(c + 1) * N], zero[:, 0:P], zero[:], start=False, stop=True)
                last.then_inc(acc_full, 1)

            over_tiles(pe, tile)
            pe.wait_ge(picker.done, PH * NT)
            nc.tensor.transpose(psE[:, 0], picker.rows[0:NS], ident[0:NS, 0:NS])
            nc.tensor.transpose(psE[:, 1], gates[0:NS, NT], ident[0:NS, 0:NS]).then_inc(s_turned, 1)
            pe.wait_ge(rooted, NT)
            for b in range(NS):
                n, j = LAST + b // R, b % R
                pe.wait_ge(slots.weighted[j], n + 1)
                pe.wait_ge(slots.v_in[j], 16 * n + 16)
                for c in range(D // N):
                    last = nc.tensor.matmul(acc[0:NS, c * N:(c + 1) * N], col[:, b], slots.v[:, j, c * N:(c + 1) * N],
                                            start=(b == 0), stop=(b == NS - 1))
                last.then_inc(slots.v_used[j], 1)
            for j in range(R):
                pe.wait_ge(slots.v_used[j], LAST + NS // R + 1)
            pe.sem_inc(acc_full, 1)


def program(nc, x_prompt, x_sample, c_prompt, c_sample, cache1, cache4, cache16, w_ada, b_ada, norm_g, w_in,
            gm_ln_g, gm_ln_b, w_s, b_s, w_out, w_q, sub_keys, expert_u, expert_v, outs):
    scratch = lambda name, shape: nc.dram_tensor(name, shape, F32, kind="Internal").ap()
    mods_d = scratch("mods_d", (ROWS, 6, D))
    proj_d = scratch("proj_d", (TOK, WIN))
    mix_d = scratch("mix_d", (TOK, D))
    x1_d = scratch("x1_d", (TOK, D))
    h2_d = scratch("h2_d", (TOK, D))
    scores_d = scratch("scores_d", (TOK, 2 * PH * NKEYS))
    with ExitStack() as ctx:
        ident = ctx.enter_context(nc.sbuf_tensor("ident", [P, P], F32))
        ident_made = nc.alloc_semaphore("ident_made")
        modulation_stage(nc, ident, ident_made, c_prompt, c_sample, w_ada, b_ada, norm_g, mods_d)
        buffer = lambda name, shape, dt=F32: ctx.enter_context(nc.sbuf_tensor(name, shape, dt))
        cache = (cache1, cache4, cache16)
        experts, gates = buffer("experts", [P, NT + 1, SLOTS], U32), buffer("gates", [P, NT + 1, SLOTS])
        projection_stage(nc, "proj1", FIRST, ident, x_prompt, x_sample, mods_d, w_in, proj_d)
        mixer_stage(nc, "mix1", FIRST, 1, ident, proj_d, cache, gm_ln_g, gm_ln_b, w_s, b_s, mix_d, outs)
        with nc.sbuf_tensor("hT1", [P, KD, width(FIRST)], F32) as hT:
            output_stage(nc, "out1", FIRST, ident, x_prompt, x_sample, mods_d, w_out, mix_d, hT, x1_d, h2_d)
            routing_stage(nc, "route1", FIRST, ident, w_q, sub_keys, hT, scores_d, experts, gates)
        slots = Slots(ctx, nc, ident, expert_u, expert_v, experts, gates, h2_d)
        slots.start()
        done = 0
        projection_stage(nc, "proj2", SECOND, ident, x_prompt, x_sample, mods_d, w_in, proj_d, slots, done)
        done += WIN // CK // 2
        mixer_stage(nc, "mix2", SECOND, NT, ident, proj_d, cache, gm_ln_g, gm_ln_b, w_s, b_s, mix_d, outs, slots, done)
        done += NT * HEADS // R
        with nc.sbuf_tensor("hT2", [P, KD, width(SECOND)], F32) as hT:
            output_stage(nc, "out2", SECOND, ident, x_prompt, x_sample, mods_d, w_out, mix_d, hT, x1_d, h2_d, slots, done)
            done += D // CK // 2
            routing_stage(nc, "route2", SECOND, ident, w_q, sub_keys, hT, scores_d, experts, gates, slots, done)
            done += D // CK // 2
        expert_stage(nc, ident, mods_d, x1_d, h2_d, scores_d, slots, done, experts, gates, outs)


_INS = ['x_prompt', 'x_sample', 'c_prompt', 'c_sample', 'cache_kv_dil1', 'cache_kv_dil4', 'cache_kv_dil16', 'w_ada',
        'b_ada', 'norm_g', 'w_in', 'gm_ln_g', 'gm_ln_b', 'w_s', 'b_s', 'w_out', 'w_q', 'sub_keys', 'expert_u', 'expert_v']
_OUTS = [(1, SEQ, D), (NS, 1, D)] + [(1, 1, min(w, SEQ), 2, HEADS, HD) for w, _ in WINDOWS] \
    + [(1, NS, 1, 2, HEADS, HD)] * 3 + [(1, NS, 1, GM_HEADS, GM // GM_HEADS)]


def kernel(**inputs):
    import concourse.bacc as _bacc
    from concourse.bass_utils import run_bass_kernel_spmd as _run

    nc = _bacc.Bacc("TRN2", target_bir_lowering=False, num_devices=1)
    arrays, args = {}, []
    for name in _INS:
        a = np.ascontiguousarray(inputs[name])
        arrays[f"in_{name}_dram"] = a
        args.append(nc.dram_tensor(f"in_{name}_dram", a.shape, mybir.dt.from_np(a.dtype), kind="ExternalInput").ap())
    outs = [nc.dram_tensor(f"out_{i}_dram", shape, F32, kind="ExternalOutput").ap() for i, shape in enumerate(_OUTS)]
    program(nc, *args, outs)
    r = _run(nc, [arrays], core_ids=[0])
    return tuple(r.results[0][f"out_{i}_dram"] for i in range(len(_OUTS)))
```

```python
from contextlib import ExitStack

import numpy as np

import concourse.bass as bass
from concourse import mybir

ALU = mybir.AluOpType
ACT = mybir.ActivationFunctionType
F32 = mybir.dt.float32
U32 = mybir.dt.uint32
AX_X = mybir.AxisListType.X
ds = bass.ds

P = 128
D = 2048
KD = D // P
SEQ = 512
NT = SEQ // P
NS = 8
TOK = SEQ + NS
FIRST = ((0, P, 0), (SEQ, NS, P))
SECOND = tuple((t * P, P, (t - 1) * P) for t in range(1, NT))
ROWS = NS + 1
HD, HEADS, GROUPS = 64, 8, 3
GW = HEADS * HD
ATT = GROUPS * GW
GM_HEADS, GM = 4, 512
WIN = 3 * ATT + 2 * GM
WINDOWS = ((128, 1), (512, 4), (2048, 16))
REACH = 128
PH, TOPK, NKEYS = 8, 16, 128
SLOTS = PH * TOPK
CK = 256
R = 4
ROUNDS = SLOTS // R
EPS = 1e-6
NEG = -1e30
SH1, SC1, GT1, SH2, SC2, GT2 = range(6)


class Stage:

    def __init__(self, nc, name):
        self.nc, self.name, self.ctx, self.sems = nc, name, ExitStack(), []

    def __enter__(self):
        return self

    def __exit__(self, *failure):
        if failure[0] is None:
            self.ctx.close()
            self.nc.clear_and_free_semaphores(self.sems)
            self.nc.all_engine_barrier()

    def sb(self, name, shape, dt=F32):
        return self.ctx.enter_context(self.nc.sbuf_tensor(f"{self.name}_{name}", shape, dt))

    def ps(self, name, shape, dt=F32):
        return self.ctx.enter_context(self.nc.psum_tensor(f"{self.name}_{name}", shape, dt))

    def sem(self, name):
        self.sems.append(self.nc.alloc_semaphore(f"{self.name}_{name}"))
        return self.sems[-1]

    def pair(self, name):
        return [self.sem(f"{name}{j}") for j in range(2)]

    def block(self):
        return self.ctx.enter_context(self.nc.Block())


class Chain:

    def __init__(self, eng, sem, base=0):
        self.eng, self.sem, self.base, self.n = eng, sem, base, 0

    def link(self, ins):
        ins.then_inc(self.sem, 1)
        self.n += 1
        self.eng.wait_ge(self.sem, self.base + self.n)


def repeat(eng, count, body):
    body(0)
    if count > 1:
        with eng.Fori(1, count) as i:
            body(i)


def after(eng, sem, value):
    if not isinstance(value, int) or value > 0:
        eng.wait_ge(sem, value)


def flat(ap):
    return ap.rearrange("p a d -> p (a d)")


def of_tile(buffer, t, cols):
    return flat(buffer[:, ds(t, 1), cols])


def identity(nc, pool, ident, made):
    nc.gpsimd.memset(ident[:], 0.0).then_inc(made, 1)
    pool.wait_ge(made, 1)
    nc.gpsimd.affine_select(out=ident[:], in_=ident[:], compare_op=ALU.not_equal, fill=1.0, base=0,
                            pattern=[[-1, P]], channel_multiplier=1).then_inc(made, 1)


def modulation_stage(nc, ident, ident_made, c_prompt, c_sample, w_ada, b_ada, norm_g, mods_d):
    N = 512
    CHUNKS = 6 * D // N
    w_view = w_ada[0].rearrange("(k p) n -> p k n", p=P)
    b_row = b_ada[0:1, :]
    with Stage(nc, "ada") as m:
        cond = m.sb("cond", [ROWS, D])
        act_c = m.sb("act_c", [ROWS, D])
        condT = m.sb("condT", [P, KD, ROWS])
        w = m.sb("w", [P, 2, KD, N])
        bias = m.sb("bias", [ROWS, 2, N])
        gains = m.sb("gains", [ROWS, 4, D])
        mods = m.sb("mods", [ROWS, 6, D])
        mods_flat = mods[:].rearrange("r s n -> r (s n)")
        psT = m.ps("psT", [P, KD, ROWS])
        acc = [m.ps(f"acc{j}", [P, N]) for j in range(2)]
        c_in, g_in = m.sem("c_in"), m.sem("g_in")
        silu_done, turned, condT_ready = m.sem("silu_done"), m.sem("turned"), m.sem("condT_ready")
        w_in = [m.sem(f"w_in{j}") for j in range(2)]
        bias_in = [m.sem(f"bias_in{j}") for j in range(2)]
        chunk_done = [m.sem(f"chunk_done{j}") for j in range(2)]
        biased = [m.sem(f"biased{j}") for j in range(2)]
        folded, stored = m.sem("folded"), m.sem("stored")
        block = m.block()

        @block.sync
        def _(sp):
            sp.dma_start(cond[0:NS, :], c_sample[:, :]).then_inc(c_in, 16)
            sp.dma_start(cond[NS:ROWS, :], c_prompt[:, :]).then_inc(c_in, 16)
            def chunk_pair(i):
                for j in range(2):
                    after(sp, chunk_done[j], i)
                    sp.dma_start(w[:, j], w_view[:, :, ds((2 * i + j) * N, N)]).then_inc(w_in[j], 16)
                    after(sp, biased[j], i)
                    sp.dma_start(bias[:, j], bcast(b_row[:, ds((2 * i + j) * N, N)], ROWS)).then_inc(bias_in[j], 16)

            repeat(sp, CHUNKS // 2, chunk_pair)
            sp.wait_ge(folded, 4)
            sp.dma_start(mods_d.rearrange("r s n -> r (s n)"), mods_flat).then_inc(stored, 16)
            sp.wait_ge(stored, 16)

        @block.gpsimd
        def _(pool):
            pool.dma_start(gains[:].rearrange("r s n -> r (s n)"),
                           bcast(norm_g.rearrange("a s n -> a (s n)"), ROWS)).then_inc(g_in, 16)
            identity(nc, pool, ident, ident_made)

        @block.scalar
        def _(act):
            act.wait_ge(c_in, 32)
            nc.scalar.activation(act_c[:], cond[:], ACT.Silu).then_inc(silu_done, 1)

        @block.tensor
        def _(pe):
            pe.wait_ge(ident_made, 2)
            pe.wait_ge(silu_done, 1)
            for k in range(KD):
                last = nc.tensor.transpose(psT[:, k, :], act_c[:, k * P:(k + 1) * P], ident[0:ROWS, 0:ROWS])
            last.then_inc(turned, 1)
            pe.wait_ge(condT_ready, 1)
            def chunk_pair(i):
                for j in range(2):
                    pe.wait_ge(w_in[j], 16 * i + 16)
                    after(pe, biased[j], i)
                    for k in range(KD):
                        last = nc.tensor.matmul(acc[j][0:ROWS, :], condT[:, k, :], w[:, j, k, :],
                                                start=(k == 0), stop=(k == KD - 1))
                    last.then_inc(chunk_done[j], 1)

            repeat(pe, CHUNKS // 2, chunk_pair)
        @block.vector
        def _(dve):
            dve.wait_ge(turned, 1)
            nc.vector.tensor_copy(condT[:], psT[:]).then_inc(condT_ready, 1)
            def chunk_pair(i):
                for j in range(2):
                    dve.wait_ge(chunk_done[j], i + 1)
                    dve.wait_ge(bias_in[j], 16 * i + 16)
                    nc.vector.tensor_tensor(mods_flat[:, ds((2 * i + j) * N, N)], acc[j][0:ROWS, :], bias[:, j],
                                            ALU.add).then_inc(biased[j], 1)

            repeat(dve, CHUNKS // 2, chunk_pair)
            dve.wait_ge(g_in, 16)
            for j in range(2):
                dve.wait_ge(biased[j], CHUNKS // 2)
            for scale, g in ((SC1, 0), (SC2, 2)):
                nc.vector.scalar_tensor_tensor(mods[:, scale], mods[:, scale], 1.0, gains[:, g], ALU.add,
                                               ALU.mult).then_inc(folded, 1)
            for gate, g in ((GT1, 1), (GT2, 3)):
                nc.vector.tensor_tensor(mods[:, gate], mods[:, gate], gains[:, g], ALU.mult).then_inc(folded, 1)


def bcast(row, n):
    return row.to_broadcast([n, row.shape[1]])


def load_mods(eng, mods_d, section, vectors, landed):
    eng.dma_start(vectors[0][:], bcast(mods_d[NS:ROWS, section, :], P)).then_inc(landed, 16)
    for v in vectors[1:]:
        eng.dma_start(v[:], mods_d[0:NS, section, :]).then_inc(landed, 16)


def turn(nc, pe, src, n, psT, ident, psT_free, turned, done):
    for q in range(4):
        if done + q >= 3:
            pe.wait_ge(psT_free, done + q - 2)
        for b in range(4):
            k = 4 * q + b
            last = nc.tensor.transpose(psT[:, (done + q) % 3, b, 0:n], src[0:n, k * P:(k + 1) * P], ident[0:n, 0:n])
        last.then_inc(turned, 1)


def width(tiles):
    return sum(n for _, n, _ in tiles)


def rows_of(tiles, prompt, sample):
    return [prompt[at:at + n, :] if at < SEQ else sample for at, n, _ in tiles]


class TurnedProduct:

    def __init__(self, m, nc, ident, tiles, hT, w):
        self.nc, self.ident, self.tiles, self.hT, self.w, self.W = nc, ident, tiles, hT, w, width(tiles)
        self.acc = [m.ps(f"product_acc{b}", [P, 512]) for b in range(2)]
        self.back = [m.ps(f"product_back{b}", [P, len(tiles), P]) for b in range(2)]
        self.colT = m.sb("colT", [P, 2, self.W])
        self.full, self.copied, self.turned, self.used = (m.pair(f"product_{s}") for s in (
            "full", "copied", "turned", "used"))

    def multiply(self, pe, c, j):
        for b in range(2):
            after(pe, self.copied[b], c)
            for k in range(KD):
                last = self.nc.tensor.matmul(self.acc[b][:, 0:self.W], self.w[:, j, k, b * P:(b + 1) * P],
                                             self.hT[:, k, :], start=(k == 0), stop=(k == KD - 1))
            last.then_inc(self.full[b], 1)
            if b:
                self.turn_back(pe, c, 0)
            elif not isinstance(c, int) or c:
                self.turn_back(pe, c - 1, 1)

    def turn_back(self, pe, c, b):
        pe.wait_ge(self.copied[b], c + 1)
        after(pe, self.used[b], c)
        for t, (_, n, col) in enumerate(self.tiles):
            last = self.nc.tensor.transpose(self.back[b][0:n, t], self.colT[:, b, col:col + n], self.ident[:])
        last.then_inc(self.turned[b], 1)

    def copy(self, act, c):
        for b in range(2):
            act.wait_ge(self.full[b], c + 1)
            after(act, self.turned[b], c)
            self.nc.scalar.copy(self.colT[:, b], self.acc[b][:, 0:self.W]).then_inc(self.copied[b], 1)

    def place(self, dve, c, place_of):
        for b in range(2):
            dve.wait_ge(self.turned[b], c + 1)
            for t, (_, n, _) in enumerate(self.tiles):
                last = self.nc.vector.tensor_copy(place_of(t, b), self.back[b][0:n, t])
            last.then_inc(self.used[b], 1)

    def wait_for(self, eng, sems, c):
        for b in range(2):
            after(eng, sems[b], c)


def projection_stage(nc, name, tiles, ident, x_prompt, x_sample, mods_d, w_in, proj_d, slots=None, scores_d=None):
    CHUNKS = WIN // CK
    NTL = len(tiles)
    w_view = w_in[0].rearrange("(k p) n -> p k n", p=P)
    x_rows = rows_of(tiles, x_prompt[0], x_sample.rearrange("b s d -> (b s) d"))
    proj_rows = rows_of(tiles, proj_d, proj_d[SEQ:TOK, :])
    with Stage(nc, name) as m:
        x = m.sb("x", [P, 2, D])
        sq = m.sb("sq", [P, D])
        kinds = [P, NS] if tiles[-1][1] == NS else [P]
        scale = [m.sb(f"scale{n}", [n, D]) for n in kinds]
        shift = [m.sb(f"shift{n}", [n, D]) for n in kinds]
        stat = m.sb("stat", [P, 3, NTL])
        eps = m.sb("eps", [P, 1])
        hT = m.sb("hT", [P, KD, width(tiles)])
        w = m.sb("w", [P, 2, KD, CK])
        out = m.sb("out", [P, 2, NTL, CK])
        psT = m.ps("psT", [P, 3, 4, P])
        product = TurnedProduct(m, nc, ident, tiles, hT, w) if len(kinds) == 2 else None
        acc = [] if product else [m.ps(f"acc{t}", [P, 512]) for t in range(NTL)]
        mod_in, eps_set, squared, rooted, inverse, scaled, shifted, turned, psT_free = (m.sem(s) for s in (
            "mod_in", "eps_set", "squared", "rooted", "inverse", "scaled", "shifted", "turned", "psT_free"))
        x_in, w_ready, acc_full, out_full, stored = (m.pair(s) for s in ("x_in", "w_ready", "acc_full", "out_full", "stored"))
        if slots:
            scores = m.sb("scores", [P, 2 * PH, NKEYS])
            picker = Picker(m, nc, scores, slots.experts, slots.gates)
            scores_in, sum_zeroed = m.sem("scores_in"), m.sem("sum_zeroed")
        block = m.block()

        @block.sync
        def _(sp):
            for t, (at, n, _) in enumerate(tiles):
                if t >= 2:
                    sp.wait_ge(turned, 4 * (t - 1))
                sp.dma_start(x[0:n, t % 2], x_rows[t]).then_inc(x_in[t % 2], 16)
                if t == 0:
                    for section, vectors in ((SC1, scale), (SH1, shift)):
                        load_mods(sp, mods_d, section, vectors, mod_in)

            def load(j, c):
                sp.dma_start(w[:, j], w_view[:, :, ds(c * CK, CK)]).then_inc(w_ready[j], 16)

            def store(j, i):
                if product:
                    product.wait_for(sp, product.used, 2 * i + j + 1)
                else:
                    sp.wait_ge(out_full[j], NTL * i + NTL)
                for t, (at, n, _) in enumerate(tiles):
                    sp.dma_start(proj_rows[t][:, ds((2 * i + j) * CK, CK)], out[0:n, j, t]).then_inc(stored[j], 16)

            load(0, 0)
            load(1, 1)
            if slots:
                sp.dma_start(scores[:].rearrange("p s k -> p (s k)"), scores_d[0:P, :]).then_inc(scores_in, 16)
                sp.dma_start(slots.h2[:], slots.h2_d[0:P, :]).then_inc(slots.h2_in, 16)
            with sp.Fori(0, CHUNKS // 2 - 1) as i:
                for j in range(2):
                    if product:
                        product.wait_for(sp, product.full, 2 * i + j + 1)
                    else:
                        sp.wait_ge(acc_full[j], NTL * i + NTL)
                    load(j, 2 * i + j + 2)
                    store(j, i)
            for j in range(2):
                store(j, CHUNKS // 2 - 1)
            for j in range(2):
                sp.wait_ge(stored[j], 16 * NTL * CHUNKS // 2)

        @block.gpsimd
        def _(pool):
            nc.gpsimd.memset(eps[:], EPS).then_inc(eps_set, 1)
            if not slots:
                return
            picker.number(pool)
            with pool.Fori(0, PH) as i:
                pool.wait_ge(picker.done, i + 1)
                slots.gather_round(pool, 0, i)
            with pool.Fori(PH, CHUNKS // 2 + 1) as i:
                slots.gather_round(pool, 0, i)

        @block.scalar
        def _(act):
            act.wait_ge(eps_set, 1)
            for t, (at, n, c) in enumerate(tiles):
                act.wait_ge(x_in[t % 2], 16 * (t // 2 + 1))
                if t:
                    act.wait_ge(squared, t)
                nc.scalar.activation(sq[0:n, :], x[0:n, t % 2], ACT.Square,
                                     accum_out=stat[0:n, 0, t:t + 1]).then_inc(squared, 1)
                act.wait_ge(squared, t + 1)
                nc.scalar.activation(stat[0:n, 1, t:t + 1], stat[0:n, 0, t:t + 1], ACT.Sqrt, bias=eps[0:n, :],
                                     scale=1.0 / D).then_inc(rooted, 1)
                for q in range(4):
                    act.wait_ge(turned, 4 * t + q + 1)
                    nc.scalar.copy(hT[:, 4 * q:4 * q + 4, c:c + n], psT[:, (4 * t + q) % 3, :, 0:n])\
                        .then_inc(psT_free, 1)

            def chunk_pair(i):
                for j in range(2):
                    if product:
                        product.copy(act, 2 * i + j)
                        continue
                    if slots:
                        for k in range(R // 2):
                            slots.weigh(act, i, R // 2 * j + k)
                    after(act, stored[j], 16 * NTL * i)
                    for t, (at, n, _) in enumerate(tiles):
                        act.wait_ge(acc_full[j], NTL * i + t + 1)
                        nc.scalar.copy(out[0:n, j, t], acc[t][0:n, 0:CK]).then_inc(out_full[j], 1)

            def picking_pair(i):
                picker.exponentials(act, i + 1)
                act.wait_ge(picker.done, i + 1)
                chunk_pair(i)

            if slots:
                picker.exponentials(act, 0)
                repeat(act, PH - 1, picking_pair)
                act.wait_ge(picker.done, PH)
                with act.Fori(PH - 1, CHUNKS // 2) as i:
                    chunk_pair(i)
            else:
                repeat(act, CHUNKS // 2, chunk_pair)

        @block.vector
        def _(dve):
            for t, (at, n, _) in enumerate(tiles):
                dve.wait_ge(rooted, t + 1)
                nc.vector.reciprocal(stat[0:n, 2, t:t + 1], stat[0:n, 1, t:t + 1]).then_inc(inverse, 1)
                dve.wait_ge(inverse, t + 1)
                if t == 0:
                    dve.wait_ge(mod_in, 32 * len(scale))
                xt = x[0:n, t % 2]
                s = len(scale) - 1 if n == NS else 0
                nc.vector.scalar_tensor_tensor(xt, xt, stat[0:n, 2, t:t + 1], scale[s][0:n, :], ALU.mult,
                                               ALU.mult).then_inc(scaled, 1)
                dve.wait_ge(scaled, t + 1)
                nc.vector.tensor_tensor(xt, xt, shift[s][0:n, :], ALU.add).then_inc(shifted, 1)

            def chunk_pair(i):
                for j in range(2):
                    after(dve, stored[j], 16 * NTL * i)
                    product.place(dve, 2 * i + j, lambda t, b: out[0:tiles[t][1], j, t, b * P:(b + 1) * P])

            if product:
                repeat(dve, CHUNKS // 2, chunk_pair)
            if not slots:
                return

            def pick(h):
                picker.pick(dve, h, 0, h)
                picker.gate(dve, h, 0, h)

            nc.vector.memset(slots.sum[:], 0.0).then_inc(sum_zeroed, 1)
            dve.wait_ge(sum_zeroed, 1)
            for j in range(R):
                dve.sem_inc(slots.dotted[j], 1)
                dve.sem_inc(slots.v_used[j], 1)
            picker.prepare(dve)
            dve.wait_ge(scores_in, 16)
            dve.wait_ge(slots.h2_in, 16)
            pick(0)
            with dve.Fori(0, PH - 1) as i:
                pick(i + 1)
                slots.sum_round(dve, i)
            with dve.Fori(PH - 1, CHUNKS // 2) as i:
                slots.sum_round(dve, i)

        @block.tensor
        def _(pe):
            for t, (at, n, _) in enumerate(tiles):
                pe.wait_ge(shifted, t + 1)
                turn(nc, pe, x[:, t % 2], n, psT, ident, psT_free, turned, 4 * t)
            pe.wait_ge(psT_free, 4 * NTL)

            def chunk_pair(i):
                for j in range(2):
                    pe.wait_ge(w_ready[j], 16 * i + 16)
                    if product:
                        product.multiply(pe, 2 * i + j, j)
                        continue
                    after(pe, out_full[1 - j], NTL * (i + j))
                    for t, (at, n, c) in enumerate(tiles):
                        for k in range(KD):
                            last = nc.tensor.matmul(acc[t][0:n, 0:CK], hT[:, k, c:c + n], w[:, j, k, :],
                                                    start=(k == 0), stop=(k == KD - 1))
                        last.then_inc(acc_full[j], 1)

            repeat(pe, CHUNKS // 2, chunk_pair)
            if product:
                product.turn_back(pe, CHUNKS - 1, 1)


class Slots:

    def __init__(self, ctx, nc, ident, expert_u, expert_v, experts, gates, h2_d):
        self.nc, self.ident, self.experts, self.gates, self.h2_d = nc, ident, experts, gates, h2_d
        buffer = lambda name, shape, dt=F32: ctx.enter_context(nc.sbuf_tensor(f"slots_{name}", shape, dt))
        semaphore = lambda name: nc.alloc_semaphore(f"slots_{name}")
        self.U, self.V = expert_u[0], expert_v[0]
        self.u, self.v = buffer("u", [P, R, D]), buffer("v", [P, R, D])
        self.h2, self.sum = buffer("h2", [P, D]), buffer("sum", [P, D])
        self.row_ids = buffer("row_ids", [P, R, 1], U32)
        self.dots, self.gelu, self.weight = (buffer(s, [P, R]) for s in ("dots", "gelu", "weight"))
        each = lambda s: [semaphore(f"{s}{j}") for j in range(R)]
        self.u_in, self.v_in, self.weighted = each("u_in"), each("v_in"), each("weighted")
        self.dotted, self.v_used = each("dotted"), each("v_used")
        self.ids_set, self.carrier, self.gelued, self.h2_in = (semaphore(s) for s in ("ids_set", "carrier", "gelued", "h2_in"))

    def gather(self, pool, j, ids):
        at = bass.IndirectOffsetOnAxis(ap=ids, axis=0)
        pool.indirect_dma_start(self.u[:, j], None, self.U, at).then_inc(self.u_in[j], 16)
        pool.indirect_dma_start(self.v[:, j], None, self.V, at).then_inc(self.v_in[j], 16)

    def gather_round(self, pool, t, i):
        n = ROUNDS * t + i
        for j in range(R):
            pool.wait_ge(self.dotted[j], n + 1)
            pool.wait_ge(self.v_used[j], n + 1)
            self.nc.gpsimd.tensor_copy(self.row_ids[:, j], self.experts[:, t, ds(R * i + j, 1)])\
                .then_inc(self.ids_set, 1)
            pool.wait_ge(self.ids_set, R * n + j + 1)
            pool.sem_inc(self.carrier, 1)
            self.gather(pool, j, self.row_ids[:, j])

    def dot(self, dve, n, j, h2):
        dve.wait_ge(self.u_in[j], 16 * n + 16)
        u = self.u[:, j]
        self.nc.vector.tensor_tensor_reduce(u, u, h2, 1.0, 0.0, ALU.mult, ALU.add, self.dots[:, j:j + 1])\
            .then_inc(self.dotted[j], 1)

    def activate(self, act, n, j):
        act.wait_ge(self.dotted[j], n + 2)
        self.nc.scalar.activation(self.gelu[:, j:j + 1], self.dots[:, j:j + 1], ACT.Gelu_apprx_tanh)\
            .then_inc(self.gelued, 1)
        act.wait_ge(self.gelued, R * n + j + 1)

    def weigh(self, act, n, j):
        self.activate(act, n, j)
        self.nc.scalar.activation(self.weight[:, j:j + 1], self.gelu[:, j:j + 1], ACT.Copy,
                                  scale=self.gates[:, 0, ds(R * n + j, 1)]).then_inc(self.weighted[j], 1)

    def add(self, dve, n, j):
        dve.wait_ge(self.weighted[j], n + 1)
        dve.wait_ge(self.v_in[j], 16 * n + 16)
        dve.wait_ge(self.v_used[j - 1], n + 2 if j else n + 1)
        self.nc.vector.scalar_tensor_tensor(self.sum[:], self.v[:, j], self.weight[:, j:j + 1], self.sum[:],
                                            ALU.mult, ALU.add).then_inc(self.v_used[j], 1)

    def sum_round(self, dve, n):
        self.dot(dve, n, 0, self.h2[:])
        for j in range(R):
            if j + 1 < R:
                self.dot(dve, n, j + 1, self.h2[:])
            self.add(dve, n, j)


def mixer_stage(nc, name, tiles, F, ident, proj_d, cache, gm_ln_g, gm_ln_b, w_s, b_s, mix_d, outs, slots=None, base=0):
    at_prompt = tiles[0][0]
    fold = proj_d[0:F * P, :].rearrange("(i r) c -> i r c", r=F)
    mix_fold = mix_d[0:F * P, :].rearrange("(i r) c -> i r c", r=F)
    samples = tiles[-1][1] == NS
    FROM = at_prompt // F
    BLOCKS, NEAR = F + 2, F * P
    KEYS = BLOCKS * P
    PAIRS = GW // P
    NQ, NK = GROUPS * PAIRS, (GROUPS - 1) * PAIRS
    TURNS = (NQ + NK) // 4
    SCALE = HD ** -0.5
    LINKS = 5
    K_LOADS, V_LOADS = 16 * (GROUPS + 3), 16 * (GROUPS + 1)
    V0 = 2 * ATT
    NTL = len(tiles)
    PROMPTS = NTL - samples
    round_of = lambda r, h: HEADS // R * r + (base + h // R)
    lag = lambda h: (2, 2, 5)[h] if h < 3 else 3
    with Stage(nc, name) as m:
        k0n = m.sb("k0n", [P, F, GW])
        v = m.sb("v", [P, F, ATT])
        qkn = m.sb("qkn", [P, (NQ + NK) * P])
        kT0 = m.sb("kT0", [P, PAIRS, F, P])
        qkT = m.sb("qkT", [P, NQ + NK, P])
        near, far = m.sb("near", [P, F, F, P]), m.sb("far", [P, F, 2, P])
        steps = m.sb("steps", [P, 3, P], mybir.dt.int32)
        off = m.sb("off", [P, 2, P])
        scores = m.sb("scores", [P, 3, KEYS])
        probsT = m.sb("probsT", [P, 2, BLOCKS, P])
        top, den, inv = m.sb("top", [P, HEADS]), m.sb("den", [P, HEADS]), m.sb("inv", [P, HEADS])
        att = m.sb("att", [P, GROUPS, HEADS, HD])
        gin = m.sb("gin", [P, 2, 2 * GM])
        gsq = m.sb("gsq", [P, GM])
        gst = m.sb("gst", [P, 3, GM_HEADS])
        gain, shift = m.sb("gain", [P, GM]), m.sb("shift", [P, GM])
        wn, wT = m.sb("wn", [P, GM_HEADS, P]), m.sb("wT", [P, GM_HEADS, P])
        bn, bT = m.sb("bn", [GM_HEADS, P]), m.sb("bT", [P, GM_HEADS])
        w00, b00 = m.sb("w00", [NS, GM_HEADS, 1]), m.sb("b00", [NS, GM_HEADS, 1])
        gout = m.sb("gout", [P, GM])
        eps = m.sb("eps", [P, 1])
        if samples:
            k_s, v_s = m.sb("k_s", [P, 2, GROUPS, GW]), m.sb("v_s", [P, 2, GROUPS, GW])
            qb = m.sb("qb", [P, 2, ATT])
            own = m.sb("own", [HEADS, 2, 3, GROUPS, HD])
            prod = m.sb("prod", [P, 2, ATT])
            s24 = m.sb("s24", [P, 2, GROUPS, HEADS])
            srow = m.sb("srow", [HEADS, 2, GROUPS, P + 1])
            oprod = m.sb("oprod", [HEADS, 2, GROUPS, HD])
            oself = m.sb("oself", [HEADS, 2, GROUPS, 1])
            sst = m.sb("sst", [HEADS, 2, 3])
            pT = m.sb("pT", [P, 2, GROUPS, HEADS])
            spread = m.sb("spread", [HEADS, 2, GROUPS, HEADS, HD])
            arow = m.sb("arow", [1, ATT])
        ones = m.sb("ones", [P, 1])

        psS = m.ps("psS", [P, 4, 512])
        psP = m.ps("psP", [P, 2, 512])
        psO = m.ps("psO", [P, 2, 512])
        psP_flat = psP[:].rearrange("p a k -> p (a k)")

        S = {n: m.sem(n) for n in (
            "k0_in", "v_in", "g_masked", "w_turned", "qk_in", "kept", "g_const", "masks", "mchain", "x_full", "x_free",
            "scored", "masked", "maxed", "exped", "p_turned", "p_copied", "mixed", "inverted", "normalised", "att_stored",
            "gelued", "gchain", "g_var", "g_root", "g_normed", "z_done", "g_out", "g_stored", "gv_stored",
            "schain", "s_scored", "s_turned", "s_max", "s_exp", "s_probs", "s_probs_v", "s_pT", "s_pT_copied", "s_spread", "s_mixed",
            "s_k_used", "s_v_used", "s_row", "s_stored", "s_seen")}
        g_in, sk_in, sv_in = m.pair("g_in"), m.pair("sk_in"), m.pair("sv_in")
        block = m.block()

        def last_of(t):
            return (t // 2 + 1) * 16

        @block.sync
        def _(sp):
            sp.dma_start(k0n[:], fold[:, :, ATT:ATT + GW]).then_inc(S["k0_in"], 16)
            for t in range(2):
                at, n, _ = tiles[t]
                sp.dma_start(gin[0:n, t], proj_d[at:at + n, 3 * ATT:WIN]).then_inc(g_in[t], 16)
            sp.dma_start(wn[:], w_s[0].rearrange("h q p -> q h p")).then_inc(S["g_const"], 16)
            sp.dma_start(bn[:], b_s[0]).then_inc(S["g_const"], 16)
            sp.dma_start(gain[:], bcast(gm_ln_g.rearrange("a h c -> a (h c)"), P)).then_inc(S["g_const"], 16)
            sp.dma_start(shift[:], bcast(gm_ln_b.rearrange("a h c -> a (h c)"), P)).then_inc(S["g_const"], 16)
            with nc.allow_non_contiguous_dma(reason="four weights of one position"):
                for h in range(GM_HEADS):
                    sp.dma_start(w00[:, h, :], bcast(w_s[0, h, 0:1, 0:1], NS)).then_inc(S["g_const"], 16)
                    sp.dma_start(b00[:, h, :], bcast(b_s[0, h:h + 1, 0:1], NS)).then_inc(S["g_const"], 16)
            sp.dma_start(v[:], fold[:, :, V0:V0 + ATT]).then_inc(S["v_in"], 16)
            for t, (at, n, _) in enumerate(tiles[2:], 2):
                sp.wait_ge(S["g_out"], t - 1)
                sp.dma_start(gin[0:n, t % 2], proj_d[at:at + n, 3 * ATT:WIN]).then_inc(g_in[t % 2], 16)

            def load_qk(r):
                if not isinstance(r, int):
                    sp.wait_ge(S["x_full"], F + 1 + TURNS * r)
                sp.dma_start(qkn[:, 0:ATT], flat(fold[:, ds(r, 1), 0:ATT])).then_inc(S["qk_in"], 16)
                sp.dma_start(qkn[:, ATT:], flat(fold[:, ds(r, 1), ATT + GW:2 * ATT])).then_inc(S["qk_in"], 16)

            repeat(sp, F, load_qk)

            def load_sample(i):
                for j in range(2):
                    b = 2 * i + j
                    row = proj_d[ds(b + SEQ, 1), :]
                    cached = [cache[g][0, ds(b, 1)].rearrange("a (j s) c h d -> (a j) s c (h d)", s=dil)[:, 0]
                              for g, (win, dil) in enumerate(WINDOWS)]
                    ours = lambda c: row[:, c * ATT:(c + 1) * ATT].rearrange("a (g h d) -> (a h) g d", g=GROUPS, h=HEADS)
                    after(sp, S["s_k_used"], b - 1)
                    for g in range(GROUPS):
                        sp.dma_start(k_s[:, j, g], cached[g][:, 0]).then_inc(sk_in[j], 16)
                    sp.dma_start(qb[:, j], bcast(row[:, 0:ATT], P)).then_inc(sk_in[j], 16)
                    for c in range(2):
                        sp.dma_start(own[:, j, c], ours(c)).then_inc(sk_in[j], 16)
                    after(sp, S["s_v_used"], b - 1)
                    for g in range(GROUPS):
                        sp.dma_start(v_s[:, j, g], cached[g][:, 1]).then_inc(sv_in[j], 16)
                    sp.dma_start(own[:, j, 2], ours(2)).then_inc(sv_in[j], 16)

            if samples:
                repeat(sp, NS // 2, load_sample)
            n = 0
            for g, (win, dil) in enumerate(WINDOWS):
                keep = min(win, SEQ)
                for c in range(2):
                    src = proj_d[:, (1 + c) * ATT + g * GW:(1 + c) * ATT + (g + 1) * GW]
                    if samples:
                        sp.dma_start(outs[5 + g][0, :, 0, c].rearrange("s h d -> s (h d)"), src[SEQ:TOK])\
                          .then_inc(S["kept"], 16)
                    else:
                        sp.dma_start(outs[2 + g][0, 0, :, c].rearrange("s h d -> s (h d)"), src[SEQ - keep:SEQ])\
                          .then_inc(S["kept"], 16)
                    n += 1
            sp.wait_ge(S["kept"], 16 * n)
            sp.wait_ge(S["g_stored"], 16 * NTL)
            if samples:
                sp.wait_ge(S["gv_stored"], 16)

        @block.gpsimd
        def _(pool):
            pool.wait_ge(S["g_const"], 16 * (4 + 2 * GM_HEADS))
            nc.gpsimd.affine_select(out=wn[:], in_=wn[:], compare_op=ALU.is_ge, fill=0.0, base=0,
                                    pattern=[[0, GM_HEADS], [-1, P]], channel_multiplier=1).then_inc(S["g_masked"], 1)
            chain = Chain(pool, S["masks"])
            chain.link(nc.gpsimd.memset(near[:], 0.0))
            chain.link(nc.gpsimd.memset(far[:], 0.0))
            chain.link(nc.gpsimd.memset(eps[:], EPS))
            chain.link(nc.gpsimd.memset(ones[:], 1.0))
            chain.link(nc.gpsimd.affine_select(out=near[:], in_=near[:], compare_op=ALU.is_ge, fill=NEG, base=0,
                                               pattern=[[1, F], [-1, F], [-F, P]], channel_multiplier=F))
            chain.link(nc.gpsimd.affine_select(out=near[:], in_=near[:], compare_op=ALU.is_ge, fill=NEG, base=REACH,
                                               pattern=[[-1, F], [1, F], [F, P]], channel_multiplier=-F))
            chain.link(nc.gpsimd.affine_select(out=far[:], in_=far[:], compare_op=ALU.is_ge, fill=NEG, base=0,
                                               pattern=[[0, F], [0, 2], [-1, P]], channel_multiplier=1))
            chain.link(nc.gpsimd.iota(steps[:, 2], pattern=[[-1, P]], base=P, channel_multiplier=1))

            def store_att(r):
                if slots:
                    for k in range(HEADS // R):
                        slots.gather_round(pool, 0, HEADS // R * r + (base + 1 + k))
                pool.wait_ge(S["normalised"], HEADS * r + HEADS)
                pool.dma_start(flat(mix_fold[FROM:, ds(r, 1), 0:ATT]),
                               att[FROM:].rearrange("p g h d -> p (g h d)")).then_inc(S["att_stored"], 16)

            repeat(pool, F, store_att)
            pool.wait_ge(S["att_stored"], 16 * F)
            if samples:
                pool.wait_ge(S["s_stored"], 16 * NS)

        def mul_bcast(out, a, b, shape):
            return nc.vector.tensor_tensor(out, a, b.to_broadcast(shape), ALU.mult)

        @block.vector
        def _(dve):
            chain = Chain(dve, S["mchain"])
            dve.wait_ge(S["masks"], 8)
            for g in range(GROUPS - 1):
                apart = WINDOWS[g + 1][1] // F
                chain.link(nc.vector.tensor_scalar(steps[:, g], steps[:, 2], apart - 1, None, ALU.bitwise_and))
                chain.link(nc.vector.tensor_scalar(off[:, g], steps[:, g], 0.5, NEG, ALU.is_gt, ALU.mult))
                for r in range(F):
                    chain.link(nc.vector.tensor_tensor(far[:, r, g], far[:, r, g], off[:, g], ALU.min))

            g = Chain(dve, S["gchain"])
            dve.wait_ge(S["g_const"], 16 * (4 + 2 * GM_HEADS))
            for t, (at, n, _) in enumerate(tiles):
                dve.wait_ge(S["gelued"], t + 1)
                u = gin[0:n, t % 2, 0:GM].rearrange("p (h c) -> p h c", h=GM_HEADS)
                w = gin[0:n, t % 2, GM:]
                wh = w.rearrange("p (h c) -> p h c", h=GM_HEADS)
                sqh = gsq[0:n].rearrange("p (h c) -> p h c", h=GM_HEADS)
                bc = [n, GM_HEADS, GM // GM_HEADS]
                mean, var, rstd = (gst[0:n, a, :] for a in range(3))
                g.link(nc.vector.tensor_reduce(mean, wh, AX_X, ALU.add))
                g.link(nc.vector.tensor_scalar(mean, mean, GM_HEADS / GM, None, ALU.mult))
                g.link(nc.vector.tensor_tensor(wh, wh, mean.unsqueeze(2).to_broadcast(bc), ALU.subtract))
                g.link(nc.vector.tensor_tensor(gsq[0:n], w, w, ALU.mult))
                nc.vector.tensor_reduce(var, sqh, AX_X, ALU.add).then_inc(S["g_var"], 1)
                dve.wait_ge(S["g_root"], t + 1)
                g.link(nc.vector.reciprocal(rstd, var))
                g.link(nc.vector.tensor_tensor(wh, wh, rstd.unsqueeze(2).to_broadcast(bc), ALU.mult))
                g.link(nc.vector.tensor_tensor(w, w, gain[0:n], ALU.mult))
                nc.vector.tensor_tensor(w, w, shift[0:n], ALU.add).then_inc(S["g_normed"], 1)
                if t >= 1:
                    dve.wait_ge(S["g_stored"], 16 * t)
                go = gout[0:n].rearrange("p (h c) -> p h c", h=GM_HEADS)
                if n == P:
                    dve.wait_ge(S["z_done"], t + 1)
                    for h in range(GM_HEADS):
                        last = nc.vector.scalar_tensor_tensor(go[:, h], psO[:, 0, h * P:(h + 1) * P], bT[:, h:h + 1],
                                                              u[:, h], ALU.add, ALU.mult)
                else:
                    dve.wait_ge(S["g_normed"], t + 1)
                    g.link(nc.vector.tensor_tensor(go, wh, w00[:].to_broadcast(bc), ALU.mult))
                    g.link(nc.vector.tensor_tensor(go, go, b00[:].to_broadcast(bc), ALU.add))
                    last = nc.vector.tensor_tensor(go, go, u, ALU.mult)
                last.then_inc(S["g_out"], 1)

            def finish(r, h):
                n = HEADS * r + h
                dve.wait_ge(S["mixed"], n + 1)
                nc.vector.reciprocal(inv[:, h:h + 1], den[:, h:h + 1]).then_inc(S["inverted"], 1)
                dve.wait_ge(S["inverted"], n + 1)
                if h == 0:
                    after(dve, S["att_stored"], 16 * r)
                nc.vector.tensor_scalar(att[:, :, h], psO[:, h % 2, 0:GROUPS * HD].rearrange("p (g d) -> p g d", g=GROUPS),
                                        inv[:, h:h + 1], None, ALU.mult).then_inc(S["normalised"], 1)

            def fold_tile(r):
                for h in range(HEADS):
                    n = HEADS * r + h
                    dve.wait_ge(S["scored"], n + 1)
                    after(dve, S["p_turned"], n - lag(h) + 1)
                    nc.vector.scalar_tensor_tensor(scores[:, h % 3, 0:NEAR], psS[:, h % 2, 0:NEAR], SCALE,
                                                   near[:, ds(r, 1)].rearrange("p a b k -> p (a b k)"), ALU.mult, ALU.add)
                    nc.vector.scalar_tensor_tensor(scores[:, h % 3, NEAR:KEYS], psS[:, 2 + h % 2, 0:KEYS - NEAR], SCALE,
                                                   far[:, ds(r, 1)].rearrange("p a b k -> p (a b k)"),
                                                   ALU.mult, ALU.add).then_inc(S["masked"], 1)
                    dve.wait_ge(S["masked"], n + 1)
                    nc.vector.tensor_reduce(top[:, h:h + 1], scores[:, h % 3], AX_X, ALU.max, negate=True)\
                        .then_inc(S["maxed"], 1)
                    if slots:
                        slots.dot(dve, round_of(r, h), h % R, slots.h2[:])
                        if h:
                            slots.add(dve, round_of(r, h - 1), (h - 1) % R)
                    if h >= 2:
                        finish(r, h - 2)
                if slots:
                    slots.add(dve, round_of(r, HEADS - 1), R - 1)
                finish(r, HEADS - 2)
                finish(r, HEADS - 1)

            repeat(dve, F, fold_tile)

            def sample_pair(i):
                c = Chain(dve, S["schain"], 2 * LINKS * i)
                grouped = lambda a: a.rearrange("p (g w) -> p g w", g=GROUPS)
                for j in range(2):
                    dve.wait_ge(sk_in[j], K_LOADS * i + K_LOADS)
                    after(dve, S["s_mixed"], 2 * i + j - 1)
                    c.link(nc.vector.tensor_tensor(grouped(prod[:, j]), k_s[:, j], grouped(qb[:, j]), ALU.mult))
                    nc.vector.tensor_reduce(s24[:, j], prod[:, j].rearrange("p (g h d) -> p g h d", g=GROUPS, h=HEADS),
                                            AX_X, ALU.add).then_inc(S["s_scored"], 1)
                    c.link(nc.vector.tensor_tensor(oprod[:, j], own[:, j, 0], own[:, j, 1], ALU.mult))
                    c.link(nc.vector.tensor_reduce(oself[:, j, :, 0], oprod[:, j], AX_X, ALU.add))
                    nc.vector.tensor_scalar(srow[:, j, :, P:P + 1], oself[:, j], SCALE, None, ALU.mult)\
                        .then_inc(S["s_k_used"], 1)
                for j in range(2):
                    b = 2 * i + j
                    dve.wait_ge(S["s_turned"], b + 1)
                    c.link(nc.vector.tensor_scalar(srow[:, j, :, 0:P],
                                                   psP[0:HEADS, j, 0:GROUPS * P].rearrange("h (g k) -> h g k", g=GROUPS),
                                                   SCALE, None, ALU.mult))
                    row = srow[:, j].rearrange("h g k -> h (g k)")
                    nc.vector.tensor_reduce(sst[:, j, 0:1], row, AX_X, ALU.max, negate=True).then_inc(S["s_max"], 1)
                for j in range(2):
                    b = 2 * i + j
                    row = srow[:, j].rearrange("h g k -> h (g k)")
                    dve.wait_ge(S["s_exp"], b + 1)
                    c.link(nc.vector.reciprocal(sst[:, j, 2:3], sst[:, j, 1:2]))
                    nc.vector.tensor_scalar(row, row, sst[:, j, 2:3], None, ALU.mult).then_inc(S["s_probs"], 1)
                for j in range(2):
                    b = 2 * i + j
                    dve.wait_ge(S["s_probs"], b + 1)
                    dve.wait_ge(sv_in[j], V_LOADS * i + V_LOADS)
                    mul_bcast(oprod[:, j], own[:, j, 2], srow[:, j, :, P:P + 1], [HEADS, GROUPS, HD])\
                        .then_inc(S["s_probs_v"], 1)
                    dve.wait_ge(S["s_probs_v"], b + 1)
                    for g in range(GROUPS):
                        last = nc.vector.tensor_tensor(
                            spread[:, j, g], oprod[:, j, g:g + 1].to_broadcast([HEADS, HEADS, HD]),
                            ident[0:HEADS, 0:HEADS].unsqueeze(2).to_broadcast([HEADS, HEADS, HD]), ALU.mult)
                    last.then_inc(S["s_spread"], 1)
                    dve.wait_ge(S["s_pT"], b + 1)
                    nc.vector.tensor_copy(pT[:, j], psO[:, j, 0:GROUPS * HEADS].rearrange("p (g h) -> p g h", g=GROUPS))\
                        .then_inc(S["s_pT_copied"], 1)
                    dve.wait_ge(S["s_pT_copied"], b + 1)
                    for g in range(GROUPS):
                        last = mul_bcast(prod[:, j, g * GW:(g + 1) * GW].rearrange("p (h d) -> p h d", h=HEADS),
                                         v_s[:, j, g].rearrange("p (h d) -> p h d", h=HEADS),
                                         pT[:, j, g].unsqueeze(2), [P, HEADS, HD])
                    last.then_inc(S["s_v_used"], 1)
                assert c.n == 2 * LINKS

            if samples:
                repeat(dve, NS // 2, sample_pair)

        @block.scalar
        def _(act):
            for t, (at, n, _) in enumerate(tiles):
                act.wait_ge(g_in[t % 2], last_of(t))
                nc.scalar.activation(gin[0:n, t % 2], gin[0:n, t % 2], ACT.Gelu_apprx_tanh).then_inc(S["gelued"], 1)
                if t == 0:
                    for n_x in range(F):
                        act.wait_ge(S["x_full"], n_x + 1)
                        nc.scalar.copy(kT0[:, :, n_x], psP[:, n_x % 2].rearrange("p (b k) -> p b k", b=PAIRS)).then_inc(S["x_free"], 1)
                    act.wait_ge(S["x_full"], F + 1)
                    nc.scalar.copy(bT[:], psO[:, 0, 0:GM_HEADS]).then_inc(S["w_turned"], 1)
                    nc.scalar.copy(wT[:], psP[:, F % 2].rearrange("p (b k) -> p b k", b=GM_HEADS)).then_inc(S["w_turned"], 1)
                    act.wait_ge(S["w_turned"], 2)
                    act.sem_inc(S["x_free"], 1)
                act.wait_ge(S["g_var"], t + 1)
                if t == 0:
                    act.wait_ge(S["masks"], 3)
                nc.scalar.activation(gst[0:n, 1, :], gst[0:n, 1, :], ACT.Sqrt, bias=eps[0:n, :],
                                     scale=GM_HEADS / GM).then_inc(S["g_root"], 1)
                if n == P:
                    act.wait_ge(S["g_out"], t + 1)
                    act.dma_start(mix_d[at:at + n, ATT:], gout[0:n]).then_inc(S["g_stored"], 16)
                else:
                    act.wait_ge(S["g_normed"], t + 1)
                    act.dma_start(outs[8].rearrange("a b s h c -> (a b s) (h c)"), gin[0:n, t % 2, GM:])\
                       .then_inc(S["gv_stored"], 16)
                    act.wait_ge(S["g_out"], t + 1)
                    act.dma_start(mix_d[at:at + n, ATT:], gout[0:n]).then_inc(S["g_stored"], 16)

            def fold_tile(r):
                for q in range(TURNS):
                    act.wait_ge(S["x_full"], F + 1 + TURNS * r + q + 1)
                    nc.scalar.copy(qkT[:, 4 * q:4 * q + 4], psP[:, q % 2].rearrange("p (b k) -> p b k", b=4))\
                        .then_inc(S["x_free"], 1)

                def exponentials(h):
                    n = HEADS * r + h
                    act.wait_ge(S["maxed"], n + 1)
                    nc.scalar.activation(scores[:, h % 3], scores[:, h % 3], ACT.Exp, bias=top[:, h:h + 1],
                                         accum_out=den[:, h:h + 1]).then_inc(S["exped"], 1)

                exponentials(0)
                for h in range(HEADS):
                    n = HEADS * r + h
                    if h + 1 < HEADS:
                        exponentials(h + 1)
                    if slots:
                        slots.weigh(act, round_of(r, h), h % R)
                    act.wait_ge(S["p_turned"], n + 1)
                    after(act, S["mixed"], n - 1)
                    nc.scalar.copy(probsT[:, h % 2].rearrange("p b k -> p (b k)"), psP_flat[:, 0:KEYS])\
                        .then_inc(S["p_copied"], 1)

            repeat(act, F, fold_tile)

            def sample_pair(i):
                for j in range(2):
                    act.wait_ge(S["s_max"], 2 * i + j + 1)
                    row = srow[:, j].rearrange("h g k -> h (g k)")
                    nc.scalar.activation(row, row, ACT.Exp, bias=sst[:, j, 0:1], accum_out=sst[:, j, 1:2])\
                        .then_inc(S["s_exp"], 1)
                for j in range(2):
                    b = 2 * i + j
                    act.wait_ge(S["s_mixed"], b + 1)
                    after(act, S["s_stored"], 16 * b)
                    nc.scalar.copy(arow[:], psS[0:1, 0:GROUPS].rearrange("p a k -> p (a k)")).then_inc(S["s_row"], 1)
                    act.wait_ge(S["s_row"], b + 1)
                    act.dma_start(mix_d[ds(b + SEQ, 1), 0:ATT], arow[:]).then_inc(S["s_stored"], 16)

            if samples:
                repeat(act, NS // 2, sample_pair)

        @block.tensor
        def _(pe):
            pe.wait_ge(S["k0_in"], 16)
            for r in range(F):
                if r >= 2:
                    pe.wait_ge(S["x_free"], r - 1)
                for p in range(PAIRS):
                    last = nc.tensor.transpose(psP[:, r % 2, p * P:(p + 1) * P], k0n[:, r, p * P:(p + 1) * P], ident[:])
                last.then_inc(S["x_full"], 1)
            pe.wait_ge(S["g_masked"], 1)
            pe.wait_ge(S["x_free"], F)
            for h in range(GM_HEADS):
                nc.tensor.transpose(psP[:, F % 2, h * P:(h + 1) * P], wn[:, h], ident[:])
            nc.tensor.transpose(psO[:, 0, 0:GM_HEADS], bn[:], ident[0:GM_HEADS, 0:GM_HEADS]).then_inc(S["x_full"], 1)
            pe.wait_ge(S["w_turned"], 2)
            for t in range(PROMPTS):
                pe.wait_ge(S["g_normed"], t + 1)
                if t:
                    pe.wait_ge(S["g_out"], t)
                for h in range(GM_HEADS):
                    last = nc.tensor.matmul(psO[:, 0, h * P:(h + 1) * P], wT[:, h],
                                            gin[:, t % 2, GM + h * P:GM + (h + 1) * P], start=True, stop=True)
                last.then_inc(S["z_done"], 1)
            pe.wait_ge(S["v_in"], 16)

            def fold_tile(r):
                pe.wait_ge(S["qk_in"], 32 * r + 32)
                after(pe, S["p_copied"], HEADS * r)
                pe.wait_ge(S["x_free"], F + 1 + TURNS * r)
                for q in range(TURNS):
                    if q >= 2:
                        pe.wait_ge(S["x_free"], F + 1 + TURNS * r + q - 1)
                    for b in range(4):
                        c = (4 * q + b) * P
                        last = nc.tensor.transpose(psP[:, q % 2, b * P:(b + 1) * P], qkn[:, c:c + P], ident[:])
                    last.then_inc(S["x_full"], 1)
                pe.wait_ge(S["x_free"], F + 1 + TURNS * r + TURNS)

                def score(h):
                    n = HEADS * r + h
                    rows, p = slice(h % 2 * HD, h % 2 * HD + HD), h // 2
                    after(pe, S["masked"], n - 1)
                    nc.tensor.matmul(psS[:, h % 2, 0:NEAR], qkT[rows, p], kT0[rows, p].rearrange("p r k -> p (r k)"),
                                     start=True, stop=True)
                    for g in range(1, GROUPS):
                        last = nc.tensor.matmul(psS[:, 2 + h % 2, (g - 1) * P:g * P], qkT[rows, g * PAIRS + p],
                                                qkT[rows, NQ + (g - 1) * PAIRS + p], start=True, stop=True)
                    last.then_inc(S["scored"], 1)

                def turn_probs(h):
                    n = HEADS * r + h
                    pe.wait_ge(S["exped"], n + 1)
                    after(pe, S["p_copied"], n)
                    for b in range(BLOCKS):
                        last = nc.tensor.transpose(psP_flat[:, b * P:(b + 1) * P], scores[:, h % 3, b * P:(b + 1) * P], ident[:])
                    last.then_inc(S["p_turned"], 1)

                def mix(h):
                    n = HEADS * r + h
                    pe.wait_ge(S["p_copied"], n + 1)
                    if isinstance(n, int) and n == 0:
                        pe.wait_ge(S["g_out"], PROMPTS)
                    after(pe, S["normalised"], n - 1)
                    for b in range(F):
                        nc.tensor.matmul(psO[:, h % 2, 0:HD], probsT[:, h % 2, b], v[:, b, h * HD:(h + 1) * HD],
                                         start=(b == 0), stop=(b == F - 1))
                    for g in range(1, GROUPS):
                        last = nc.tensor.matmul(psO[:, h % 2, g * HD:(g + 1) * HD], probsT[:, h % 2, F + g - 1],
                                                flat(v[:, ds(r, 1), g * GW + h * HD:g * GW + (h + 1) * HD]),
                                                start=True, stop=True)
                    last.then_inc(S["mixed"], 1)

                score(0)
                score(1)
                for h in range(HEADS):
                    if h + 2 < HEADS:
                        score(h + 2)
                    turn_probs(h)
                    if h:
                        mix(h - 1)
                mix(HEADS - 1)

            repeat(pe, F, fold_tile)
            if not samples:
                return
            pe.wait_ge(S["normalised"], F * HEADS)

            def sample_pair(i):
                for j in range(2):
                    pe.wait_ge(S["s_scored"], 2 * i + j + 1)
                    pe.sem_inc(S["s_seen"], 1)
                    for g in range(GROUPS):
                        last = nc.tensor.transpose(psP[0:HEADS, j, g * P:(g + 1) * P], s24[:, j, g], ident[:])
                    last.then_inc(S["s_turned"], 1)
                for j in range(2):
                    pe.wait_ge(S["s_probs"], 2 * i + j + 1)
                    pe.sem_inc(S["s_seen"], 1)
                    for g in range(GROUPS):
                        last = nc.tensor.transpose(psO[:, j, g * HEADS:(g + 1) * HEADS], srow[:, j, g, 0:P],
                                                   ident[0:HEADS, 0:HEADS])
                    last.then_inc(S["s_pT"], 1)
                for j in range(2):
                    b = 2 * i + j
                    pe.wait_ge(S["s_v_used"], b + 1)
                    pe.wait_ge(S["s_spread"], b + 1)
                    after(pe, S["s_row"], b)
                    sums = psS[0:1, 0:GROUPS].rearrange("p a k -> p (a k)")
                    for g in range(GROUPS):
                        cols = slice(g * GW, (g + 1) * GW)
                        nc.tensor.matmul(sums[:, cols], ones[:], prod[:, j, cols], start=True, stop=False)
                        last = nc.tensor.matmul(sums[:, cols], ones[0:HEADS], spread[:, j, g].rearrange("p h d -> p (h d)"),
                                                start=False, stop=True)
                    last.then_inc(S["s_mixed"], 1)

            repeat(pe, NS // 2, sample_pair)


def output_stage(nc, name, tiles, ident, x_prompt, x_sample, mods_d, w_out, mix_d, hT, x1_d, h2_d, slots=None, base=0):
    CHUNKS = D // CK
    NTL = len(tiles)
    HALF = KD // 2
    w_view = w_out[0].rearrange("(k p) n -> p k n", p=P)
    x_rows = rows_of(tiles, x_prompt[0], x_sample.rearrange("b s d -> (b s) d"))
    with Stage(nc, name) as m:
        xin = m.sb("xin", [P, 2, D])
        y = m.sb("y", [P, NTL, D])
        w = m.sb("w", [P, 2, KD, CK])
        quarter = lambda j, a: w[:, j, a * HALF:(a + 1) * HALF].rearrange("p k n -> p (k n)")
        sq = quarter(1, 1)
        vec = {GT1: [quarter(0, 0)], SC2: [quarter(0, 1)], SH2: [quarter(1, 0)]}
        if tiles[-1][1] == NS:
            for s in vec:
                vec[s].append(m.sb(f"vec_s{s}", [NS, D])[:])
        stat = m.sb("stat", [P, 6, NTL])
        eps = m.sb("eps", [P, 1])
        psT = m.ps("psT", [P, 3, 4, P])
        product = TurnedProduct(m, nc, ident, tiles, hT, w) if tiles[-1][1] == NS else None
        acc = [] if product else [m.ps(f"acc{t}", [P, 512]) for t in range(NTL)]
        mix_in, x_in, w_ready, acc_full, copied = (m.pair(s) for s in ("mix_in", "x_in", "w_ready", "acc_full", "copied"))
        mod_in, eps_set, turned, psT_free, squared, rooted, chain_v, x1_done, h2_done, stored = (m.sem(s) for s in (
            "mod_in", "eps_set", "turned", "psT_free", "squared", "rooted", "chain", "x1_done", "h2_done", "stored"))
        block = m.block()

        @block.sync
        def _(sp):
            for t, (at, n, _) in enumerate(tiles):
                if t >= 2:
                    sp.wait_ge(turned, 4 * (t - 1))
                sp.dma_start(xin[0:n, t % 2], mix_d[at:at + n, :]).then_inc(mix_in[t % 2], 16)

            def chunk_pair(i):
                for j in range(2):
                    if not product:
                        after(sp, acc_full[j], NTL * i)
                    elif not isinstance(i, int):
                        product.wait_for(sp, product.full, 2 * i + j - 1)
                    sp.dma_start(w[:, j], w_view[:, :, ds((2 * i + j) * CK, CK)]).then_inc(w_ready[j], 16)

            repeat(sp, CHUNKS // 2, chunk_pair)
            for t in range(2):
                n = tiles[t][1]
                if t == 0:
                    sp.wait_ge(turned, 4 * NTL)
                sp.dma_start(xin[0:n, t], x_rows[t]).then_inc(x_in[t], 16)
            if product:
                product.wait_for(sp, product.full, CHUNKS)
            for j in range(0 if product else 2):
                sp.wait_ge(acc_full[j], NTL * CHUNKS // 2)
            for s in (GT1, SC2, SH2):
                load_mods(sp, mods_d, s, vec[s], mod_in)
            for t, (at, n, _) in enumerate(tiles):
                sp.wait_ge(h2_done, t + 1)
                sp.dma_start(x1_d[at:at + n, :], xin[0:n, t % 2]).then_inc(stored, 16)
                sp.dma_start(h2_d[at:at + n, :], y[0:n, t]).then_inc(stored, 16)
                sp.wait_ge(stored, 32 * (t + 1))
                if t + 2 < NTL:
                    sp.dma_start(xin[0:tiles[t + 2][1], t % 2], x_rows[t + 2]).then_inc(x_in[t % 2], 16)

        @block.gpsimd
        def _(pool):
            nc.gpsimd.memset(eps[:], EPS).then_inc(eps_set, 1)
            if slots:
                repeat(pool, CHUNKS // 2 + 1, lambda i: slots.gather_round(pool, 0, base + 1 + i))

        @block.scalar
        def _(act):
            for t, (at, n, c) in enumerate(tiles):
                for q in range(4):
                    act.wait_ge(turned, 4 * t + q + 1)
                    nc.scalar.copy(hT[:, 4 * q:4 * q + 4, c:c + n], psT[:, (4 * t + q) % 3, :, 0:n])\
                        .then_inc(psT_free, 1)

            def chunk_pair(i):
                for j in range(2):
                    if product:
                        product.copy(act, 2 * i + j)
                        continue
                    for t, (at, n, _) in enumerate(tiles):
                        if slots and t < R // 2:
                            slots.weigh(act, base + i, R // 2 * j + t)
                        act.wait_ge(acc_full[j], NTL * i + t + 1)
                        nc.scalar.copy(y[0:n, t, ds((2 * i + j) * CK, CK)], acc[t][0:n, 0:CK]).then_inc(copied[j], 1)

            repeat(act, CHUNKS // 2, chunk_pair)
            act.wait_ge(eps_set, 1)
            if product:
                product.wait_for(act, product.used, CHUNKS)
                product.wait_for(act, product.full, CHUNKS)
            for j in range(0 if product else 2):
                act.wait_ge(copied[j], NTL * CHUNKS // 2)
                act.wait_ge(acc_full[j], NTL * CHUNKS // 2)
            for t, (at, n, c) in enumerate(tiles):
                for part, src in ((0, y[0:n, t]), (1, xin[0:n, t % 2])):
                    if part:
                        act.wait_ge(x1_done, t + 1)
                    if t or part:
                        act.wait_ge(squared, 2 * t + part)
                    s = 3 * part
                    nc.scalar.activation(sq[0:n, :], src, ACT.Square, accum_out=stat[0:n, s, t:t + 1]).then_inc(squared, 1)
                    act.wait_ge(squared, 2 * t + part + 1)
                    nc.scalar.activation(stat[0:n, s + 1, t:t + 1], stat[0:n, s, t:t + 1], ACT.Sqrt, bias=eps[0:n, :],
                                         scale=1.0 / D).then_inc(rooted, 1)
                for q in range(4):
                    act.wait_ge(turned, 4 * (NTL + t) + q + 1)
                    nc.scalar.copy(hT[:, 4 * q:4 * q + 4, c:c + n], psT[:, (4 * (NTL + t) + q) % 3, :, 0:n])\
                        .then_inc(psT_free, 1)
                if slots:
                    slots.weigh(act, base + CHUNKS // 2, t)
            if slots:
                slots.weigh(act, base + CHUNKS // 2, R - 1)

        @block.vector
        def _(dve):

            def chunk_pair(i):
                for j in range(2):
                    product.place(dve, 2 * i + j,
                                  lambda t, b: y[0:tiles[t][1], t, ds((2 * i + j) * CK + b * P, P)])

            if product:
                repeat(dve, CHUNKS // 2, chunk_pair)
            if slots:
                repeat(dve, CHUNKS // 2, lambda i: slots.sum_round(dve, base + i))
            chain = Chain(dve, chain_v)
            dve.wait_ge(mod_in, 16 * sum(len(v) for v in vec.values()))
            for t, (at, n, _) in enumerate(tiles):
                gate, scale, shift = (vec[s][-1 if n == NS else 0][0:n] for s in (GT1, SC2, SH2))
                yt, xt = y[0:n, t], xin[0:n, t % 2]
                dve.wait_ge(rooted, 2 * t + 1)
                chain.link(nc.vector.reciprocal(stat[0:n, 2, t:t + 1], stat[0:n, 1, t:t + 1]))
                chain.link(nc.vector.scalar_tensor_tensor(yt, yt, stat[0:n, 2, t:t + 1], gate, ALU.mult, ALU.mult))
                dve.wait_ge(x_in[t % 2], 16 * (t // 2 + 1))
                nc.vector.tensor_tensor(xt, xt, yt, ALU.add).then_inc(x1_done, 1)
                dve.wait_ge(rooted, 2 * t + 2)
                chain.link(nc.vector.reciprocal(stat[0:n, 5, t:t + 1], stat[0:n, 4, t:t + 1]))
                chain.link(nc.vector.scalar_tensor_tensor(yt, xt, stat[0:n, 5, t:t + 1], scale, ALU.mult, ALU.mult))
                nc.vector.tensor_tensor(yt, yt, shift, ALU.add).then_inc(h2_done, 1)
                if slots:
                    slots.dot(dve, base + CHUNKS // 2, t, slots.h2[:])
                    if t:
                        slots.add(dve, base + CHUNKS // 2, t - 1)
            if slots:
                slots.dot(dve, base + CHUNKS // 2, R - 1, slots.h2[:])
                for j in range(R - 2, R):
                    slots.add(dve, base + CHUNKS // 2, j)

        @block.tensor
        def _(pe):
            for t, (at, n, _) in enumerate(tiles):
                pe.wait_ge(mix_in[t % 2], 16 * (t // 2 + 1))
                turn(nc, pe, xin[:, t % 2], n, psT, ident, psT_free, turned, 4 * t)
            pe.wait_ge(psT_free, 4 * NTL)

            def chunk_pair(i):
                for j in range(2):
                    pe.wait_ge(w_ready[j], 16 * i + 16)
                    if product:
                        product.multiply(pe, 2 * i + j, j)
                        continue
                    for t, (at, n, c) in enumerate(tiles):
                        after(pe, copied[1 - j], 0 if isinstance(i, int) and not j else NTL * (i + j - 1) + t + 1)
                        for k in range(KD):
                            last = nc.tensor.matmul(acc[t][0:n, 0:CK], hT[:, k, c:c + n], w[:, j, k, :],
                                                    start=(k == 0), stop=(k == KD - 1))
                        last.then_inc(acc_full[j], 1)

            repeat(pe, CHUNKS // 2, chunk_pair)
            if product:
                product.turn_back(pe, CHUNKS - 1, 1)
            for t, (at, n, _) in enumerate(tiles):
                pe.wait_ge(h2_done, t + 1)
                turn(nc, pe, y[:, t], n, psT, ident, psT_free, turned, 4 * (NTL + t))


class Picker:
    LINKS, MIN = 18, -3.0e38

    def __init__(self, m, nc, scores, experts, gates):
        self.nc, self.scores, self.experts, self.gates = nc, scores, experts, gates
        self.keys, self.left = m.sb("keys", [P, 2, NKEYS]), m.sb("left", [P, 2, NKEYS])
        self.best, self.place = m.sb("best", [P, 2, TOPK]), m.sb("place", [P, 2, TOPK], U32)
        self.placef = m.sb("placef", [P, 2, TOPK])
        self.sums, self.sums_left = m.sb("sums", [P, 1, TOPK * TOPK]), m.sb("sums_left", [P, 1, TOPK * TOPK])
        self.picked, self.pos = m.sb("picked", [P, 1, TOPK]), m.sb("pos", [P, 1, TOPK], U32)
        self.half, self.halff = m.sb("half", [P, 2, TOPK], U32), m.sb("halff", [P, 2, TOPK])
        self.onehot, self.found = m.sb("onehot", [P, 2 * TOPK, TOPK]), m.sb("found", [P, 2, TOPK])
        self.row, self.rows = m.sb("row", [P, TOPK]), m.sb("rows", [P, SLOTS])
        self.expo, self.total = m.sb("expo", [P, TOPK]), m.sb("total", [P, 2])
        self.iota_i, self.iota_f = m.sb("iota_i", [P, TOPK], mybir.dt.int32), m.sb("iota_f", [P, TOPK])
        self.iota_set, self.chain, self.shifted, self.exped, self.done, self.carrier = (m.sem(s) for s in (
            "iota_set", "pick_chain", "pick_shifted", "pick_exped", "pick_done", "pick_carrier"))

    def number(self, pool):
        self.nc.gpsimd.iota(self.iota_i[:], pattern=[[1, TOPK]], base=0, channel_multiplier=0).then_inc(self.iota_set, 1)

    def prepare(self, dve):
        dve.wait_ge(self.iota_set, 1)
        self.nc.vector.tensor_copy(self.iota_f[:], self.iota_i[:]).then_inc(self.iota_set, 1)
        dve.wait_ge(self.iota_set, 2)

    def top16(self, dve, c, values, left, top, index):
        segments = range(values.shape[1])
        for lo in (0, 8):
            src = left if lo else values
            dve.sem_inc(self.carrier, 1)
            for s in segments:
                last = self.nc.vector.max(top[:, s, lo:lo + 8], src[:, s])
            c.link(last)
            dve.sem_inc(self.carrier, 1)
            for s in segments:
                last = self.nc.vector.max_index(index[:, s, lo:lo + 8], top[:, s, lo:lo + 8], src[:, s])
                if not lo:
                    last = self.nc.vector.match_replace(left[:, s], top[:, s, 0:8], values[:, s], self.MIN)
            c.link(last)

    def pick(self, dve, h, t, n):
        v, c = self.nc.vector, Chain(dve, self.chain, self.LINKS * n)
        c.link(v.tensor_copy(self.keys[:], self.scores[:, ds(2 * h, 2)]))
        self.top16(dve, c, self.keys, self.left, self.best, self.place)
        v.tensor_copy(self.placef[:], self.place[:])
        shape = [P, TOPK, TOPK]
        c.link(v.tensor_tensor(self.sums[:, 0].rearrange("p (a b) -> p a b", a=TOPK),
                               self.best[:, 0].unsqueeze(2).to_broadcast(shape),
                               self.best[:, 1].unsqueeze(1).to_broadcast(shape), ALU.add))
        self.top16(dve, c, self.sums, self.sums_left, self.picked, self.pos)
        v.tensor_tensor(self.expo[:], self.picked[:, 0], self.picked[:, 0, 0:1].to_broadcast([P, TOPK]), ALU.subtract)\
            .then_inc(self.shifted, 1)
        v.tensor_scalar(self.half[:, 0], self.pos[:, 0], 4, None, ALU.logical_shift_right)
        c.link(v.tensor_scalar(self.half[:, 1], self.pos[:, 0], TOPK - 1, None, ALU.bitwise_and))
        c.link(v.tensor_copy(self.halff[:], self.half[:]))
        c.link(v.tensor_tensor(self.onehot[:], self.halff[:].rearrange("p a k -> p (a k)").unsqueeze(2)
                               .to_broadcast([P, 2 * TOPK, TOPK]),
                               self.iota_f[:].unsqueeze(1).to_broadcast([P, 2 * TOPK, TOPK]), ALU.is_equal))
        for a in range(2):
            hot = self.onehot[:, a * TOPK:(a + 1) * TOPK]
            last = v.tensor_tensor(hot, hot, self.placef[:, a].unsqueeze(1).to_broadcast(shape), ALU.mult)
        c.link(last)
        c.link(v.tensor_reduce(self.found[:].rearrange("p a k -> p (a k)"), self.onehot[:], AX_X, ALU.add))
        c.link(v.scalar_tensor_tensor(self.row[:], self.found[:, 0], float(NKEYS), self.found[:, 1], ALU.mult, ALU.add))
        v.tensor_copy(self.rows[:, ds(TOPK * h, TOPK)], self.row[:])
        c.link(v.tensor_copy(of_tile(self.experts, t, ds(TOPK * h, TOPK)), self.row[:]))
        assert c.n == self.LINKS - 1

    def exponentials(self, act, n):
        act.wait_ge(self.shifted, n + 1)
        self.nc.scalar.activation(self.expo[:], self.expo[:], ACT.Exp, accum_out=self.total[:, 0:1]).then_inc(self.exped, 1)

    def gate(self, dve, h, t, n):
        c = Chain(dve, self.chain, self.LINKS * n + self.LINKS - 1)
        dve.wait_ge(self.exped, n + 1)
        c.link(self.nc.vector.reciprocal(self.total[:, 1:2], self.total[:, 0:1]))
        self.nc.vector.tensor_scalar(of_tile(self.gates, t, ds(TOPK * h, TOPK)), self.expo[:], self.total[:, 1:2], None,
                                     ALU.mult).then_inc(self.done, 1)
        dve.wait_ge(self.done, n + 1)


def routing_stage(nc, name, tiles, ident, w_q, sub_keys, hT, scores_d, slots=None, base=0):
    CHUNKS = D // CK
    NTL, W = len(tiles), width(tiles)
    SEG = 2 * PH
    w_view = w_q[0].rearrange("(k p) n -> p k n", p=P)
    with Stage(nc, name) as m:
        w = m.sb("w", [P, 2, KD, CK])
        qrT = m.sb("qrT", [P, SEG, W])
        keys_n, keysT = m.sb("keys_n", [P, 2, P]), m.sb("keysT", [P, 2, P])
        sc = m.sb("sc", [P, 2, SEG, NKEYS])
        acc = [m.ps(f"acc{j}", [P, 512]) for j in range(2)]
        psC = m.ps("psC", [P, SEG, NKEYS])
        keys_in, keys_turned, keys_set, scored, sc_copied = (m.sem(s) for s in (
            "keys_in", "keys_turned", "keys_set", "scored", "sc_copied"))
        w_ready, acc_full, copied, stored = (m.pair(s) for s in ("w_ready", "acc_full", "copied", "stored"))
        block = m.block()

        @block.sync
        def _(sp):
            sp.dma_start(keys_n[:], sub_keys[0].rearrange("a k c -> k a c")).then_inc(keys_in, 16)

            def chunk_pair(i):
                for j in range(2):
                    if not isinstance(i, int):
                        sp.wait_ge(acc_full[0], 2 * i + j - 1)
                        sp.wait_ge(acc_full[1], 2 * i + j - 1)
                    sp.dma_start(w[:, j], w_view[:, :, ds((2 * i + j) * CK, CK)]).then_inc(w_ready[j], 16)

            repeat(sp, CHUNKS // 2, chunk_pair)
            for t, (at, n, _) in enumerate(tiles):
                sp.wait_ge(sc_copied, t + 1)
                sp.dma_start(scores_d[at:at + n, :], sc[0:n, t % 2].rearrange("p s k -> p (s k)")).then_inc(stored[t % 2], 16)
            for j in range(2):
                sp.wait_ge(stored[j], 16 * ((NTL + 1 - j) // 2))

        @block.gpsimd
        def _(pool):
            if slots:
                repeat(pool, CHUNKS // 2 + 1, lambda i: slots.gather_round(pool, 0, base + 1 + i))

        @block.scalar
        def _(act):
            act.wait_ge(keys_turned, 1)
            nc.scalar.copy(keysT[:], psC[:, 0:2]).then_inc(keys_set, 1)

            def chunk_pair(i):
                for j in range(2):
                    for b in range(2):
                        if slots:
                            slots.weigh(act, base + i, R // 2 * j + b)
                        act.wait_ge(acc_full[b], 2 * i + j + 1)
                        nc.scalar.copy(flat(qrT[:, ds(2 * (2 * i + j) + b, 1)]), acc[b][:, 0:W]).then_inc(copied[b], 1)

            repeat(act, CHUNKS // 2, chunk_pair)
            for t, (at, n, _) in enumerate(tiles):
                act.wait_ge(scored, t + 1)
                if t >= 2:
                    act.wait_ge(stored[t % 2], 16 * (t // 2))
                nc.scalar.copy(sc[0:n, t % 2], psC[0:n]).then_inc(sc_copied, 1)
                if slots:
                    slots.weigh(act, base + CHUNKS // 2, t)
            if slots:
                slots.weigh(act, base + CHUNKS // 2, R - 1)

        @block.vector
        def _(dve):
            if slots:
                repeat(dve, CHUNKS // 2 + 1, lambda i: slots.sum_round(dve, base + i))

        @block.tensor
        def _(pe):
            pe.wait_ge(keys_in, 16)
            for a in range(2):
                last = nc.tensor.transpose(psC[:, a], keys_n[:, a], ident[:])
            last.then_inc(keys_turned, 1)

            def chunk_pair(i):
                for j in range(2):
                    pe.wait_ge(w_ready[j], 16 * i + 16)
                    for b in range(2):
                        after(pe, copied[b], 2 * i + j)
                        for k in range(KD):
                            last = nc.tensor.matmul(acc[b][:, 0:W], w[:, j, k, b * P:(b + 1) * P], hT[:, k, :],
                                                    start=(k == 0), stop=(k == KD - 1))
                        last.then_inc(acc_full[b], 1)

            repeat(pe, CHUNKS // 2, chunk_pair)
            pe.wait_ge(keys_set, 1)
            for b in range(2):
                pe.wait_ge(copied[b], CHUNKS)
            for t, (at, n, c) in enumerate(tiles):
                if t:
                    pe.wait_ge(sc_copied, t)
                for s in range(SEG):
                    last = nc.tensor.matmul(psC[0:n, s], qrT[:, s, c:c + n], keysT[:, s % 2], start=True, stop=True)
                last.then_inc(scored, 1)


def expert_stage(nc, ident, mods_d, x1_d, h2_d, scores_d, slots, base, experts, gates, outs):
    N = 512
    SEG = 2 * PH
    LAST = NT * ROUNDS
    with Stage(nc, "exp") as m:
        x1, y = m.sb("x1", [P, D]), m.sb("y", [P, D])
        gain_p, gain_s = m.sb("gain_p", [P, D]), m.sb("gain_s", [NS, D])
        h2_odd, h2_s = m.sb("h2_odd", [P, D]), m.sb("h2_s", [P, 2, D])
        scores = m.sb("scores", [P, SEG, NKEYS])
        diag = m.sb("diag", [P, R, P])
        col = m.sb("col", [P, NS, NS])
        experts_s, gates_s = m.sb("experts_s", [P, NS], U32), m.sb("gates_s", [P, NS])
        zero = m.sb("zero", [P, N])
        stat = m.sb("stat", [P, 3])
        eps = m.sb("eps", [P, 1])
        acc = m.ps("acc", [P, D])
        psE = m.ps("psE", [P, 2, NS])
        picker = Picker(m, nc, scores, experts, gates)
        const, scores_in, x1_in, gain_in, weight_set = (m.sem(s) for s in (
            "const", "scores_in", "x1_in", "gain_in", "weight_set"))
        h2_s_in = m.pair("h2_s_in")
        chain_v, tile_dotted, acc_full, squared, rooted, y_done, stored, s_turned, s_kept = (m.sem(s) for s in (
            "chain_v", "tile_dotted", "acc_full", "squared", "rooted", "y_done", "stored", "s_turned", "s_kept"))
        block = m.block()
        h2 = lambda t: h2_odd if t % 2 else slots.h2
        rows = lambda t: slice(t * P, (t + 1) * P)
        n_pick = lambda t, h: PH * (t - 1) + h
        scores_flat = scores[:].rearrange("p s k -> p (s k)")

        def over_rounds(eng, t, own, middle, plain):
            at = base
            if t:
                with eng.Fori(0, PH - 1) as i:
                    own(i + 1, i)
                at = PH - 1
            with eng.Fori(at, at + 2) as i:
                plain(i)
            at += 2
            at += middle(at)
            with eng.Fori(at, ROUNDS) as i:
                plain(i)

        @block.sync
        def _(sp):
            load_mods(sp, mods_d, GT2, [gain_p, gain_s], gain_in)

            for t in range(NT):
                if t:
                    sp.wait_ge(tile_dotted, t)
                if t + 1 < NT:
                    sp.dma_start(h2(t + 1)[:], h2_d[rows(t + 1), :]).then_inc(slots.h2_in, 16)
                    if t:
                        sp.wait_ge(picker.done, n_pick(t + 1, 0))
                    sp.dma_start(scores_flat, scores_d[rows(t + 1), :]).then_inc(scores_in, 16)
                else:
                    sp.wait_ge(picker.done, n_pick(NT, 0))
                    sp.dma_start(scores_flat[0:NS], scores_d[SEQ:TOK, :]).then_inc(scores_in, 16)
                if t:
                    sp.wait_ge(y_done, t)
                    sp.dma_start(outs[0][0, rows(t - 1), :], y[:]).then_inc(stored, 16)
                sp.dma_start(x1[:], x1_d[rows(t), :]).then_inc(x1_in, 16)
            for b in range(NS):
                if b >= 2:
                    sp.wait_ge(slots.dotted[(b - 2) % R], LAST + (b - 2) // R + 2)
                sp.dma_start(h2_s[:, b % 2], bcast(h2_d[SEQ + b:SEQ + b + 1, :], P)).then_inc(h2_s_in[b % 2], 16)
                if b == 1:
                    sp.wait_ge(y_done, NT)
                    sp.dma_start(outs[0][0, rows(NT - 1), :], y[:]).then_inc(stored, 16)
                    sp.dma_start(x1[0:NS], x1_d[SEQ:TOK, :]).then_inc(x1_in, 16)
            sp.wait_ge(y_done, NT + 1)
            sp.dma_start(outs[1].rearrange("b s d -> (b s) d"), y[0:NS]).then_inc(stored, 16)
            sp.wait_ge(stored, 16 * (NT + 1))

        @block.gpsimd
        def _(pool):
            nc.gpsimd.memset(eps[:], EPS).then_inc(const, 1)
            nc.gpsimd.memset(zero[:], 0.0).then_inc(const, 1)
            nc.gpsimd.memset(col[:], 0.0).then_inc(const, 1)
            picker.number(pool)

            for t in range(NT):
                if t == 0:
                    with pool.Fori(base + 1, ROUNDS) as i:
                        slots.gather_round(pool, 0, i)
                    continue
                with pool.Fori(0, PH) as i:
                    pool.wait_ge(picker.done, i + n_pick(t, 1))
                    slots.gather_round(pool, t, i)
                with pool.Fori(PH, ROUNDS) as i:
                    slots.gather_round(pool, t, i)
            pool.wait_ge(s_kept, 1)
            for b in range(NS):
                n, j = LAST + b // R, b % R
                pool.wait_ge(slots.dotted[j], n + 1)
                pool.wait_ge(slots.v_used[j], n + 1)
                slots.gather(pool, j, experts_s[:, b:b + 1])

        @block.vector
        def _(dve):
            picker.prepare(dve)

            def finish_tile(n, gain, t):
                c = Chain(dve, chain_v, 2 * t)
                dve.wait_ge(rooted, t + 1)
                c.link(nc.vector.reciprocal(stat[0:n, 2:3], stat[0:n, 1:2]))
                dve.wait_ge(x1_in, 16 * t + 16)
                c.link(nc.vector.scalar_tensor_tensor(y[0:n], y[0:n], stat[0:n, 2:3], gain[0:n], ALU.mult, ALU.mult))
                nc.vector.tensor_tensor(y[0:n], y[0:n], x1[0:n], ALU.add).then_inc(y_done, 1)

            def pick(t, h):
                picker.pick(dve, h, t, h + n_pick(t, 0))
                picker.gate(dve, h, t, h + n_pick(t, 0))

            def tile(t):
                dve.wait_ge(slots.h2_in, 16 * t + 16)

                def plain(i):
                    for j in range(R):
                        slots.dot(dve, i + ROUNDS * t, j, h2(t)[:])

                def picking(of, h, i):
                    pick(of, h)
                    plain(i)

                def middle(at):
                    if t:
                        finish_tile(P, gain_p, t - 1)
                    dve.wait_ge(scores_in, 16 * t + 16)
                    if t + 1 < NT:
                        pick(t + 1, 0)
                        return 0
                    with dve.Fori(0, PH) as h:
                        picking(NT, h, h + at)
                    return PH

                over_rounds(dve, t, lambda h, i: picking(t, h, i), middle, plain)
                for j in range(R):
                    dve.wait_ge(slots.dotted[j], ROUNDS * t + ROUNDS + 1)
                dve.sem_inc(tile_dotted, 1)

            dve.wait_ge(gain_in, 32)
            for t in range(NT):
                tile(t)
            dve.wait_ge(s_turned, 1)
            nc.vector.tensor_copy(experts_s[:], psE[:, 0])
            nc.vector.tensor_copy(gates_s[:], psE[:, 1]).then_inc(s_kept, 1)
            finish_tile(P, gain_p, NT - 1)
            for b in range(NS):
                dve.wait_ge(h2_s_in[b % 2], 16 * (b // 2 + 1))
                slots.dot(dve, LAST + b // R, b % R, h2_s[:, b % 2])
            finish_tile(NS, gain_s, NT)

        @block.scalar
        def _(act):
            def weigh(t, i, j):
                n = ROUNDS * t + i
                slots.activate(act, n, j)
                nc.scalar.activation(slots.weight[:, j:j + 1], slots.gelu[:, j:j + 1], ACT.Copy,
                                     scale=gates[:, t, ds(R * i + j, 1)]).then_inc(weight_set, 1)
                act.wait_ge(weight_set, R * (n - base) + j + 1)
                nc.scalar.activation(diag[:, j], ident[:], ACT.Copy, scale=slots.weight[:, j:j + 1])\
                    .then_inc(slots.weighted[j], 1)

            def norm(n, t):
                act.wait_ge(acc_full, t + 1)
                if t:
                    act.wait_ge(stored, 16 * t)
                nc.scalar.copy(y[0:n], acc[0:n]).then_inc(squared, 1)
                nc.scalar.activation(acc[0:n], acc[0:n], ACT.Square, accum_out=stat[0:n, 0:1]).then_inc(squared, 1)
                act.wait_ge(squared, 2 * t + 2)
                nc.scalar.activation(stat[0:n, 1:2], stat[0:n, 0:1], ACT.Sqrt, bias=eps[0:n], scale=1.0 / D)\
                    .then_inc(rooted, 1)

            def tile(t):
                def plain(i):
                    for j in range(R):
                        weigh(t, i, j)

                def own(h, i):
                    picker.exponentials(act, h + n_pick(t, 0))
                    act.wait_ge(picker.done, h + n_pick(t, 0))
                    plain(i)

                def middle(at):
                    if t + 1 < NT:
                        picker.exponentials(act, n_pick(t + 1, 0))
                        act.wait_ge(picker.done, n_pick(t + 1, 1))
                        return 0
                    with act.Fori(0, PH) as h:
                        picker.exponentials(act, h + n_pick(NT, 0))
                        act.wait_ge(picker.done, h + n_pick(NT, 0))
                        plain(h + at)
                    return PH

                over_rounds(act, t, own, middle, plain)
                norm(P, t)

            act.wait_ge(const, 3)
            for t in range(NT):
                tile(t)
            act.wait_ge(s_kept, 1)
            for b in range(NS):
                n, j = LAST + b // R, b % R
                slots.activate(act, n, j)
                nc.scalar.activation(col[:, b, b:b + 1], slots.gelu[:, j:j + 1], ACT.Copy, scale=gates_s[:, b:b + 1])\
                    .then_inc(slots.weighted[j], 1)
            norm(NS, NT)

        @block.tensor
        def _(pe):
            pe.wait_ge(const, 3)

            def spread(lhsT, rows, **flags):
                for c in range(D // N):
                    last = nc.tensor.matmul(acc[:, c * N:(c + 1) * N], lhsT, rows[:, c * N:(c + 1) * N], **flags)
                return last

            def add(n):
                for j in range(R):
                    pe.wait_ge(slots.weighted[j], n + 1)
                    pe.wait_ge(slots.v_in[j], 16 * n + 16)
                    spread(diag[:, j], slots.v[:, j], start=False, stop=False).then_inc(slots.v_used[j], 1)

            def tile(t):
                if t == 0:
                    spread(ident[:], slots.sum, start=True, stop=False)
                else:
                    pe.wait_ge(rooted, t)
                    for c in range(D // N):
                        nc.tensor.matmul(acc[:, c * N:(c + 1) * N], zero[:, 0:P], zero[:], start=True, stop=False)
                with pe.Fori(base if t == 0 else 0, ROUNDS) as i:
                    add(ROUNDS * t + i)
                for c in range(D // N):
                    last = nc.tensor.matmul(acc[:, c * N:(c + 1) * N], zero[:, 0:P], zero[:], start=False, stop=True)
                last.then_inc(acc_full, 1)

            for t in range(NT):
                tile(t)
            pe.wait_ge(picker.done, PH * NT)
            nc.tensor.transpose(psE[:, 0], picker.rows[0:NS], ident[0:NS, 0:NS])
            nc.tensor.transpose(psE[:, 1], gates[0:NS, NT], ident[0:NS, 0:NS]).then_inc(s_turned, 1)
            pe.wait_ge(rooted, NT)
            for b in range(NS):
                n, j = LAST + b // R, b % R
                pe.wait_ge(slots.weighted[j], n + 1)
                pe.wait_ge(slots.v_in[j], 16 * n + 16)
                for c in range(D // N):
                    last = nc.tensor.matmul(acc[0:NS, c * N:(c + 1) * N], col[:, b], slots.v[:, j, c * N:(c + 1) * N],
                                            start=(b == 0), stop=(b == NS - 1))
                last.then_inc(slots.v_used[j], 1)
            for j in range(R):
                pe.wait_ge(slots.v_used[j], LAST + NS // R + 1)
            pe.sem_inc(acc_full, 1)


def program(nc, x_prompt, x_sample, c_prompt, c_sample, cache1, cache4, cache16, w_ada, b_ada, norm_g, w_in,
            gm_ln_g, gm_ln_b, w_s, b_s, w_out, w_q, sub_keys, expert_u, expert_v, outs):
    scratch = lambda name, shape: nc.dram_tensor(name, shape, F32, kind="Internal").ap()
    mods_d = scratch("mods_d", (ROWS, 6, D))
    proj_d = scratch("proj_d", (TOK, WIN))
    mix_d = scratch("mix_d", (TOK, D))
    x1_d = scratch("x1_d", (TOK, D))
    h2_d = scratch("h2_d", (TOK, D))
    scores_d = scratch("scores_d", (TOK, 2 * PH * NKEYS))
    with ExitStack() as ctx:
        ident = ctx.enter_context(nc.sbuf_tensor("ident", [P, P], F32))
        ident_made = nc.alloc_semaphore("ident_made")
        modulation_stage(nc, ident, ident_made, c_prompt, c_sample, w_ada, b_ada, norm_g, mods_d)
        buffer = lambda name, shape, dt=F32: ctx.enter_context(nc.sbuf_tensor(name, shape, dt))
        cache = (cache1, cache4, cache16)
        experts, gates = buffer("experts", [P, NT + 1, SLOTS], U32), buffer("gates", [P, NT + 1, SLOTS])
        projection_stage(nc, "proj1", FIRST, ident, x_prompt, x_sample, mods_d, w_in, proj_d)
        mixer_stage(nc, "mix1", FIRST, 1, ident, proj_d, cache, gm_ln_g, gm_ln_b, w_s, b_s, mix_d, outs)
        with nc.sbuf_tensor("hT1", [P, KD, width(FIRST)], F32) as hT:
            output_stage(nc, "out1", FIRST, ident, x_prompt, x_sample, mods_d, w_out, mix_d, hT, x1_d, h2_d)
            routing_stage(nc, "route1", FIRST, ident, w_q, sub_keys, hT, scores_d)
        slots = Slots(ctx, nc, ident, expert_u, expert_v, experts, gates, h2_d)
        projection_stage(nc, "proj2", SECOND, ident, x_prompt, x_sample, mods_d, w_in, proj_d, slots, scores_d)
        done = WIN // CK // 2
        mixer_stage(nc, "mix2", SECOND, NT, ident, proj_d, cache, gm_ln_g, gm_ln_b, w_s, b_s, mix_d, outs, slots, done)
        done += NT * HEADS // R
        with nc.sbuf_tensor("hT2", [P, KD, width(SECOND)], F32) as hT:
            output_stage(nc, "out2", SECOND, ident, x_prompt, x_sample, mods_d, w_out, mix_d, hT, x1_d, h2_d, slots, done)
            done += D // CK // 2 + 1
            routing_stage(nc, "route2", SECOND, ident, w_q, sub_keys, hT, scores_d, slots, done)
            done += D // CK // 2 + 1
        expert_stage(nc, ident, mods_d, x1_d, h2_d, scores_d, slots, done, experts, gates, outs)


_INS = ['x_prompt', 'x_sample', 'c_prompt', 'c_sample', 'cache_kv_dil1', 'cache_kv_dil4', 'cache_kv_dil16', 'w_ada',
        'b_ada', 'norm_g', 'w_in', 'gm_ln_g', 'gm_ln_b', 'w_s', 'b_s', 'w_out', 'w_q', 'sub_keys', 'expert_u', 'expert_v']
_OUTS = [(1, SEQ, D), (NS, 1, D)] + [(1, 1, min(w, SEQ), 2, HEADS, HD) for w, _ in WINDOWS] \
    + [(1, NS, 1, 2, HEADS, HD)] * 3 + [(1, NS, 1, GM_HEADS, GM // GM_HEADS)]


def kernel(**inputs):
    import concourse.bacc as _bacc
    from concourse.bass_utils import run_bass_kernel_spmd as _run

    nc = _bacc.Bacc("TRN2", target_bir_lowering=False, num_devices=1)
    arrays, args = {}, []
    for name in _INS:
        a = np.ascontiguousarray(inputs[name])
        arrays[f"in_{name}_dram"] = a
        args.append(nc.dram_tensor(f"in_{name}_dram", a.shape, mybir.dt.from_np(a.dtype), kind="ExternalInput").ap())
    outs = [nc.dram_tensor(f"out_{i}_dram", shape, F32, kind="ExternalOutput").ap() for i, shape in enumerate(_OUTS)]
    program(nc, *args, outs)
    r = _run(nc, [arrays], core_ids=[0])
    return tuple(r.results[0][f"out_{i}_dram"] for i in range(len(_OUTS)))
```
